# Optimizing a Trainium2 kernel written in Bass

```python
import jax, jax.numpy as jnp
from jax import lax
import numpy as np
import math

D_MODEL = 1024
BATCH = 1
SEQ = 1024
DEPTH = 1

N_META = 16
GRID_W = 64
HEAD_DIM = 64
N_Q_HEADS = 8
N_KV_HEADS = 2
GQA_GROUP = N_Q_HEADS // N_KV_HEADS
ATTN_WIDTH = N_Q_HEADS * HEAD_DIM
KV_WIDTH = N_KV_HEADS * HEAD_DIM
FOURIER_GROUPS = 8
FOURIER_GROUP_DIM = 64
FOURIER_WIDTH = FOURIER_GROUPS * FOURIER_GROUP_DIM
MIX_WIDTH = FOURIER_WIDTH + ATTN_WIDTH
IN_WIDTH = 2 * FOURIER_WIDTH + ATTN_WIDTH + 2 * KV_WIDTH + ATTN_WIDTH
SPLIT_POINTS = (FOURIER_WIDTH, 2 * FOURIER_WIDTH, 2 * FOURIER_WIDTH + ATTN_WIDTH,
                2 * FOURIER_WIDTH + ATTN_WIDTH + KV_WIDTH,
                2 * FOURIER_WIDTH + ATTN_WIDTH + 2 * KV_WIDTH)
Q_BLOCK = 128
ROPE_THETA = 10000.0
AXIS_ROT_DIM = HEAD_DIM // 2
AXIS_N_FREQ = AXIS_ROT_DIM // 2
EPS = 1e-6


def rmsnorm(x, g):
    xf = x.astype(jnp.float32)
    y = xf * lax.rsqrt(jnp.mean(xf * xf, axis=-1, keepdims=True) + EPS)
    return (y * g.astype(jnp.float32)).astype(x.dtype)

def axial_rope_tables(n_tok):
    rows = n_tok // GRID_W
    j = jnp.arange(n_tok, dtype=jnp.int32)
    row = (j // GRID_W - rows // 2).astype(jnp.float32)
    col = (j % GRID_W - GRID_W // 2).astype(jnp.float32)
    freqs = 1.0 / (ROPE_THETA ** (jnp.arange(AXIS_N_FREQ, dtype=jnp.float32) * 2.0 / AXIS_ROT_DIM))
    ang = jnp.concatenate([row[:, None] * freqs, col[:, None] * freqs], axis=-1)
    ang = jnp.concatenate([jnp.zeros((N_META, HEAD_DIM // 2), jnp.float32), ang], axis=0)
    return jnp.cos(ang), jnp.sin(ang)

def apply_rope(x, cos, sin):
    b, h, l, d = x.shape
    xf = x.astype(jnp.float32).reshape(b, h, l, d // 2, 2)
    x0, x1 = xf[..., 0], xf[..., 1]
    out = jnp.stack([x0 * cos - x1 * sin, x0 * sin + x1 * cos], axis=-1)
    return out.reshape(b, h, l, d).astype(x.dtype)

def gqa_block(q_blk, k, v):
    s = jnp.einsum('bkgqd,bksd->bkgqs', q_blk, k).astype(jnp.float32) * (HEAD_DIM ** -0.5)
    p = jax.nn.softmax(s, axis=-1)
    return jnp.einsum('bkgqs,bksd->bkgqd', p.astype(v.dtype), v)

def fourier_branch(f_in, w_fmix, b_fmix):
    b, l, _ = f_in.shape
    f = f_in.reshape(b, l, FOURIER_GROUPS, FOURIER_GROUP_DIM).astype(jnp.float32)
    fr = jnp.real(jnp.fft.fftn(f, axes=(1, 3), norm='ortho')).astype(f_in.dtype)
    out = jnp.einsum('blgc,gcd->blgd', fr, w_fmix) + b_fmix
    return out.reshape(b, l, FOURIER_WIDTH)

def attention_branch(q, k, v, q_g, k_g, cos, sin, n_tok):
    b, l, _ = q.shape
    q = q.reshape(b, l, N_Q_HEADS, HEAD_DIM).transpose(0, 2, 1, 3)
    k = k.reshape(b, l, N_KV_HEADS, HEAD_DIM).transpose(0, 2, 1, 3)
    v = v.reshape(b, l, N_KV_HEADS, HEAD_DIM).transpose(0, 2, 1, 3)
    q = apply_rope(rmsnorm(q, q_g), cos, sin)
    k = apply_rope(rmsnorm(k, k_g), cos, sin)
    q = q.reshape(b, N_KV_HEADS, GQA_GROUP, l, HEAD_DIM)
    out_meta = gqa_block(q[:, :, :, :N_META], k, v)
    n_blk = n_tok // Q_BLOCK
    q_real = q[:, :, :, N_META:].reshape(b, N_KV_HEADS, GQA_GROUP, n_blk, Q_BLOCK, HEAD_DIM)
    q_real = q_real.transpose(3, 0, 1, 2, 4, 5)
    out_real = lax.map(lambda qb: gqa_block(qb, k, v), q_real)
    out_real = out_real.transpose(1, 2, 3, 0, 4, 5).reshape(b, N_KV_HEADS, GQA_GROUP, n_tok, HEAD_DIM)
    out = jnp.concatenate([out_meta, out_real], axis=3).reshape(b, N_Q_HEADS, l, HEAD_DIM)
    return out.transpose(0, 2, 1, 3).reshape(b, l, ATTN_WIDTH)

def first_inputs(seed: int = 0) -> dict:
    key = jax.random.key(seed)
    ks = jax.random.split(key, 10)
    f32 = jnp.float32
    x = jax.random.normal(ks[0], (BATCH, SEQ, D_MODEL), f32)
    meta_tokens = jax.random.normal(ks[1], (N_META, D_MODEL), f32)
    norm_g = 1.0 + 0.05 * jax.random.normal(ks[2], (DEPTH, D_MODEL), f32)
    w_in = jax.random.normal(ks[3], (DEPTH, D_MODEL, IN_WIDTH), f32) * D_MODEL ** -0.5
    w_fmix = jax.random.normal(ks[4], (DEPTH, FOURIER_GROUPS, FOURIER_GROUP_DIM, FOURIER_GROUP_DIM), f32) * FOURIER_GROUP_DIM ** -0.5
    b_fmix = 0.02 * jax.random.normal(ks[5], (DEPTH, FOURIER_GROUPS, FOURIER_GROUP_DIM), f32)
    q_norm_g = 1.0 + 0.05 * jax.random.normal(ks[6], (DEPTH, HEAD_DIM), f32)
    k_norm_g = 1.0 + 0.05 * jax.random.normal(ks[7], (DEPTH, HEAD_DIM), f32)
    w_out = jax.random.normal(ks[8], (DEPTH, MIX_WIDTH, D_MODEL), f32) * MIX_WIDTH ** -0.5
    final_g = 1.0 + 0.05 * jax.random.normal(ks[9], (D_MODEL,), f32)
    return {"x": x, "meta_tokens": meta_tokens, "norm_g": norm_g, "w_in": w_in,
            "w_fmix": w_fmix, "b_fmix": b_fmix, "q_norm_g": q_norm_g, "k_norm_g": k_norm_g,
            "w_out": w_out, "final_g": final_g}

def first_block(x, meta_tokens, norm_g, w_in, w_fmix, b_fmix, q_norm_g, k_norm_g, w_out, final_g):
    b, n_tok, d = x.shape
    cos, sin = axial_rope_tables(n_tok)
    meta = jnp.broadcast_to(meta_tokens.astype(x.dtype)[None], (b, N_META, d))
    h = jnp.concatenate([meta, x], axis=1)
    for i in range(DEPTH):
        u = rmsnorm(h, norm_g[i])
        proj = jnp.einsum('bld,de->ble', u, w_in[i])
        f_in, f_gate, q, k, v, a_gate = jnp.split(proj, SPLIT_POINTS, axis=-1)
        f_out = fourier_branch(f_in, w_fmix[i], b_fmix[i]) * jax.nn.silu(f_gate)
        a_out = attention_branch(q, k, v, q_norm_g[i], k_norm_g[i], cos, sin, n_tok) * jax.nn.silu(a_gate)
        mixed = jnp.concatenate([f_out, a_out], axis=-1)
        h = h + jnp.einsum('ble,ed->bld', mixed, w_out[i])
    h = rmsnorm(h, final_g)
    return h[:, N_META:]


PLE_DIM = 256
D_MIX = D_MODEL
RET_HEADS = 4
RET_HEAD_DIM = 128
RET_WIDTH = RET_HEADS * RET_HEAD_DIM
RET_CHUNK = 128
MLA_HEADS = 8
MLA_NOPE_DIM = 64
MLA_ROPE_DIM = 32
MLA_QK_DIM = MLA_NOPE_DIM + MLA_ROPE_DIM
MLA_V_DIM = 64
MLA_WIDTH = MLA_HEADS * MLA_V_DIM
MLA_Q_LORA = 384
MLA_KV_LORA = 256
IN_COLS = 4 * RET_WIDTH + MLA_Q_LORA + MLA_KV_LORA + MLA_ROPE_DIM
D_FF = ((8 * D_MODEL // 3 + 255) // 256) * 256
ROPE_BASE = 10000.0


def rmsnorm_2(x, w):
    xf = x.astype(jnp.float32)
    y = xf * lax.rsqrt(jnp.mean(xf * xf, axis=-1, keepdims=True) + EPS)
    return (y * w.astype(jnp.float32)).astype(x.dtype)

def head_groupnorm(x, w):
    xf = x.astype(jnp.float32)
    mu = jnp.mean(xf, axis=-1, keepdims=True)
    var = jnp.mean(jnp.square(xf - mu), axis=-1, keepdims=True)
    y = (xf - mu) * lax.rsqrt(var + EPS)
    B, S, H, d = x.shape
    return (y.reshape(B, S, H * d) * w.astype(jnp.float32)).astype(x.dtype)

def rope(x, positions):
    d = x.shape[-1]
    half = d // 2
    inv = 1.0 / (ROPE_BASE ** (jnp.arange(half, dtype=jnp.float32) / half))
    ang = positions.astype(jnp.float32)[..., None] * inv
    cos = jnp.cos(ang)[:, :, None, :].astype(x.dtype)
    sin = jnp.sin(ang)[:, :, None, :].astype(x.dtype)
    x1, x2 = x[..., :half], x[..., half:]
    return jnp.concatenate([x1 * cos - x2 * sin, x2 * cos + x1 * sin], axis=-1)

def retention_chunkwise(q, k, v):
    B, S, H, d = q.shape
    C = RET_CHUNK
    N = S // C
    dt = q.dtype
    log_g = jnp.log(1.0 - 2.0 ** (-5.0 - jnp.arange(H, dtype=jnp.float32)))
    j = jnp.arange(C, dtype=jnp.float32)
    diff = j[:, None] - j[None, :]
    D = jnp.where(diff[None] >= 0, jnp.exp(jnp.maximum(diff, 0.0)[None] * log_g[:, None, None]), 0.0).astype(dt)
    zeta = jnp.exp((C - 1 - j)[None, :] * log_g[:, None]).astype(dt)
    xi = jnp.exp((j + 1)[None, :] * log_g[:, None]).astype(dt)
    g_chunk = jnp.exp(C * log_g).astype(dt)

    qc = q.reshape(B, N, C, H, d)
    kc = k.reshape(B, N, C, H, d)
    vc = v.reshape(B, N, C, H, d)
    scores = jnp.einsum('bnchd,bnmhd->bnhcm', qc, kc) * D[None, None]
    inner = jnp.einsum('bnhcm,bnmhe->bnche', scores, vc)
    U = jnp.einsum('bnmhd,bnmhe,hm->nbhde', kc, vc, zeta)

    def step(R, u):
        return g_chunk[None, :, None, None] * R + u, R

    _, R_prev = lax.scan(step, jnp.zeros_like(U[0]), U)
    cross = jnp.einsum('bnchd,nbhde->bnche', qc, R_prev) * xi.T[None, None, :, :, None]
    return (inner + cross).reshape(B, S, H, d)

def mla_causal(q, k, v):
    B, S, H, dqk = q.shape
    dv = v.shape[-1]
    NB = S // Q_BLOCK
    scale = 1.0 / math.sqrt(dqk)
    kt = k.transpose(0, 2, 1, 3)
    vt = v.transpose(0, 2, 1, 3)
    qb = q.reshape(B, NB, Q_BLOCK, H, dqk).transpose(1, 0, 3, 2, 4)
    kpos = jnp.arange(S)

    def block(args):
        qi, bi = args
        s = jnp.einsum('bhqd,bhkd->bhqk', qi, kt).astype(jnp.float32) * scale
        qpos = bi * Q_BLOCK + jnp.arange(Q_BLOCK)
        mask = kpos[None, :] <= qpos[:, None]
        s = jnp.where(mask[None, None], s, -1e30)
        pr = jax.nn.softmax(s, axis=-1).astype(vt.dtype)
        return jnp.einsum('bhqk,bhkd->bhqd', pr, vt)

    out = lax.map(block, (qb, jnp.arange(NB)))
    return out.transpose(1, 0, 3, 2, 4).reshape(B, S, H * dv)

def token_mixer(xn, positions, w_in, ret_gn_w, mla_q_norm, w_uq, mla_kv_norm, w_ukv, w_o):
    B, S, _ = xn.shape
    proj = xn @ w_in
    o = 0
    rq = proj[..., o:o + RET_WIDTH]; o += RET_WIDTH
    rk = proj[..., o:o + RET_WIDTH]; o += RET_WIDTH
    rv = proj[..., o:o + RET_WIDTH]; o += RET_WIDTH
    rg = proj[..., o:o + RET_WIDTH]; o += RET_WIDTH
    cq = proj[..., o:o + MLA_Q_LORA]; o += MLA_Q_LORA
    ckv = proj[..., o:o + MLA_KV_LORA]; o += MLA_KV_LORA
    kr = proj[..., o:o + MLA_ROPE_DIM]

    shp = (B, S, RET_HEADS, RET_HEAD_DIM)
    rq = rope(rq.reshape(shp), positions)
    rk = rope(rk.reshape(shp), positions) * (RET_HEAD_DIM ** -0.5)
    ry = retention_chunkwise(rq, rk, rv.reshape(shp))
    ret_out = jax.nn.silu(rg) * head_groupnorm(ry, ret_gn_w)

    qh = (rmsnorm_2(cq, mla_q_norm) @ w_uq).reshape(B, S, MLA_HEADS, MLA_QK_DIM)
    q = jnp.concatenate([qh[..., :MLA_NOPE_DIM], rope(qh[..., MLA_NOPE_DIM:], positions)], axis=-1)
    kvh = (rmsnorm_2(ckv, mla_kv_norm) @ w_ukv).reshape(B, S, MLA_HEADS, MLA_NOPE_DIM + MLA_V_DIM)
    k_rope = rope(kr[:, :, None, :], positions)
    k = jnp.concatenate([kvh[..., :MLA_NOPE_DIM],
                         jnp.broadcast_to(k_rope, (B, S, MLA_HEADS, MLA_ROPE_DIM))], axis=-1)
    v = kvh[..., MLA_NOPE_DIM:]
    mla_out = mla_causal(q, k, v)

    return jnp.concatenate([ret_out, mla_out], axis=-1) @ w_o

def second_inputs(seed: int = 0) -> dict:
    key = jax.random.key(seed)
    ks = jax.random.split(key, 24)
    L = DEPTH

    def nrm(k, shape, fan_in):
        return jax.random.normal(k, shape, jnp.float32) * (fan_in ** -0.5)

    def gain(k, shape):
        return 1.0 + 0.05 * jax.random.normal(k, shape, jnp.float32)

    return {
        "x": jax.random.normal(ks[0], (BATCH, SEQ, D_MODEL), jnp.float32),
        "p": jax.random.normal(ks[1], (DEPTH, BATCH, SEQ, PLE_DIM), jnp.float32),
        "positions": jnp.broadcast_to(jnp.arange(SEQ, dtype=jnp.int32)[None], (BATCH, SEQ)),
        "pre_mix_norm": gain(ks[2], (L, D_MODEL)),
        "w_in": nrm(ks[3], (L, D_MODEL, IN_COLS), D_MODEL),
        "ret_gn_w": gain(ks[4], (L, RET_WIDTH)),
        "mla_q_norm": gain(ks[5], (L, MLA_Q_LORA)),
        "w_uq": nrm(ks[6], (L, MLA_Q_LORA, MLA_HEADS * MLA_QK_DIM), MLA_Q_LORA),
        "mla_kv_norm": gain(ks[7], (L, MLA_KV_LORA)),
        "w_ukv": nrm(ks[8], (L, MLA_KV_LORA, MLA_HEADS * (MLA_NOPE_DIM + MLA_V_DIM)), MLA_KV_LORA),
        "w_o": nrm(ks[9], (L, D_MIX, D_MODEL), D_MIX),
        "post_mix_norm": gain(ks[10], (L, D_MODEL)),
        "pre_ffn_norm": gain(ks[11], (L, D_MODEL)),
        "w_gate": nrm(ks[12], (L, D_MODEL, D_FF), D_MODEL),
        "w_up": nrm(ks[13], (L, D_MODEL, D_FF), D_MODEL),
        "w_down": nrm(ks[14], (L, D_FF, D_MODEL), D_FF),
        "post_ffn_norm": gain(ks[15], (L, D_MODEL)),
        "w_ple_proj": nrm(ks[16], (L, PLE_DIM, D_MODEL), PLE_DIM),
        "ple_norm": gain(ks[17], (L, D_MODEL)),
        "w_ple_gate": nrm(ks[18], (L, D_MODEL, D_MODEL), D_MODEL),
        "b_ple_gate": 0.02 * jax.random.normal(ks[19], (L, D_MODEL), jnp.float32),
    }

def second_block(x, p, positions, pre_mix_norm, w_in, ret_gn_w, mla_q_norm, w_uq, mla_kv_norm,
              w_ukv, w_o, post_mix_norm, pre_ffn_norm, w_gate, w_up, w_down, post_ffn_norm,
              w_ple_proj, ple_norm, w_ple_gate, b_ple_gate):
    h = x
    for i in range(DEPTH):
        xn = rmsnorm_2(h, pre_mix_norm[i])
        mix = token_mixer(xn, positions, w_in[i], ret_gn_w[i], mla_q_norm[i], w_uq[i],
                          mla_kv_norm[i], w_ukv[i], w_o[i])
        h = h + rmsnorm_2(mix, post_mix_norm[i])
        hn = rmsnorm_2(h, pre_ffn_norm[i])
        ff = (jax.nn.silu(hn @ w_gate[i]) * (hn @ w_up[i])) @ w_down[i]
        h = h + rmsnorm_2(ff, post_ffn_norm[i])
        e = rmsnorm_2(p[i] @ w_ple_proj[i], ple_norm[i])
        gate = jax.nn.sigmoid(h @ w_ple_gate[i] + b_ple_gate[i])
        h = h + e * gate
    return h


def setup_inputs(seed=0):
    out = dict(first_inputs(seed))
    for name, value in second_inputs(seed + 1).items():
        if name != "x":
            out[name + "_2"] = value
    return out


def reference(
    x, meta_tokens, norm_g, w_in, w_fmix, b_fmix, q_norm_g, k_norm_g, w_out, final_g, p_2,
    positions_2, pre_mix_norm_2, w_in_2, ret_gn_w_2, mla_q_norm_2, w_uq_2, mla_kv_norm_2,
    w_ukv_2, w_o_2, post_mix_norm_2, pre_ffn_norm_2, w_gate_2, w_up_2, w_down_2,
    post_ffn_norm_2, w_ple_proj_2, ple_norm_2, w_ple_gate_2, b_ple_gate_2,
):
    x = first_block(
        x, meta_tokens, norm_g, w_in, w_fmix, b_fmix, q_norm_g, k_norm_g, w_out, final_g,
    )
    return second_block(
        x, p_2, positions_2, pre_mix_norm_2, w_in_2, ret_gn_w_2, mla_q_norm_2, w_uq_2,
        mla_kv_norm_2, w_ukv_2, w_o_2, post_mix_norm_2, pre_ffn_norm_2, w_gate_2, w_up_2,
        w_down_2, post_ffn_norm_2, w_ple_proj_2, ple_norm_2, w_ple_gate_2, b_ple_gate_2,
    )


_drawn_inputs = setup_inputs


def setup_inputs(seed=0):
    import zlib

    import numpy as np

    out = dict(_drawn_inputs(seed))
    spreads = {}
    factors = {'b_fmix': 3.725,
     'q_norm_g': 8.0,
     'k_norm_g': 8.0,
     'mla_q_norm_2': 7.703,
     'mla_kv_norm_2': 5.123,
     'ple_norm_2': 3.581,
     'b_ple_gate_2': 8.0,
     'ret_gn_w_2': 8.0}
    for name, (base, spread) in spreads.items():
        noise = np.random.default_rng([zlib.crc32(name.encode()), seed]).standard_normal(out[name].shape)
        drawn = base * np.exp(spread * noise) if base else spread * noise
        out[name] = __import__('jax').numpy.asarray(drawn.astype(out[name].dtype))
    for name, factor in factors.items():
        out[name] = (out[name] * factor).astype(out[name].dtype)
    return out
```

```python
from contextlib import ExitStack

import numpy as np
import concourse.bass as bass
from concourse import mybir

F32 = mybir.dt.float32
F32R = mybir.dt.float32r
BF16 = mybir.dt.bfloat16
I32 = mybir.dt.int32
ALU = mybir.AluOpType
ACT = mybir.ActivationFunctionType
AX = mybir.AxisListType

P = 128
T = 1024
META = 16
L = T + META
D = 1024
KT = D // P
EPS = 1e-6
HD = 64
NH1 = 8
FW = 512
NL = L // 2
NM = NL + 1
MT5 = (NM + P - 1) // P
DFF = 2816
CH = 128
NCH = T // CH
RH = 4
MH_ = 8
MQK = 96
HALF = 512

S_IN1 = 0
S_OUT1 = 18
S_RET = S_OUT1 + 8
S_LORA = S_RET + 4 * RH
S_MLA = S_LORA + 6
S_OUT2 = S_MLA + MH_
S_FFN = S_OUT2 + 8
S_PLEP = S_FFN + 6 * (DFF // 256)
S_PLEG = S_PLEP + 2
NSLAB = S_PLEG + 8

_names = [("norm_g", 8), ("final_g", 8), ("pre_mix", 8), ("post_mix", 8), ("pre_ffn", 8), ("post_ffn", 8),
          ("ple_norm", 8), ("b_ple", 8), ("mla_q", 3), ("mla_kv", 2), ("ret_gn", 4), ("b_fmix", 4), ("q_g", 1),
          ("k_g", 1), ("zeta", 4), ("inv_ret", 1), ("inv_mla", 1), ("sgn_ret", 1), ("sgn_mla", 1), ("eps", 1),
          ("halfpi", 1), ("gch", 4)]
COL = {}
NCOL = 0
for _n, _k in _names:
    COL[_n] = NCOL
    NCOL += _k
SQ = {n: i for i, n in enumerate(["ident", "ones", "headones", "mean", "causal", "xi0", "xi1", "xi2", "xi3",
                                  "dec0", "dec1", "dec2", "dec3"])}


class Tok:

    def __init__(self, q, off, loop, back=0):
        self.q, self.off, self.loop, self.back = q, off, loop, back

    @property
    def prev(self):
        return Tok(self.q, self.off, self.loop, 1)

    def sem(self):
        return self.q.sem

    def value(self, loop):
        if self.loop is None:
            return self.off, 0
        n = self.loop.incs[self.q]
        if self.loop is loop:
            low = self.off - self.back * n
            assert low > 0, ("wait below one", self.q.name, self.off, n)
            return low, n
        return self.off + (self.loop.n - 1) * n, 0


class Later(Tok):

    def __init__(self):
        self.tok = None

    def sem(self):
        return self.tok.sem()

    def value(self, loop):
        return self.tok.prev.value(loop)


class At:

    def __init__(self, sem, const, step=0):
        self._sem, self.const, self.step = sem, const, step

    def sem(self):
        return self._sem

    def value(self, loop):
        return self.const, (self.step if loop is not None else 0)


class Queue:
    def __init__(self, name, sem):
        self.name, self.sem, self.count, self.ops = name, sem, 0, []


class Loop:
    def __init__(self, n):
        self.n, self.incs, self.bodies = n, {}, {}


class Program:

    def __init__(self, queues):
        self.q = queues
        self.loop = None

    def do(self, name, fn, *waits, inc=(), mark=True, counter=None):
        q = self.q[name]
        c = self.q[counter or name]
        q.ops.append((fn, waits, tuple(inc), c.sem if mark else None))
        if mark:
            c.count += 1
        return Tok(c, c.count, self.loop)

    def last(self, name):
        q = self.q[name]
        return Tok(q, q.count, self.loop)

    def begin(self, n):
        self.loop = Loop(n)
        self.saved = {k: (q.ops, q.count) for k, q in self.q.items()}
        for q in self.q.values():
            q.ops = []

    def end(self):
        for k, q in self.q.items():
            ops, count = self.saved[k]
            self.loop.incs[q] = q.count - count
            if q.ops:
                ops.append((self.loop, q.ops))
            q.count = count + self.loop.n * (q.count - count)
            q.ops = ops
        self.loop = None

    def emit(self, name, eng):
        q = self.q[name]

        def run(ops, loop, i):
            for op in ops:
                if isinstance(op[0], Loop):
                    with eng.Fori(0, op[0].n) as k:
                        run(op[1], op[0], k)
                    continue
                fn, waits, inc, mark = op
                most = {}
                for w in waits:
                    if w is not None:
                        low, step = w.value(loop)
                        s = most.setdefault((id(w.sem()), step), [w.sem(), low])
                        s[1] = max(s[1], low)
                for (_, step), (s, low) in most.items():
                    eng.wait_ge(s, i * step + low if step else low)
                ins = fn(eng, i)
                if mark is not None:
                    ins.then_inc(mark, 1)
                for s, k in inc:
                    ins.then_inc(s, k)
        run(q.ops, None, 0)


class Slot:

    def __init__(self, tok=None):
        self.free = tok
        self.outer = self.later = None

    def waits(self):
        if self.free is not None or self.later is None:
            return [self.free]
        return [self.outer, self.later]

    def enter(self):
        self.outer, self.later, self.free = self.free, Later(), None

    def leave(self):
        if self.free is None:
            self.free = self.outer
        else:
            self.later.tok = self.free
        self.outer = self.later = None


def two_block_kernel(nc, xT, pT, pos, slabs, cols, squares, rope1, dft, wf, cd, outT):
    with ExitStack() as ctx:
        base = 16512
        top = 207 * 1024

        def at(name, shape, dt, kb):
            size = int(np.prod(shape[1:])) * (2 if dt == BF16 else 4)
            assert int(kb * 1024) + size <= top, (name, kb, size)
            return nc.alloc_sbuf_tensor_at(name, shape, dt, offset=base + int(kb * 1024))

        def sem(name):
            return ctx.enter_context(nc.semaphore(name))

        ctx.enter_context(nc.sbuf_tensor("arena", [P, top // 4], F32))

        RAW = at("wraw", [P, 2, 1024], F32, 0)
        WH = [at(f"wh{j}", [P, 1024], F32R, 8 + 4 * j) for j in range(2)]
        WL = [at(f"wl{j}", [P, 1024], F32R, 16 + 4 * j) for j in range(2)]
        COLS = at("cols", [P, NCOL], F32, 24)
        SQC = at("sqc", [P, 4, P], F32, 24.5)
        TINY = at("tiny", [P, 64], F32, 26.5)
        ONE = at("one", [P, 1], F32, 26.75)
        XH = at("xh", [P, KT, L], F32R, 27)
        XL = at("xl", [P, KT, L], F32R, 59.5)
        X = at("x", [P, KT, L], F32, 92)
        FT = at("ft", [P, 4, 1042], F32, 92)
        K1 = at("k1", [P, L], F32, 112.75)
        V1 = at("v1", [P, L], F32, 117)
        Q1 = at("q1", [P, 4, T], F32, 121.25)
        TMP = [at(f"tmp{j}", [P, L], F32, 137.5 + 4.125 * j) for j in range(5)]
        COS1 = at("cos1", [P, L], F32, 158.25)
        SIN1 = at("sin1", [P, L], F32, 162.5)
        GT = at("gt", [P, KT, T], F32, 166.75)
        RS = at("rs", [P, L], F32, 199)
        CT = at("ct", [P, MT5, NL], F32, 27)
        ST = at("st", [P, MT5, NL], F32, 37.5)
        FE = at("fe", [P, 4, NM + 1], F32, 137.5)
        FO = at("fo", [P, 4, NM + 1], F32, 146)
        WF = at("wf", [64, 512], F32, 154.5)
        CD = at("cd", [64, 2, P], F32, 156.5)
        WBD = at("wbd", [P, 2, 4, P], F32, 158)
        GA = at("ga", [P, MT5, 512], F32, 92)
        GB = at("gb", [P, MT5, 512], F32, 102)
        QSB = at("qsb", [P, NL], F32, 203.5)
        PSB = at("psb", [P, NL], F32, 162.5)
        PTH = [at(f"pth{j}", [P, 8, HALF], F32R, 27 + 32 * j) for j in range(2)]
        PTL = [at(f"ptl{j}", [P, 8, HALF], F32R, 43 + 32 * j) for j in range(2)]
        PM = [at(f"pm{j}", [P, 4, META], F32, 91 + 0.25 * j) for j in range(2)]
        KHH = [at(f"khh{j}", [P, L], F32R, 92 + 8.25 * j) for j in range(2)]
        KLL = [at(f"kll{j}", [P, L], F32R, 96.125 + 8.25 * j) for j in range(2)]
        PMH = at("pmh", [META, HALF], F32R, 108.5)
        PML = at("pml", [META, HALF], F32R, 110.5)
        VS1 = [at(f"vs1{j}", [P, 9, P], F32R, 137.5 + 4.625 * j) for j in range(2)]
        QST = [at(f"qst{j}", [P, T], F32R, 146.75 + 4 * j) for j in range(2)]
        PB = [at(f"pb{j}", [P, T], F32, 154.75 + 4 * j) for j in range(2)]
        OT = [at(f"ot{j}", [P, HALF], F32, 162.75 + 2 * j) for j in range(2)]
        MH = at("mh", [P, KT, T], F32R, 27)
        ML = at("ml", [P, KT, T], F32R, 59)
        H = at("h", [P, KT, T], F32, 92)
        COS2 = at("cos2", [P, T], F32, 124)
        SIN2 = at("sin2", [P, T], F32, 128)
        COS3 = at("cos3", [P, T], F32, 132)
        SIN3 = at("sin3", [P, T], F32, 136)
        PI = at("pi", [P, T], I32, 140)
        ANG = at("ang", [P, T], F32, 144)
        KR_ = at("kround", [P, T], F32, 148)
        RED = at("red", [P, T], F32, 152)
        N1 = [at(f"n1{j}", [P, T], F32, 199 + 4 * j) for j in range(2)]
        ACC1 = at("acc1", [P, T], F32, 156)
        RS1 = at("rs1", [P, T], F32, 160)
        MX = at("mx", [P, KT, T], F32, 140)
        GR = at("gr", [P, 4, T], F32, 156)
        RRAW = at("rraw", [P, T], F32, 172)
        RT1 = at("rt1", [P, T], F32, 176)
        RK = at("rk", [P, T], F32, 180)
        RQ = at("rq", [P, T], F32, 184)
        RV = at("rv", [P, T], F32, 188)
        RKN = at("rkn", [P, NCH, CH], F32, 192)
        RVN = at("rvn", [P, NCH, CH], F32, 196)
        RX = at("rx", [P, 8, P], F32, 200)
        CQR = at("cqr", [P, 5, T], F32, 172)
        KRR = at("krr", [P, T], F32, 192)
        LT = [at(f"lt{j}", [P, T], F32, 196 + 4 * j) for j in range(2)]
        CNH = at("cnh", [P, 5, T], F32R, 27)
        CNL = at("cnl", [P, 5, T], F32R, 47)
        QKS = [[at(f"qks{j}{n}", [P, T], F32R, (67 if j == 0 else 92) + 4 * n) for n in range(4)] for j in range(2)]
        VS2 = [at(f"vs2{j}", [P, 8, P], F32R, 83 + 4 * j) for j in range(2)]
        LTH = at("lth", [P, 8, HALF], F32R, 108)
        LTL = at("ltl", [P, 8, HALF], F32R, 172)
        LP = [at(f"lp{j}", [P, T], F32, 124 + 4 * j) for j in range(2)]
        MQ = at("mq", [P, T], F32, 188)
        MKV = at("mkv", [P, T], F32, 192)
        MT1 = at("mt1", [P, T], F32, 196)
        MOT = at("mot", [P, HALF], F32, 200)
        CMB = at("cmb", [P, 2, P], BF16, 202)
        CMF = at("cmf", [P, 1, P], F32, 203)
        O2 = at("o2", [P, KT, T], F32, 172)
        N2 = [at(f"n2{j}", [P, T], F32, 124 + 4 * j) for j in range(2)]
        ACC2 = at("acc2", [P, T], F32, 132)
        RS2 = at("rs2", [P, T], F32, 136)
        HBH = [at(f"hbh{j}", [P, 2, T], F32R, 124 + 16 * j) for j in range(2)]
        HBL = [at(f"hbl{j}", [P, 2, T], F32R, 132 + 16 * j) for j in range(2)]
        FA = at("fa", [P, KT, T], F32, 156)
        TH = [at(f"th{j}", [P, T], F32, 188 + 4 * j) for j in range(2)]
        HF = [at(f"hf{j}", [P, T], F32, 196 + 4 * j) for j in range(2)]
        PR = at("pr", [P, 2, T], F32, 124)
        PH = at("ph", [P, 2, T], F32R, 132)
        PL = at("pl", [P, 2, T], F32R, 140)
        EB = at("eb", [P, KT, T], F32, 27)
        OB = at("ob", [P, KT, T], F32, 59)
        RS3 = at("rs3", [P, T], F32, 59)
        RS4 = at("rs4", [P, T], F32, 63)
        GH = at("gh", [P, KT, T], F32R, 124)
        GL = at("gl", [P, KT, T], F32R, 156)

        PS = [ctx.enter_context(nc.psum_tensor(f"ps{n}", [P, 2, HALF], F32)) for n in "abcd"]
        A, B, C, Dp = range(4)

        s_q = {n: sem(f"s_{n}") for n in ("sp", "act", "pool", "pe", "dve")}
        s_raw = [sem(f"s_raw{j}") for j in range(2)]
        s_split = sem("s_split")
        s_used = sem("s_used")
        s_out = sem("s_out")
        s_q["used"] = s_used
        pr = Program({n: Queue(n, s_q[n]) for n in s_q})
        do = pr.do

        def act(fn, *w, **k):
            return do("act", fn, *w, **k)

        def dve(fn, *w, **k):
            return do("dve", fn, *w, **k)

        def pe(fn, *w, **k):
            return do("pe", fn, *w, **k)

        def own(*operands):
            return [pr.last("dve")] if any(callable(x) for x in operands) else []

        def copy_(o, i, *w, scale=1.0):
            return act(lambda e, k: e.activation(r(o, k), r(i, k), ACT.Copy, scale=scale), *w)

        def fun(f, o, i, *w, scale=1.0, bias=0.0, acc=None):
            if acc is None:
                return act(lambda e, k: e.activation(r(o, k), r(i, k), f, scale=scale, bias=bias), *w)
            return act(lambda e, k: e.activation(r(o, k), r(i, k), f, scale=scale, bias=bias, accum_out=acc), *w)

        def tt(o, a, b, op, *w, q="dve"):
            return do(q, lambda e, k: e.tensor_tensor(r(o, k), r(a, k), r(b, k), op), *w,
                      *(own(o, a, b) if q == "dve" else []))

        def ts(o, a, s1, op0, *w, s2=None, op1=None, q="dve"):
            if op1 is None:
                return do(q, lambda e, k: e.tensor_scalar(r(o, k), r(a, k), s1, None, op0), *w, *own(o, a))
            return do(q, lambda e, k: e.tensor_scalar(r(o, k), r(a, k), s1, s2, op0, op1), *w)

        def stt(o, a, s, b, op0, op1, *w):
            return dve(lambda e, k: e.scalar_tensor_tensor(out=r(o, k), in0=r(a, k), scalar=s, in1=r(b, k),
                                                           op0=op0, op1=op1), *w, *own(o, a, b))

        def vcopy(o, i, *w):
            return ts(o, i, 1.0, MUL, *w)

        def dcopy(o, i, *w):
            return dve(lambda e, k: e.tensor_copy(r(o, k), r(i, k)), *w)

        def recip(o, i, *w):
            return dve(lambda e, k: e.reciprocal(r(o, k), r(i, k)), *w)

        def mm(o, l, rh, st, sp, *w, **kw):
            return pe(lambda e, k: e.matmul(r(o, k), lhsT=r(l, k), rhs=r(rh, k), start=st, stop=sp,
                                            skip_group_check=True), *w, **kw)

        def tr(o, i, ident, *w, **kw):
            return pe(lambda e, k: e.transpose(r(o, k), r(i, k), ident), *w, **kw)

        def r(x, k):
            return x(k) if callable(x) else x

        loads = [0]

        def load(q, dst, src, *w):
            loads[0] += 1
            s = sem(f"s_load{loads[0]}")
            do(q, lambda e, k: e.dma_start(dst, src), *w, inc=[(s, 16)], mark=False)
            return At(s, 16)

        def col(name, j=0, lo=0, hi=P):
            return COLS[lo:hi, COL[name] + j:COL[name] + j + 1]

        MUL, ADD, SUB, MAX = ALU.mult, ALU.add, ALU.subtract, ALU.max

        def slab_in(s, step, *w):
            j = s % 2
            free = [] if s < 2 else [At(s_split, s - 1, step)]
            do("sp", lambda e, k: e.dma_start(RAW[:, j, :], slabs[s + (k * step if step else 0)]),
               *free, *w, inc=[(s_raw[j], 16)], mark=False)

        def slab_split(s, step):
            j = s % 2
            free = [] if s < 2 else [At(s_used, s - 1, step)]
            if s == 0:
                do("pool", lambda e, k: e.memset(ONE[:, :], 1.0))
            h = do("pool", lambda e, k: e.tensor_tensor(WH[j][:, :], RAW[:, j, :], ONE[:, 0:1].to_broadcast([P, 1024]), MUL),
                   At(s_raw[j], 16 * (s // 2 + 1), 16 * step // 2), *free, At(s_q["pool"], 1))
            do("pool", lambda e, k: e.tensor_tensor(WL[j][:, :], RAW[:, j, :], WH[j][:, :], SUB), h,
               inc=[(s_split, 1)], mark=False)

        def feed(fn, a, b):
            if b > a:
                pr.begin((b - a) // 2)
                fn(a, 2)
                fn(a + 1, 2)
                pr.end()

        done_split = [0]

        def split_to(b):
            if done_split[0] == 0:
                slab_split(0, 0)
                slab_split(1, 0)
                done_split[0] = 2
            feed(slab_split, done_split[0], b)
            done_split[0] = b

        def project(s, step, blocks, xh, xl, outs, *w, xw=None, m=P, last=True, start=True, stop=True):
            j = s % 2
            n = 0
            total = 3 * len(blocks)
            tok = None
            for bi, (blk, kt) in enumerate(blocks):
                wh, wl = WH[j][:, blk * P:blk * P + m], WL[j][:, blk * P:blk * P + m]
                for pas, (lw, xx) in enumerate(((wh, xh), (wh, xl), (wl, xh))):
                    for oi, (o, c0, cn) in enumerate(outs):
                        ws = []
                        if n == 0 and oi == 0:
                            ws += [At(s_split, s + 1, step), *w]
                        if pas < 2 and oi == 0 and xw is not None:
                            ws.append(xw[pas][kt])
                        end = n == total - 1 and oi == len(outs) - 1
                        tok = mm(o, lw, xx(kt, c0, cn), start and n == 0, stop and n == total - 1, *ws,
                                 mark=end, counter="used" if last else None)
                    n += 1
            return tok

        def halves(p):
            return [(PS[p][:, 0, :], 0, HALF), (PS[p][:, 1, :], HALF, HALF)]

        def both(p):
            return PS[p][:, :, :].rearrange("p a b -> p (a b)")

        ps = [Slot() for _ in range(4)]

        def loop(n, slots, body):
            pr.begin(n)
            for x in slots:
                x.enter()
            body()
            for x in slots:
                x.leave()
            pr.end()

        def sums(tile, pair, w, meta=None, square=None):
            sq = SQC[:, 1, :] if square is None else square
            o = halves(pair)
            t = mm(o[0][0], sq, tile[:, 0:HALF], True, True, w, *ps[pair].waits(), mark=False)
            t = mm(o[1][0], sq, tile[:, HALF:T], True, True)
            if meta is not None:
                t = mm(PS[meta][:, 0, 0:META], sq, tile[:, T:L], True, True, *ps[meta].waits())
            return t

        def rstd(rs, pair, n, *w, meta=None):
            a = fun(ACT.Sqrt, rs[:, 0:T], both(pair), *w, scale=1.0 / n, bias=col("eps"))
            if meta is not None:
                a = fun(ACT.Sqrt, rs[:, T:L], PS[meta][:, 0, 0:META], *w, scale=1.0 / n, bias=col("eps"))
                ps[meta].free = a
            ps[pair].free = a
            return recip(rs[:, 0:L if meta is not None else T], rs[:, 0:L if meta is not None else T], a)

        def split_tile(hi, lo, src, tmp, w):
            h = copy_(hi, src, w)
            return h, tt(lo, src, hi, SUB, h)

        w_cols = load("sp", COLS[:, :], cols)
        w_x = [load("sp", X[:, kt, :], xT[kt]) for kt in range(KT)]
        w_sq = load("act", SQC[:, :, :], squares[0:4].rearrange("n p c -> p n c"))
        w_cs = load("act", COS1[:, :], rope1[0])
        w_sn = load("act", SIN1[:, :], rope1[1])
        slab_in(0, 0)
        slab_in(1, 0)
        feed(slab_in, 2, NSLAB)
        split_to(S_OUT1)

        def squares_to_psum(tiles, waits, tmp, pair, meta, width):
            n = len(tiles)
            free = [None, None]
            for j in range(n):
                a = fun(ACT.Square, tmp[j % 2][:, 0:width], tiles[j], waits[j], free[j % 2])
                o = halves(pair)
                first, last = j == 0, j == n - 1
                mm(o[0][0], SQC[:, 1, :], tmp[j % 2][:, 0:HALF], first, last, a,
                   *(ps[pair].waits() + [w_sq] if first else []), mark=False)
                t = mm(o[1][0], SQC[:, 1, :], tmp[j % 2][:, HALF:T], first, last)
                if meta is not None:
                    t = mm(PS[meta][:, 0, 0:META], SQC[:, 1, :], tmp[j % 2][:, T:L], first, last,
                           *(ps[meta].waits() if first else []))
                free[j % 2] = t
            return t

        t = squares_to_psum([X[:, kt, :] for kt in range(KT)], w_x, TMP, C, Dp, L)
        t_rs = rstd(RS, C, D, t, w_cols, meta=Dp)
        xw = ([None] * KT, [None] * KT)
        free = [None, None]
        for kt in range(KT):
            n_ = stt(TMP[2 + kt % 2][:, :], X[:, kt, :], col("norm_g", kt), RS[:, :], MUL, MUL, t_rs, w_cols,
                     free[kt % 2])
            xw[0][kt] = copy_(XH[:, kt, :], TMP[2 + kt % 2][:, :], n_)
            free[kt % 2] = xw[1][kt] = tt(XL[:, kt, :], TMP[2 + kt % 2][:, :], XH[:, kt, :], SUB, xw[0][kt])

        def xh(kt, c, n):
            return XH[:, kt, c:c + n]

        def xl(kt, c, n):
            return XL[:, kt, c:c + n]

        full = [(kt, kt) for kt in range(KT)]

        pair_meta = [(A, C), (B, Dp)]
        ft_zero = dve(lambda e, k: e.memset(FT[:, :, L:L + 2], 0.0), xw[1][KT - 1])

        def f_in():
            for j in range(2):
                p, m = pair_meta[j]
                t = project(S_IN1 + j, 2, full, xh, xl, halves(p) + [(PS[m][:, 0, 0:META], T, META)],
                            *ps[p].waits(), *ps[m].waits(), xw=xw)
                a = vcopy(lambda k, j=j: FT[:, k * 2 + j, META:L], both(p), t)
                a = vcopy(lambda k, j=j: FT[:, k * 2 + j, 0:META], PS[m][:, 0, 0:META], t)
                ps[p].free = ps[m].free = a

        loop(2, ps, f_in)
        ft_done = ps[B].free

        raw, sqt, t1, rsk, t2 = TMP
        S_raw, S_sq, S_t1, S_rs, S_t2 = (Slot() for _ in range(5))
        kq_slots = [S_raw, S_sq, S_t1, S_rs, S_t2]
        for x in kq_slots:
            x.free = xw[1][KT - 1]

        def turn(t, p, pm, meta, g, width):
            a = copy_(raw[:, 0:T], both(p), t, *S_raw.waits())
            ps[p].free = a
            if meta:
                a = copy_(raw[:, T:L], pm, t)
            b = fun(ACT.Square, sqt[:, 0:width], raw[:, 0:width], a, *S_sq.waits())
            stt(t1[:, 0:width], raw[:, 0:width], col(g), COS1[:, 0:width], MUL, MUL, a, w_cs, w_sn, *S_t1.waits())
            for q4 in range(4):
                lo, src = 32 * q4, 32 * (q4 ^ 1)
                v = stt(t2[lo:lo + 32, 0:width], raw[src:src + 32, 0:width], col(g, 0, src, src + 32),
                        SIN1[src:src + 32, 0:width], MUL, MUL, *(S_t2.waits() if q4 == 0 else []))
            S_raw.free = v
            v = tt(t1[:, 0:width], t1[:, 0:width], t2[:, 0:width], ADD, v)
            S_t2.free = v
            return a, b, v

        def norm_heads(b, v, pair, meta, out, width):
            s = sums(sqt, pair, b, meta=meta, square=SQC[:, 2, :])
            S_sq.free = s
            x = rstd(rsk, pair, HD, s, *S_rs.waits(), meta=meta)
            x = tt(out, t1[:, 0:width], rsk[:, 0:width], MUL, x, v)
            S_rs.free = S_t1.free = x
            return x

        t = project(S_IN1 + 4, 0, full, xh, xl, halves(A) + [(PS[C][:, 0, 0:META], T, META)],
                    *ps[A].waits(), *ps[C].waits(), xw=xw)
        a, b_, v_ = turn(t, A, PS[C][:, 0, 0:META], True, "k_g", L)
        ps[C].free = a
        t = project(S_IN1 + 5, 0, full, xh, xl, halves(B) + [(PS[Dp][:, 1, 0:META], T, META)],
                    *ps[B].waits(), *ps[Dp].waits())
        t_v = copy_(V1[:, 0:T], both(B), t)
        t_v = copy_(V1[:, T:L], PS[Dp][:, 1, 0:META], t)
        ps[B].free = ps[Dp].free = t_v
        t_k = norm_heads(b_, v_, C, Dp, K1[:, :], L)

        def q_tiles():
            t = project(S_IN1 + 6, 2, full, xh, xl, halves(A), *ps[A].waits())
            _, b0, v0 = turn(t, A, None, False, "q_g", T)
            t = project(S_IN1 + 7, 2, full, xh, xl, halves(B), *ps[B].waits())
            norm_heads(b0, v0, C, None, lambda k: Q1[:, k * 2, :], T)
            _, b1, v1 = turn(t, B, None, False, "q_g", T)
            norm_heads(b1, v1, Dp, None, lambda k: Q1[:, k * 2 + 1, :], T)

        loop(2, ps + kq_slots, q_tiles)
        t_q = S_t1.free

        S_th = [Slot(t_q), Slot(t_q)]

        def gates():
            for j in range(2):
                p = (A, B)[j]
                t = project(S_IN1 + 10 + j, 2, full, xh, xl, halves(p), *ps[p].waits())
                a = fun(ACT.Tanh, TMP[j][:, 0:T], both(p), t, *S_th[j].waits(), scale=0.5)
                g = stt(lambda k, j=j: GT[:, k * 2 + j, :], TMP[j][:, 0:T], 1.0, both(p), ADD, MUL, a)
                S_th[j].free = ps[p].free = g

        loop(4, ps + S_th, gates)
        t_gates = ps[B].free
        split_to(S_OUT1 + 2)

        w_ct = load("act", CT[:, :, :], dft[0].rearrange("(m p) n -> p m n", p=P), t_gates)
        w_st = load("act", ST[:, :, :], dft[1].rearrange("(m p) n -> p m n", p=P))
        w_wf = load("act", WF[:, :], wf)
        w_cd = load("act", CD[:, :, :], cd.rearrange("a p c -> p a c"))
        f1 = tt(FE[:, :, 0:NM], FT[:, :, 0:NM], FT[:, :, L:L - NM:-1], ADD, t_gates, ft_done, ft_zero)
        f2 = tt(FO[:, :, 0:NM], FT[:, :, 0:NM], FT[:, :, L:L - NM:-1], SUB)
        z = dve(lambda e, k: e.memset(WBD[:, :, :, :], 0.0), f1)
        for a in range(2):
            t = mm(PS[A][:, a, :], CD[:, a, :], WF[:, :], True, True, *ps[A].waits(), w_wf, w_cd)
        for a in range(2):
            for h in range(2):
                rows = slice(64 * h, 64 * h + 64)
                c = dcopy(WBD[rows, a, :, 64 * h:64 * h + 64],
                          PS[A][rows, a, :].rearrange("p (j two c) -> p j two c", two=2, c=64)[:, :, h, :], t, z)
        ps[A].free = c
        w_g = c
        for mt in range(MT5):
            w = min(P, NM - mt * P)
            p = (A, B, C, Dp)[mt % 4]
            for a, F_ in enumerate((FE, FO)):
                for ct in range(4):
                    t = mm(PS[p][0:w, a, ct * P:ct * P + P], F_[:, ct, mt * P:mt * P + w], WBD[:, a, ct, :],
                           True, True, w_g, f2, *ps[p].waits(), mark=(a == 1 and ct == 3))
            ga = copy_(GA[0:w, mt, :], PS[p][0:w, 0, :], t)
            gb = copy_(GB[0:w, mt, :], PS[p][0:w, 1, :], t)
            ps[p].free = gb
        S_q, S_p = Slot(), Slot()
        n = 0
        for dt in range(4):
            for h in range(2):
                p = (A, B, C, Dp)[(MT5 + n) % 4]
                n += 1
                c0, cn = h * (NL // 2), NL // 2
                for a, (G_, TB) in enumerate(((GA, CT), (GB, ST))):
                    for mt in range(MT5):
                        w = min(P, NM - mt * P)
                        t = mm(PS[p][:, a, 0:cn], G_[0:w, mt, dt * P:dt * P + P], TB[0:w, mt, c0:c0 + cn],
                               mt == 0, mt == MT5 - 1, gb, w_ct, w_st, *ps[p].waits(),
                               mark=(a == 1 and mt == MT5 - 1))
                q_ = copy_(QSB[:, 0:cn], PS[p][:, 1, 0:cn], t, *S_q.waits())
                k0 = META - 1 if h == 0 else 0
                k1 = cn if h == 0 else cn - 1
                x = stt(PSB[:, 0:cn], PS[p][:, 0, 0:cn], col("b_fmix", dt), QSB[:, 0:cn], ADD, SUB, q_, S_p.free)
                r0 = c0 + 1 + k0 - META
                seg = GT[:, dt, r0:r0 + cn - k0]
                x = stt(seg, PSB[:, k0:cn], 0.5, seg, MUL, MUL, x)
                y = stt(PSB[:, cn:2 * cn], PS[p][:, 0, 0:cn], col("b_fmix", dt), QSB[:, 0:cn], ADD, ADD)
                S_q.free = ps[p].free = y
                hi_, lo_ = T - (c0 + 1), T - (c0 + k1)
                seg = GT[:, dt, lo_:hi_ + 1]
                S_p.free = stt(seg, PSB[:, cn + k1 - 1:cn - 1:-1] if cn > 0 else None, 0.5, seg, MUL, MUL, y)
        t_four = S_p.free

        for kv in range(2):
            mine, rest = slice(64 * kv, 64 * kv + 64), slice(64 - 64 * kv, 128 - 64 * kv)
            a = copy_(KHH[kv][mine, :], K1[mine, :], t_four, t_k)
            t_kh = copy_(KHH[kv][rest, :], K1[mine, :])
            tt(KLL[kv][mine, :], K1[mine, :], KHH[kv][mine, :], SUB, a)
            t_kl = tt(KLL[kv][rest, :], K1[mine, :], KHH[kv][mine, :], SUB)
        for kt in range(8):
            t = tr(PS[C][:, kt // 4, (kt % 4) * P:(kt % 4) * P + P], V1[:, kt * P:kt * P + P], SQC[:, 0, :],
                   *ps[C].waits(), t_v, mark=kt == 7)
        t = tr(PS[Dp][0:META, 0, 0:P], V1[:, T:L], SQC[:, 0, :], *ps[Dp].waits())
        src = [PS[C][:, :, :].rearrange("p a (k c) -> p (a k) c", c=P)[:, :, 64 * kv:64 * kv + 64] for kv in range(2)]
        srm = [PS[Dp][0:META, 0, 64 * kv:64 * kv + 64] for kv in range(2)]
        for kv in range(2):
            copy_(VS1[kv][:, 0:8, 0:64], src[kv], t, t_four)
            a = copy_(VS1[kv][0:META, 8, 0:64], srm[kv])
        for kv in range(2):
            t_vs = tt(VS1[kv][:, 0:8, 64:128], src[kv], VS1[kv][:, 0:8, 0:64], SUB, a)
            t_vs = tt(VS1[kv][0:META, 8, 64:128], srm[kv], VS1[kv][0:META, 8, 0:64], SUB)
        ps[C].free = ps[Dp].free = t_vs

        MXM, NB, RSA, RSB, RI = (TINY[:, 4 * n:4 * n + 4] for n in range(1, 6))
        MXT = TINY[:, 24:32]
        S_qs = [Slot(), Slot()]
        S_pb = [Slot(), Slot()]
        S_pm = [Slot(), Slot()]
        S_pt = [Slot(), Slot()]
        S_pmh, S_sm, S_av, S_tc = Slot(), Slot(t_vs), Slot(t_vs), [Slot(t_vs), Slot(t_vs)]
        S_ot = [Slot(), Slot()]
        S_sc = [ps[A], ps[B]]
        at_slots = S_qs + S_pb + S_pm + S_pt + [S_pmh, S_sm, S_av] + S_tc + S_ot + S_sc
        scale1 = HD ** -0.5
        st = {}

        def heads_of_tile(kv):
            def stage(s):
                mine, rest = slice(64 * s, 64 * s + 64), slice(64 - 64 * s, 128 - 64 * s)
                a = vcopy(QST[s][mine, :], lambda k: Q1[mine, k + 2 * kv, :], *S_qs[s].waits())
                st["q", s] = tt(QST[s][rest, :], lambda k: Q1[mine, k + 2 * kv, :], QST[s][mine, :], SUB, a)

            def scores(u):
                s, qt = divmod(u, 8)
                p = S_sc[u % 2]
                b = PS[u % 2]
                q = QST[s][:, qt * P:qt * P + P]
                for h in range(2):
                    c = slice(h * HALF, h * HALF + HALF)
                    mm(b[:, h, :], q, KHH[kv][:, c], True, False, st["q", s], *p.waits(), t_kl, t_kh, mark=False)
                    t = mm(b[:, h, :], q, KLL[kv][:, c], False, True, mark=h == 1)
                st["s", u] = t
                if u % 4 == 0:
                    for v in range(4):
                        q = QST[s][:, (qt + v) * P:(qt + v) * P + P]
                        o = PS[Dp][:, 0, v * META:v * META + META]
                        mm(o, q, KHH[kv][:, T:L], True, False, *S_sm.waits(), mark=False)
                        t = mm(o, q, KLL[kv][:, T:L], False, True, mark=v == 3)
                    st["sm"] = t
                if qt == 7:
                    S_qs[s].free = st["s", u]

            def maxima(u):
                v = u % 4
                g = (u // 4) % 2
                if v == 0:
                    st["mt"] = dve(lambda e, k: e.tensor_reduce(
                        MXT[:, 4 * g:4 * g + 4], PS[Dp][:, 0, 0:4 * META].rearrange("p (a b) -> p a b", b=META),
                        AX.X, MAX), st["sm"])
                m = dve(lambda e, k: e.tensor_reduce(MXM[:, v:v + 1], both(u % 2), AX.X, MAX), st["s", u],
                        st["mt"])
                st["nb", u] = ts(NB[:, v:v + 1], MXM[:, v:v + 1], MXT[:, 4 * g + v:4 * g + v + 1], MAX, m,
                                 s2=-scale1, op1=MUL)

            def exps(u):
                v, g = u % 4, (u // 4) % 2
                fun(ACT.Exp, PB[u % 2][:, :], both(u % 2), st["nb", u], *S_pb[u % 2].waits(), scale=scale1,
                    bias=NB[:, v:v + 1], acc=RSA[:, v:v + 1])
                a = fun(ACT.Exp, PM[g][:, v, :], PS[Dp][:, 0, v * META:v * META + META],
                        *(S_pm[g].waits() if v == 0 else []), scale=scale1, bias=NB[:, v:v + 1],
                        acc=RSB[:, v:v + 1])
                st["e", u] = S_sc[u % 2].free = a
                if v == 3:
                    S_sm.free = a

            def norms(u):
                v, g = u % 4, (u // 4) % 2
                x = tt(RI[:, v:v + 1], RSA[:, v:v + 1], RSB[:, v:v + 1], ADD, st["e", u])
                x = recip(RI[:, v:v + 1], RI[:, v:v + 1], x)
                tt(PB[u % 2][:, :], PB[u % 2][:, :], RI[:, v:v + 1].to_broadcast([P, T]), MUL, x, q="pool")
                st["p", u] = tt(PM[g][:, v, :], PM[g][:, v, :], RI[:, v:v + 1].to_broadcast([P, META]), MUL,
                                q="pool")

            def turns(u):
                v, g = u % 4, (u // 4) % 2
                for h in range(2):
                    for kt in range(4):
                        c = (4 * h + kt) * P
                        t = tr(PS[C][:, h, kt * P:kt * P + P], PB[u % 2][:, c:c + P], SQC[:, 0, :],
                               st["p", u], *(S_tc[h].waits() if kt == 0 else []), mark=kt == 3)
                    st["t", u, h] = t
                S_pb[u % 2].free = t
                if v == 3:
                    for x in range(4):
                        t = tr(PS[Dp][0:META, 1, x * P:x * P + P], PM[g][:, x, :], SQC[:, 0, :],
                               *(S_av.waits() if x == 0 else []), mark=x == 3)
                    st["tm"] = S_pm[g].free = t

            def parts(u):
                v, g = u % 4, (u // 4) % 2
                w = S_pt[g].waits() if v == 0 else []
                for h in range(2):
                    src = PS[C][:, h, :].rearrange("p (k q) -> p k q", q=P)
                    dst = slice(4 * h, 4 * h + 4)
                    a = copy_(PTH[g][:, dst, v * P:v * P + P], src, st["t", u, h], *w)
                    S_tc[h].free = tt(PTL[g][:, dst, v * P:v * P + P], src, PTH[g][:, dst, v * P:v * P + P],
                                      SUB, a, *w)
                st["l", u] = S_tc[1].free
                if v == 3:
                    a = copy_(PMH[:, :], PS[Dp][0:META, 1, :], st["tm"], *S_pmh.waits())
                    st["lm"] = tt(PML[:, :], PS[Dp][0:META, 1, :], PMH[:, :], SUB, a, *S_pmh.waits())

            def values(u):
                s, qt = divmod(u, 8)
                g = (u // 4) % 2
                o = PS[Dp][:, 1, :]
                n = 0
                for kt in range(9):
                    rows = slice(0, P) if kt < 8 else slice(0, META)
                    for hl, (Pm, Pmm) in enumerate(((PTH, PMH), (PTL, PML))):
                        rh = Pm[g][:, kt, :] if kt < 8 else Pmm[:, :]
                        t = mm(o, VS1[kv][rows, kt, :], rh, n == 0, n == 17, st["lm"], st["l", u], t_vs,
                               mark=n == 17)
                        n += 1
                S_pt[g].free = S_pmh.free = t
                mine, rest = slice(64 * s, 64 * s + 64), slice(64 - 64 * s, 128 - 64 * s)
                a = copy_(OT[g][mine, :], PS[Dp][rest, 1, :], t, *S_ot[g].waits())
                x = tt(OT[g][mine, :], OT[g][mine, :], PS[Dp][mine, 1, :], ADD, a)
                S_av.free = x
                c0 = (qt - 3) * P
                seg = lambda k: GT[mine, k + 4 + 2 * kv, c0:c0 + HALF]
                S_ot[g].free = stt(seg, OT[g][mine, :], 0.5, seg, MUL, MUL, x)

            def body():
                stage(0)
                stage(1)
                for u in range(16 + 2):
                    if u < 16:
                        scores(u)
                        maxima(u)
                        exps(u)
                    if u >= 2 and (u - 2) % 4 == 3:
                        values(u - 2)
                    if 1 <= u <= 16:
                        turns(u - 1)
                        parts(u - 1)
                    if u < 16:
                        norms(u)
            return body

        for kv in range(2):
            loop(2, at_slots, heads_of_tile(kv))
        t_att = S_ot[1].free
        ps[C].free, ps[Dp].free = S_tc[1].free, S_av.free

        w_h = [load("act", H[:, m, :], xT[m][:, 0:T], t_att if m == 0 else None) for m in range(KT)]

        def mh(kt, c, n):
            return MH[:, kt, c:c + n]

        def ml(kt, c, n):
            return ML[:, kt, c:c + n]

        def split_all(src, w, hi=MH, lo=ML):
            xw = ([None] * KT, [None] * KT)
            for m in range(KT):
                xw[0][m] = copy_(hi[:, m, :], src[:, m, :], w)
                xw[1][m] = tt(lo[:, m, :], src[:, m, :], hi[:, m, :], SUB, xw[0][m])
            return xw

        xw = split_all(GT, t_att)
        z1 = dve(lambda e, k: e.memset(ACC1[:, :], 0.0), t_att)

        w_pos = load("act", PI[:, :], pos.broadcast_to((P, T)), t_att)
        TWO_PI = 2 * np.pi
        C1 = 6.28125
        C2 = float(np.round((TWO_PI - C1) * 2 ** 21) / 2 ** 21)
        C3 = float(np.float32(TWO_PI - C1 - C2))
        MAGIC = float(3 << 22)
        PI_LO = float(np.nextafter(np.float32(np.pi), np.float32(0)))
        last_a = None
        for inv, sgn, CO, SI in (("inv_ret", "sgn_ret", COS2, SIN2), ("inv_mla", "sgn_mla", COS3, SIN3)):
            x = ts(ANG[:, :], PI[:, :], col(inv), MUL, w_pos, last_a)
            x = ts(KR_[:, :], ANG[:, :], 1.0 / TWO_PI, MUL, x, s2=MAGIC, op1=ADD)
            x = ts(KR_[:, :], KR_[:, :], MAGIC, SUB, x)
            for c in (C1, C2, C3):
                x = stt(RED[:, :], KR_[:, :], -c, ANG[:, :] if c == C1 else RED[:, :],
                        MUL, ADD, x)
            x = ts(RED[:, :], RED[:, :], PI_LO, ALU.min, x, s2=-PI_LO, op1=MAX)
            a = fun(ACT.Sin, SI[:, :], RED[:, :], x)
            a = fun(ACT.Abs, ANG[:, :], RED[:, :])
            last_a = fun(ACT.Sin, CO[:, :], ANG[:, :], a, scale=-1.0, bias=col("halfpi"))
            t_tab = ts(SI[:, :], SI[:, :], col(sgn), MUL, last_a)

        S_n = [Slot(), Slot()]
        split_to(S_RET)
        n1 = N1

        def out1():
            for j in range(2):
                p = (A, B)[j]
                t = project(S_OUT1 + j, 2, full, mh, ml, halves(p), *ps[p].waits(), xw=xw)
                hm = lambda k, j=j: H[:, k * 2 + j, :]
                x = tt(hm, hm, both(p), ADD, t, *w_h)
                ps[p].free = x
                a = tt(N1[j][:, :], hm, hm, MUL, x)
                S_n[j].free = st["acc"] = tt(ACC1[:, :], ACC1[:, :], N1[j][:, :], ADD, a)

        loop(4, ps + S_n, out1)

        def norm_sum(acc, pair, rs, n, w):
            t = sums(acc, pair, w)
            return rstd(rs, pair, n, t)

        x = norm_sum(ACC1, C, RS1, D, st["acc"])
        hw = []
        sq = []
        for m in range(KT):
            hw.append(stt(H[:, m, :], H[:, m, :], col("final_g", m), RS1[:, :], MUL, MUL, x))
            a = fun(ACT.Square, N1[m % 2][:, :], H[:, m, :], hw[m], S_n[m % 2].free)
            if m == 0:
                y = dcopy(ACC1[:, :], N1[0][:, :], a)
            else:
                y = tt(ACC1[:, :], ACC1[:, :], N1[m % 2][:, :], ADD, a)
            S_n[m % 2].free = y

        def norm_split(src, g, rs, w, tmp, slots):
            xw = ([None] * KT, [None] * KT)
            for m in range(KT):
                v = stt(tmp[m % 2][:, :], src[:, m, :], col(g, m), rs[:, :], MUL, MUL, w, slots[m % 2].free)
                xw[0][m] = copy_(MH[:, m, :], tmp[m % 2][:, :], v)
                slots[m % 2].free = xw[1][m] = tt(ML[:, m, :], tmp[m % 2][:, :], MH[:, m, :], SUB, xw[0][m])
            return xw

        x = norm_sum(ACC1, Dp, RS1, D, y)
        xw = norm_split(H, "pre_mix", RS1, x, N1, S_n)
        xw_norm2 = xw[1][KT - 1]

        w_rx = load("act", RX[:, :, :], squares[5:13].rearrange("n p c -> p n c"), xw_norm2)
        hs = nc.dram_tensor("residual", (KT, P, T), F32, kind="Internal").ap()
        w_spill = [load("act", hs[m], H[:, m, :], hw[m]) for m in range(KT)]
        (S_rr, S_t, S_rk, S_rq, S_rv, S_kn, S_vn, S_zt) = ret_slots = [Slot(xw_norm2) for _ in range(8)]
        s_ret = S_RET
        ret_scale = CH ** -0.5
        split_to(S_LORA)

        def turn2(p, dst, slot, t, sc):
            a = copy_(RRAW[:, :], both(p), t, *S_rr.waits(), scale=sc)
            ps[p].free = a
            x = tt(RT1[:, :], RRAW[:, :], COS2[:, :], MUL, a, t_tab, *S_t.waits())
            tt(dst[0:64, :], RRAW[64:128, :], SIN2[64:128, :], MUL, *slot.waits())
            y = tt(dst[64:128, :], RRAW[0:64, :], SIN2[0:64, :], MUL)
            S_rr.free = y
            y = tt(dst[:, :], dst[:, :], RT1[:, :], ADD, y)
            S_t.free = y
            return y

        def chunk(x, n):
            return x[:, n * CH:n * CH + CH]

        def retention():
            t = project(s_ret, 4, full, mh, ml, halves(A), *ps[A].waits(), xw=xw)
            k_ = turn2(A, RK, S_rk, t, ret_scale)
            z_ = dcopy(TINY[:, 32:33], lambda k: COLS[:, bass.ds(k + COL["zeta"], 1)], *S_zt.waits())
            z_ = dcopy(TINY[:, 33:34], lambda k: COLS[:, bass.ds(k + COL["gch"], 1)])
            t = project(s_ret + 1, 4, full, mh, ml, halves(B), *ps[B].waits())
            v_ = copy_(RV[:, :], both(B), t, *S_rv.waits())
            ps[B].free = v_
            for n in range(NCH):
                t = tr(PS[C][:, n // 4, (n % 4) * CH:(n % 4) * CH + CH], chunk(RK, n), SQC[:, 0, :], k_,
                       *ps[C].waits(), mark=n == 7)
            kn = ts(RKN[:, :, :].rearrange("p a b -> p (a b)"), both(C), TINY[:, 32:33], MUL, t, z_, *S_kn.waits())
            ps[C].free = kn
            for n in range(NCH):
                t = tr(PS[Dp][:, n // 4, (n % 4) * CH:(n % 4) * CH + CH], chunk(RV, n), SQC[:, 0, :], v_,
                       *ps[Dp].waits(), mark=n == 7)
            S_rv.free = t
            vn = copy_(RVN[:, :, :].rearrange("p a b -> p (a b)"), both(Dp), t, *S_vn.waits())
            ps[Dp].free = vn
            t = project(s_ret + 2, 4, full, mh, ml, halves(A), *ps[A].waits())
            for n in range(NCH - 1):
                u = mm(PS[C][:, n // 4, (n % 4) * CH:(n % 4) * CH + CH], RKN[:, n, :], RVN[:, n, :], True, True, kn, vn,
                       *ps[C].waits(), mark=n == 6)
            S_kn.free = u
            x = dve(lambda e, k: e.memset(chunk(RV, 0), 0.0), u)
            for n in range(NCH - 1):
                x = stt(chunk(RV, n + 1), chunk(RV, n), TINY[:, 33:34],
                        PS[C][:, n // 4, (n % 4) * CH:(n % 4) * CH + CH], MUL, ADD, x)
            ps[C].free = S_zt.free = x
            states = x
            q_ = turn2(A, RQ, S_rq, t, 1.0)
            t = project(s_ret + 3, 4, full, mh, ml, halves(B), *ps[B].waits())
            th = RKN[:, :, :].rearrange("p a b -> p (a b)")
            a = fun(ACT.Tanh, th, both(B), t, u, scale=0.5)
            x = stt(lambda k: GR[:, k, :], th, 1.0, both(B), ADD, MUL, a)
            S_kn.free = x
            ps[B].free = x
            xq = tt(RRAW[:, :].rearrange("p (n c) -> p n c", c=CH), RQ[:, :].rearrange("p (n c) -> p n c", c=CH),
                    lambda k: RX[:, k, :].unsqueeze(1).to_broadcast([P, NCH, CH]), MUL, w_rx, q_)
            for n in range(NCH):
                t = mm(PS[Dp][:, n // 4, (n % 4) * CH:(n % 4) * CH + CH], chunk(RK, n), chunk(RQ, n), True, True, q_,
                       *ps[Dp].waits(), mark=n == 7)
            S_rk.free = S_rq.free = t
            sc = tt(RT1[:, :].rearrange("p (n c) -> p n c", c=CH),
                    PS[Dp][:, :, :].rearrange("p a (n c) -> p (a n) c", c=CH),
                    lambda k: RX[:, k + 4, :].unsqueeze(1).to_broadcast([P, NCH, CH]), MUL, t, q_)
            ps[Dp].free = sc
            for n in range(NCH):
                o = PS[A][:, n // 4, (n % 4) * CH:(n % 4) * CH + CH]
                mm(o, chunk(RV, n), chunk(RRAW, n), True, False, xq, states, *ps[A].waits(), mark=False)
                t = mm(o, RVN[:, n, :], chunk(RT1, n), False, True, sc, mark=n == 7)
            S_rr.free = S_t.free = S_rv.free = S_vn.free = t
            a = vcopy(lambda k: MX[:, k, :], both(A), t)
            ps[A].free = a

        loop(4, ps + ret_slots, retention)
        t_ret = ps[A].free

        split_to(S_MLA)
        S_lt = [Slot(t_ret), Slot(t_ret)]
        lora = []
        xw_mean = SQC[:, 3, :]
        y = sq_ = None
        for n in range(6):
            p = (A, B)[n % 2]
            t = project(S_LORA + n, 0, full, mh, ml, halves(p), *ps[p].waits())
            a = copy_(CQR[:, n, :] if n < 5 else KRR[:, :], both(p), t, t_ret)
            ps[p].free = a
            lora.append(a)
            if 1 <= n < 5:
                m = n - 1
                v = sums(LT[0], Dp, sq_, square=xw_mean)
                S_lt[0].free = v
                y = rstd(LT[1], Dp, 1, v, S_lt[1].free)
                y = stt(MX[:, m, :], MX[:, m, :], col("ret_gn", m), LT[1][:, :], MUL, MUL, y)
                S_lt[1].free = y
                y = stt(MX[:, m, :], MX[:, m, :], 0.5, GR[:, m, :], MUL, MUL, y)
            if n < 4:
                v = sums(MX[:, n, :], C, t_ret, square=xw_mean)
                x = tt(MX[:, n, :], MX[:, n, :], both(C), SUB, v)
                ps[C].free = x
                sq_ = fun(ACT.Square, LT[0][:, :], MX[:, n, :], x, S_lt[0].free)
        t_gn = y
        t_lora = t

        cw = ([None] * 5, [None] * 5)
        free = [S_lt[0].free, t_gn]
        for name, lo, cnt, pair, rs in (("mla_q", 0, 3, C, LP[0]), ("mla_kv", 3, 2, Dp, LP[1])):
            for j in range(cnt):
                b = j % 2
                a = fun(ACT.Square, LT[b][:, :], CQR[:, lo + j, :], free[b], t_gn)
                mm(PS[pair][:, 0, :], SQC[:, 1, :], LT[b][:, 0:HALF], j == 0, j == cnt - 1, a, *ps[pair].waits(),
                   mark=False)
                free[b] = mm(PS[pair][:, 1, :], SQC[:, 1, :], LT[b][:, HALF:T], j == 0, j == cnt - 1)
            x = rstd(rs, pair, cnt * P, free[(cnt - 1) % 2])
            for j in range(cnt):
                b = j % 2
                v = stt(LT[b][:, :], CQR[:, lo + j, :], col(name, j), rs[:, :], MUL, MUL, x, free[b])
                cw[0][lo + j] = copy_(CNH[:, lo + j, :], LT[b][:, :], v, t_lora)
                free[b] = cw[1][lo + j] = tt(CNL[:, lo + j, :], LT[b][:, :], CNH[:, lo + j, :], SUB, cw[0][lo + j])
        cn_done = free[0], free[1]
        tt(KRR[64:96, :], KRR[64:96, :], COS3[64:96, :], MUL, lora[5], t_tab)
        x = tt(LT[0][64:96, :], KRR[96:128, :], SIN3[96:128, :], MUL, *cn_done)
        x = tt(KRR[64:96, :], KRR[64:96, :], LT[0][64:96, :], ADD, x)
        for j in range(2):
            a = copy_(QKS[j][2][64:96, :], KRR[64:96, :], x, t_lora, *w_spill)
            t_kr = tt(QKS[j][3][64:96, :], KRR[64:96, :], QKS[j][2][64:96, :], SUB, a)
        cm = load("act", CMF[:, :, :], squares[4:5].rearrange("n p c -> p n c"), t_kr)
        c1 = dcopy(CMB[:, 0, :], CMF[:, 0, :], cm)
        t_cmb = dcopy(CMB[:, 1, :], SQC[:, 0, :], c1)

        def cnh(kt, c, n):
            return CNH[:, kt, c:c + n]

        def cnl(kt, c, n):
            return CNL[:, kt, c:c + n]

        S_set, S_v2 = [Slot(t_kr), Slot(t_kr)], [Slot(t_kr), Slot(t_kr)]
        ready = [Slot(), Slot()]
        S_mq, S_mkv, S_mt = Slot(t_kr), Slot(t_kr), Slot(t_kr)
        S_lp = [Slot(t_kr), Slot(t_kr)]
        S_ptl, S_mot = Slot(t_kr), Slot()
        S_av = Slot(ps[Dp].free)
        S_tc = [Slot(ps[C].free), Slot(ps[C].free)]
        ml_slots = ready + S_set + S_v2 + [S_mq, S_mkv, S_mt] + S_lp + [S_ptl, S_mot, S_av] + S_tc + [ps[A], ps[B]]
        scale2 = MQK ** -0.5
        st = {}

        def mla_project(h, step, j):
            s = S_MLA + h
            QH, QL, KH, KL = QKS[j]
            project(s, step, [(0, 0), (1, 1), (2, 2)], cnh, cnl, halves(A), *ps[A].waits(), xw=cw, last=False)
            t = project(s, step, [(3, 3), (4, 4)], cnh, cnl, halves(B), *ps[B].waits(), xw=cw)
            a = copy_(MQ[:, :], both(A), t, *S_mq.waits())
            ps[A].free = a
            b = copy_(MKV[:, :], both(B), t, *S_mkv.waits())
            ps[B].free = b
            tt(MT1[64:96, :], MQ[96:128, :], SIN3[96:128, :], MUL, a, *S_mt.waits())
            x = tt(MQ[64:96, :], MQ[64:96, :], COS3[64:96, :], MUL)
            x = tt(MQ[64:96, :], MQ[64:96, :], MT1[64:96, :], ADD, x)
            S_mt.free = x
            kh = copy_(KH[0:64, :], MKV[0:64, :], b, *S_set[j].waits())
            for kt in range(8):
                t = tr(PS[C][:, kt // 4, (kt % 4) * P:(kt % 4) * P + P], MKV[:, kt * P:kt * P + P], SQC[:, 0, :], b,
                       *S_tc[0].waits(), *S_tc[1].waits(), mark=kt == 7)
            a = copy_(QH[0:MQK, :], MQ[0:MQK, :], x)
            S_mq.free = tt(QL[0:MQK, :], MQ[0:MQK, :], QH[0:MQK, :], SUB, a, *S_set[j].waits())
            x = tt(KL[0:64, :], MKV[0:64, :], KH[0:64, :], SUB, kh)
            S_mkv.free = x
            v = PS[C][:, :, :].rearrange("p a (k c) -> p (a k) c", c=P)[:, :, 64:128]
            a = copy_(VS2[j][:, :, 0:64], v, t, *S_v2[j].waits())
            ready[j].free = S_tc[0].free = S_tc[1].free = tt(VS2[j][:, :, 64:128], v, VS2[j][:, :, 0:64], SUB, a, x)
            S_mkv.free = ready[j].free

        def mla_head(j, tile):
            QH, QL, KH, KL = QKS[j]

            def scores(u):
                p = ps[u % 2]
                q0 = u * P
                n = q0 + P
                for h in range((n + HALF - 1) // HALF):
                    c = slice(h * HALF, min(n, h * HALF + HALF))
                    o = PS[u % 2][:, h, 0:c.stop - c.start]
                    diag = c.start <= q0 < c.stop
                    mm(o, QH[0:MQK, q0:q0 + P], KH[0:MQK, c], True, False, *ready[j].waits(), *p.waits(),
                       mark=False)
                    mm(o, QH[0:MQK, q0:q0 + P], KL[0:MQK, c], False, False, mark=False)
                    t = mm(o, QL[0:MQK, q0:q0 + P], KH[0:MQK, c], False, not diag, mark=not diag)
                    if diag:
                        t = mm(PS[u % 2][:, h, q0 - c.start:q0 - c.start + P], CMB[:, 1, :], CMB[:, 0, :], False, True,
                               t_cmb)
                st["s", u] = t

            def maxima(u):
                v, n = u % 4, u * P + P
                m = dve(lambda e, k: e.tensor_reduce(MXM[:, v:v + 1], both(u % 2)[:, 0:n], AX.X, MAX), st["s", u])
                st["nb", u] = ts(NB[:, v:v + 1], MXM[:, v:v + 1], -scale2, MUL, m)

            def exps(u):
                v, n = u % 4, u * P + P
                a = fun(ACT.Exp, LP[u % 2][:, 0:n], both(u % 2)[:, 0:n], st["nb", u], *S_lp[u % 2].waits(),
                        scale=scale2, bias=NB[:, v:v + 1], acc=RSA[:, v:v + 1])
                st["e", u] = ps[u % 2].free = a

            def norms(u):
                v, n = u % 4, u * P + P
                x = recip(RI[:, v:v + 1], RSA[:, v:v + 1], st["e", u])
                st["p", u] = tt(LP[u % 2][:, 0:n], LP[u % 2][:, 0:n], RI[:, v:v + 1].to_broadcast([P, n]), MUL, x,
                                q="pool")

            def turns(u):
                for kt in range(u + 1):
                    h = kt // 4
                    last = kt == u or kt % 4 == 3
                    t = tr(PS[C][:, h, (kt % 4) * P:(kt % 4) * P + P], LP[u % 2][:, kt * P:kt * P + P], SQC[:, 0, :],
                           st["p", u], *(S_tc[h].waits() if kt % 4 == 0 else []), mark=last)
                    st["t", u, h] = t
                S_lp[u % 2].free = t

            def parts(u):
                v = u % 4
                w = S_ptl.waits() if v == 0 else []
                for h in range((u + 4) // 4):
                    k0, k1 = 4 * h, min(4 * h + 4, u + 1)
                    src = PS[C][:, h, 0:(k1 - k0) * P].rearrange("p (k q) -> p k q", q=P)
                    a = copy_(LTH[:, k0:k1, v * P:v * P + P], src, st["t", u, h], *w)
                    S_tc[h].free = tt(LTL[:, k0:k1, v * P:v * P + P], src, LTH[:, k0:k1, v * P:v * P + P], SUB, a, *w)
                    st["l", u] = S_tc[h].free

            def values(u):
                g = u // 4
                nk = 4 * g + 4
                for kt in range(nk):
                    c0 = max(0, kt - 4 * g) * P
                    for hl, Pt in enumerate((LTH, LTL)):
                        last = kt == nk - 1 and hl == 1
                        t = mm(PS[Dp][:, 1, c0:HALF], VS2[j][:, kt, :], Pt[:, kt, c0:HALF], kt == 0 and hl == 0, last,
                               st["l", u], *ready[j].waits(), *S_av.waits(), mark=last)
                S_ptl.free = t
                if g == 1:
                    S_v2[j].free = S_set[j].free = t
                mine, rest = slice(64 * j, 64 * j + 64), slice(64 - 64 * j, 128 - 64 * j)
                a = copy_(MOT[mine, :], PS[Dp][rest, 1, :], t, *S_mot.waits())
                dst = lambda k: MX[mine, tile(k), g * HALF:g * HALF + HALF]
                S_av.free = S_mot.free = tt(dst, MOT[mine, :], PS[Dp][mine, 1, :], ADD, a, t_gn)

            for u in range(8 + 2):
                if u < 8:
                    scores(u)
                    maxima(u)
                    exps(u)
                if u >= 2 and (u - 2) % 4 == 3:
                    values(u - 2)
                if 1 <= u <= 8:
                    turns(u - 1)
                    parts(u - 1)
                if u < 8:
                    norms(u)

        split_to(S_MLA + 2)
        mla_project(0, 0, 0)

        def mla_pair():
            slab_split(S_MLA + 2, 2)
            slab_split(S_MLA + 3, 2)
            mla_project(1, 2, 1)
            mla_head(0, lambda k: k + 4)
            mla_project(2, 2, 0)
            mla_head(1, lambda k: k + 4)

        loop(3, ml_slots, mla_pair)
        mla_project(7, 0, 1)
        mla_head(0, lambda k: 7)
        mla_head(1, lambda k: 7)
        done_split[0] = S_OUT2
        t_mla = S_av.free
        ps[C].free, ps[Dp].free = S_tc[1].free, S_av.free

        w_h = [load("act", H[:, m, :], hs[m], t_mla, *w_spill) for m in range(KT)]
        xw = split_all(MX, t_mla)
        z2 = dve(lambda e, k: e.memset(ACC2[:, :], 0.0), t_mla)
        S_n = [Slot(), Slot()]
        split_to(S_FFN)

        def out2():
            for j in range(2):
                p = (A, B)[j]
                t = project(S_OUT2 + j, 2, full, mh, ml, halves(p), *ps[p].waits(), xw=xw)
                b = fun(ACT.Square, N2[j][:, :], both(p), t, z2, *S_n[j].waits())
                a = vcopy(lambda k, j=j: O2[:, k * 2 + j, :], both(p), b)
                ps[p].free = a
                S_n[j].free = st["acc"] = tt(ACC2[:, :], ACC2[:, :], N2[j][:, :], ADD, b)

        loop(4, ps + S_n, out2)
        x = norm_sum(ACC2, C, RS2, D, st["acc"])
        for m in range(KT):
            b = m % 2
            v = stt(O2[:, m, :], O2[:, m, :], col("post_mix", m), RS2[:, :], MUL, MUL, x)
            v = tt(H[:, m, :], H[:, m, :], O2[:, m, :], ADD, v, w_h[m])
            a = fun(ACT.Square, N2[b][:, :], H[:, m, :], v, S_n[b].free)
            y = dcopy(ACC2[:, :], N2[b][:, :], a) if m == 0 else tt(ACC2[:, :], ACC2[:, :], N2[b][:, :], ADD, a)
            S_n[b].free = y
        x = norm_sum(ACC2, Dp, RS2, D, y)
        xw = norm_split(H, "pre_ffn", RS2, x, N2, S_n)

        z3 = dve(lambda e, k: e.memset(FA[:, :, :].rearrange("p a b -> p (a b)"), 0.0), xw[1][KT - 1])
        S_th, S_hf, S_hb = [Slot(z3), Slot(z3)], [Slot(z3), Slot(z3)], [Slot(z3), Slot(z3)]
        hb_ready = [Slot(), Slot()]
        ffn_slots = ps + S_th + S_hf + S_hb + hb_ready
        st = {}

        def gate_up(s, step, b):
            for m in range(2):
                pg, pu = (A, C)[m], (B, Dp)[m]
                t = project(s + 2 * m, step, full, mh, ml, halves(pg), *ps[pg].waits(), xw=xw)
                a = fun(ACT.Tanh, TH[m][:, :], both(pg), t, *S_th[m].waits(), scale=0.5)
                x = stt(TH[m][:, :], TH[m][:, :], 1.0, both(pg), ADD, MUL, a)
                ps[pg].free = x
                t = project(s + 2 * m + 1, step, full, mh, ml, halves(pu), *ps[pu].waits())
                x = stt(HF[m][:, :], TH[m][:, :], 0.5, both(pu), MUL, MUL, t, x, *S_hf[m].waits())
                ps[pu].free = S_th[m].free = x
                a = copy_(HBH[b][:, m, :], HF[m][:, :], x, *(S_hb[b].waits() if m == 0 else []))
                S_hf[m].free = tt(HBL[b][:, m, :], HF[m][:, :], HBH[b][:, m, :], SUB, a,
                                  *(S_hb[b].waits() if m == 0 else []))
            hb_ready[b].free = S_hf[1].free

        def down(s, step, b):
            for m in range(8):
                p = m % 4
                hx = lambda kt, c, n: HBH[b][:, kt, c:c + n]
                lx = lambda kt, c, n: HBL[b][:, kt, c:c + n]
                ws = hb_ready[b].waits() if m == 0 else []
                t = project(s + m // 4, step, [(2 * (m % 4), 0), (2 * (m % 4) + 1, 1)], hx, lx, halves(p),
                            *ps[p].waits(), *ws, last=m % 4 == 3)
                x = tt(FA[:, m, :], FA[:, m, :], both(p), ADD, t)
                ps[p].free = x
            S_hb[b].free = t
            st["fa"] = x

        split_to(S_PLEP)
        gate_up(S_FFN, 0, 0)

        def ffn_pair():
            gate_up(S_FFN + 4, 12, 1)
            down(S_FFN + 8, 12, 0)
            gate_up(S_FFN + 10, 12, 0)
            down(S_FFN + 14, 12, 1)

        loop(5, ffn_slots, ffn_pair)
        down(S_PLEP - 2, 0, 0)
        t_ffn = st["fa"]

        w_p = load("act", PR[:, :, :], pT.rearrange("a p t -> p a t"), t_ffn)
        split_to(NSLAB)
        pw = ([None] * 2, [None] * 2)
        for j in range(2):
            pw[0][j] = copy_(PH[:, j, :], PR[:, j, :], w_p)
            pw[1][j] = tt(PL[:, j, :], PR[:, j, :], PH[:, j, :], SUB, pw[0][j])
        S_n = [Slot(t_ffn), Slot(t_ffn)]

        def add_square(src, b, acc, first, w):
            a = fun(ACT.Square, TH[b][:, :], src, w, S_n[b].free)
            y = dcopy(acc, TH[b][:, :], a) if first else tt(acc, acc, TH[b][:, :], ADD, a)
            S_n[b].free = y
            return y

        for m in range(8):
            p = m % 2
            t = project(S_PLEP + m // 4, 0, [(2 * (m % 4), 0), (2 * (m % 4) + 1, 1)],
                        lambda kt, c, n: PH[:, kt, c:c + n], lambda kt, c, n: PL[:, kt, c:c + n], halves(p),
                        *ps[p].waits(), xw=pw, last=m % 4 == 3)
            a = copy_(EB[:, m, :], both(p), t, t_ffn)
            ps[p].free = a
            y1 = add_square(FA[:, m, :], 0, HF[0][:, :], m == 0, t_ffn)
            y2 = add_square(EB[:, m, :], 1, HF[1][:, :], m == 0, a)
        t_e = t
        x = norm_sum(HF[0], C, RS3, D, y1)
        hw = ([None] * KT, [None] * KT)
        for m in range(KT):
            v = stt(FA[:, m, :], FA[:, m, :], col("post_ffn", m), RS3[:, :], MUL, MUL, x)
            v = tt(H[:, m, :], H[:, m, :], FA[:, m, :], ADD, v)
            hw[0][m] = copy_(GH[:, m, :], H[:, m, :], v, t_e)
            hw[1][m] = tt(GL[:, m, :], H[:, m, :], GH[:, m, :], SUB, hw[0][m], v)
        x = norm_sum(HF[1], Dp, RS4, D, y2)
        hb = ts(TINY[:, 40:48], COLS[:, COL["b_ple"]:COL["b_ple"] + 8], 0.5, MUL)
        e_done = [stt(EB[:, m, :], EB[:, m, :], col("ple_norm", m), RS4[:, :], MUL, MUL, x) for m in range(KT)]
        for m in range(KT):
            p = (A, B, C, Dp)[m % 4]
            t = project(S_PLEG + m, 0, full, lambda kt, c, n: GH[:, kt, c:c + n], lambda kt, c, n: GL[:, kt, c:c + n],
                        halves(p), *ps[p].waits(), xw=hw)
            a = fun(ACT.Tanh, OB[:, m, :], both(p), t, e_done[KT - 1], hb, scale=0.5, bias=TINY[:, 40 + m:41 + m])
            ps[p].free = a
            x = stt(OB[:, m, :], OB[:, m, :], 1.0, EB[:, m, :], ADD, MUL, a, e_done[m], hb)
            x = stt(OB[:, m, :], OB[:, m, :], 0.5, H[:, m, :], MUL, ADD, x)
            do("act", lambda e, k, m=m: e.dma_start(outT[m], OB[:, m, :]), x, inc=[(s_out, 16)], mark=False)
        block = ctx.enter_context(nc.Block())

        @block.sync
        def _(e):
            pr.emit("sp", e)
            e.wait_ge(s_out, 16 * KT)

        @block.scalar
        def _(e):
            pr.emit("act", e)

        @block.gpsimd
        def _(e):
            pr.emit("pool", e)

        @block.tensor
        def _(e):
            pr.emit("pe", e)

        @block.vector
        def _(e):
            pr.emit("dve", e)


def shape_constants():
    sq = np.zeros((13, P, P), np.float64)
    sq[0] = np.eye(P)
    sq[1] = 1.0
    sq[2, :64, :64] = sq[2, 64:, 64:] = 1.0
    sq[3] = 1.0 / P
    j = np.arange(P)
    sq[4] = np.where(j[None, :] > j[:, None], -1e30, 0.0)
    zeta, gch = np.zeros((P, RH)), np.zeros((P, RH))
    for h in range(RH):
        lg = np.log(1.0 - 2.0 ** (-5.0 - h))
        sq[5 + h] = np.exp((j + 1) * lg)[None, :]
        diff = j[None, :] - j[:, None]
        sq[9 + h] = np.where(diff >= 0, np.exp(np.maximum(diff, 0) * lg), 0.0)
        zeta[:, h] = np.exp((CH - 1 - j) * lg)
        gch[:, h] = np.exp(CH * lg)
    n_f = HD // 4
    fr = 1.0 / (10000.0 ** (np.arange(n_f) * 2.0 / (HD // 2)))
    tok = np.arange(T)
    row, cl = tok // 64 - (T // 64) // 2, tok % 64 - 32
    ang = np.concatenate([row[:, None] * fr, cl[:, None] * fr], axis=1)
    ang = np.concatenate([ang, np.zeros((META, HD // 2))], axis=0).T
    rope1 = np.stack([np.tile(np.cos(ang), (4, 1)),
                      np.concatenate([np.sin(ang), -np.sin(ang)] * 2, axis=0)])
    m, l = np.arange(MT5 * P)[:, None], np.arange(1, NL + 1)[None, :]
    dft = np.stack([np.cos(2 * np.pi * ((m * l) % L) / L), np.sin(2 * np.pi * ((m * l) % L) / L)]) / np.sqrt(L * 64.0)
    dft[:, NM:] = 0.0
    dft[:, NL] *= 0.5
    c = np.arange(64)
    cd = np.stack([np.cos(2 * np.pi * c[:, None] * c[None, :] / 64), np.sin(2 * np.pi * c[:, None] * c[None, :] / 64)])
    cd = np.concatenate([cd, cd], axis=2)
    inv_ret = np.tile(1.0 / 10000.0 ** (np.arange(64) / 64.0), 2)
    inv_mla = np.tile(1.0 / 10000.0 ** (np.arange(16) / 16.0), 8)
    half = np.repeat([1.0, -1.0], 64)
    sgn_mla = np.ones(P)
    sgn_mla[96:112] = -1.0
    vec = {"zeta": zeta, "gch": gch, "inv_ret": inv_ret[:, None], "inv_mla": inv_mla[:, None],
           "sgn_ret": half[:, None], "sgn_mla": sgn_mla[:, None], "eps": np.full((P, 1), EPS),
           "halfpi": np.full((P, 1), np.pi / 2)}
    f = np.float32
    return sq.astype(f), rope1.astype(f), dft.astype(f), cd.astype(f), {k: v.astype(f) for k, v in vec.items()}


def slab_layout(w_in, w_out, w_in2, w_uq, w_ukv, w_o, w_gate, w_up, w_down, w_pp, w_pg):
    def tile(w, m):
        k = w.shape[0] // P
        return w[:, m * P:m * P + P].reshape(k, P, P).transpose(1, 0, 2).reshape(P, k * P)

    def pairs(w, k0, m0):
        x = w[k0 * P:k0 * P + 2 * P, m0 * P:m0 * P + 4 * P].reshape(2, P, 4, P)
        return x.transpose(1, 2, 0, 3).reshape(P, 8 * P)

    halves_ = np.concatenate([np.arange(0, HD, 2), np.arange(1, HD, 2)])
    q0 = 2 * FW
    k0 = q0 + 512
    v0 = k0 + 128
    perm_q = np.concatenate([q0 + h * HD + halves_ for h in range(8)])
    perm_k = np.concatenate([k0 + h * HD + halves_ for h in range(2)])
    order = np.concatenate([np.arange(FW), perm_k, np.arange(v0, v0 + 128), perm_q, np.arange(FW, 2 * FW),
                            np.arange(v0 + 128, v0 + 128 + 512)])
    w1 = w_in[:, order]
    out = [tile(w1, m) for m in range(18)] + [tile(w_out, m) for m in range(8)]
    for h in range(RH):
        out += [tile(w_in2, 4 * x + h) for x in (1, 2, 0, 3)]
    out += [tile(w_in2, 16 + n) for n in range(5)]
    kr = w_in2[:, 2048 + 640:]
    sw = np.concatenate([np.arange(16, 32), np.arange(16)])
    out.append(tile(np.concatenate([np.zeros((D, 64), kr.dtype), kr, kr[:, sw]], axis=1), 0))
    for h in range(MH_):
        q = w_uq[:, h * MQK:h * MQK + MQK]
        q = np.concatenate([q, q[:, 64 + sw]], axis=1)
        kv = w_ukv[:, h * 128:h * 128 + 128]
        x = np.concatenate([tile(q, 0), tile(kv, 0)], axis=1)
        out.append(np.concatenate([x, np.zeros((P, 1024 - x.shape[1]), x.dtype)], axis=1))
    out += [tile(w_o, m) for m in range(8)]

    def gu(c):
        return [tile(w, 2 * c + m) for m in range(2) for w in (w_gate, w_up)]

    def dn(c):
        return [pairs(w_down, 2 * c, 0), pairs(w_down, 2 * c, 4)]

    n = DFF // 256
    out += gu(0)
    for c in range(1, n):
        out += gu(c) + dn(c - 1)
    out += dn(n - 1)
    out += [pairs(w_pp, 0, 0), pairs(w_pp, 0, 4)] + [tile(w_pg, m) for m in range(8)]
    return np.ascontiguousarray(np.stack(out))


def kernel(**inputs):
    import concourse.bacc as bacc
    from concourse.bass_utils import run_bass_kernel_spmd as run

    a = {k: np.asarray(v) for k, v in inputs.items()}
    sq, rope1, dft, cd, vec = shape_constants()
    xm = np.concatenate([a["x"][0], a["meta_tokens"]], axis=0)
    xT = np.ascontiguousarray(xm.T.reshape(KT, P, L))
    pT = np.ascontiguousarray(a["p_2"][0, 0].T.reshape(2, P, T))
    slabs = slab_layout(a["w_in"][0], a["w_out"][0], a["w_in_2"][0], a["w_uq_2"][0], a["w_ukv_2"][0], a["w_o_2"][0],
                        a["w_gate_2"][0], a["w_up_2"][0], a["w_down_2"][0], a["w_ple_proj_2"][0],
                        a["w_ple_gate_2"][0])
    assert slabs.shape == (NSLAB, P, 1024)
    halves_ = np.concatenate([np.arange(0, HD, 2), np.arange(1, HD, 2)])
    put = {"norm_g": a["norm_g"], "final_g": a["final_g"], "pre_mix": a["pre_mix_norm_2"],
           "post_mix": a["post_mix_norm_2"], "pre_ffn": a["pre_ffn_norm_2"], "post_ffn": a["post_ffn_norm_2"],
           "ple_norm": a["ple_norm_2"], "b_ple": a["b_ple_gate_2"], "mla_q": a["mla_q_norm_2"],
           "mla_kv": a["mla_kv_norm_2"], "ret_gn": a["ret_gn_w_2"], "b_fmix": a["b_fmix"],
           "q_g": np.tile(a["q_norm_g"][0][halves_], 2), "k_g": np.tile(a["k_norm_g"][0][halves_], 2)}
    cols = np.zeros((P, NCOL), np.float32)
    for n, k in _names:
        cols[:, COL[n]:COL[n] + k] = vec[n] if n in vec else put[n].reshape(k, P).T
    wf = np.ascontiguousarray(a["w_fmix"][0].transpose(1, 0, 2).reshape(64, 512))
    arrays = {"xT": xT, "pT": pT, "pos": np.ascontiguousarray(a["positions_2"]), "slabs": slabs, "cols": cols,
              "squares": sq, "rope1": rope1, "dft": dft, "wf": wf, "cd": cd}
    nc = bacc.Bacc("TRN2", target_bir_lowering=False, num_devices=1)
    args = [nc.dram_tensor(n, v.shape, mybir.dt.from_np(v.dtype), kind="ExternalInput").ap() for n, v in arrays.items()]
    args.append(nc.dram_tensor("outT", (KT, P, T), F32, kind="ExternalOutput").ap())
    two_block_kernel(nc, *args)
    r = run(nc, [arrays], core_ids=[0])
    o = r.results[0]["outT"].reshape(D, T)
    return np.ascontiguousarray(o.T)[None]
```

```python
from contextlib import ExitStack

import numpy as np
import concourse.bass as bass
from concourse import mybir

F32 = mybir.dt.float32
F32R = mybir.dt.float32r
BF16 = mybir.dt.bfloat16
I32 = mybir.dt.int32
ALU = mybir.AluOpType
ACT = mybir.ActivationFunctionType
AX = mybir.AxisListType

P = 128
T = 1024
META = 16
L = T + META
D = 1024
KT = D // P
EPS = 1e-6
HD = 64
NH1 = 8
FW = 512
NL = L // 2
NM = NL + 1
MT5 = (NM + P - 1) // P
DFF = 2816
CH = 128
NCH = T // CH
RH = 4
MH_ = 8
MQK = 96
HALF = 512

S_IN1 = 0
S_OUT1 = 18
S_RET = S_OUT1 + 8
S_LORA = S_RET + 4 * RH
S_MLA = S_LORA + 6
S_OUT2 = S_MLA + MH_
S_FFN = S_OUT2 + 8
S_PLEP = S_FFN + 6 * (DFF // 256)
S_PLEG = S_PLEP + 2
NSLAB = S_PLEG + 8

_names = [("norm_g", 8), ("final_g", 8), ("pre_mix", 8), ("post_mix", 8), ("pre_ffn", 8), ("post_ffn", 8),
          ("ple_norm", 8), ("b_ple", 8), ("mla_q", 3), ("mla_kv", 2), ("ret_gn", 4), ("b_fmix", 4), ("q_g", 1),
          ("k_g", 1), ("zeta", 4), ("inv_ret", 1), ("inv_mla", 1), ("sgn_ret", 1), ("sgn_mla", 1), ("eps", 1),
          ("halfpi", 1), ("gch", 4)]
COL = {}
NCOL = 0
for _n, _k in _names:
    COL[_n] = NCOL
    NCOL += _k
SQ = {n: i for i, n in enumerate(["ident", "ones", "headones", "mean", "causal", "xi0", "xi1", "xi2", "xi3",
                                  "dec0", "dec1", "dec2", "dec3"])}


class Tok:

    def __init__(self, q, off, loop, back=0):
        self.q, self.off, self.loop, self.back = q, off, loop, back

    @property
    def prev(self):
        return Tok(self.q, self.off, self.loop, 1)

    def sem(self):
        return self.q.sem

    def value(self, loop):
        if self.loop is None:
            return self.off, 0
        n = self.loop.incs[self.q]
        if self.loop is loop:
            low = self.off - self.back * n
            assert low > 0, ("wait below one", self.q.name, self.off, n)
            return low, n
        return self.off + (self.loop.n - 1) * n, 0


class Later(Tok):

    def __init__(self):
        self.tok = None

    def sem(self):
        return self.tok.sem()

    def value(self, loop):
        return self.tok.prev.value(loop)


class At:

    def __init__(self, sem, const, step=0):
        self._sem, self.const, self.step = sem, const, step

    def sem(self):
        return self._sem

    def value(self, loop):
        return self.const, (self.step if loop is not None else 0)


class Queue:
    def __init__(self, name, sem):
        self.name, self.sem, self.count, self.ops = name, sem, 0, []


class Loop:
    def __init__(self, n):
        self.n, self.incs, self.bodies = n, {}, {}


class Program:

    def __init__(self, queues):
        self.q = queues
        self.loop = None

    def do(self, name, fn, *waits, inc=(), mark=True, counter=None):
        q = self.q[name]
        c = self.q[counter or name]
        q.ops.append((fn, waits, tuple(inc), c.sem if mark else None))
        if mark:
            c.count += 1
        return Tok(c, c.count, self.loop)

    def last(self, name):
        q = self.q[name]
        return Tok(q, q.count, self.loop)

    def begin(self, n):
        self.loop = Loop(n)
        self.saved = {k: (q.ops, q.count) for k, q in self.q.items()}
        for q in self.q.values():
            q.ops = []

    def end(self):
        for k, q in self.q.items():
            ops, count = self.saved[k]
            self.loop.incs[q] = q.count - count
            if q.ops:
                ops.append((self.loop, q.ops))
            q.count = count + self.loop.n * (q.count - count)
            q.ops = ops
        self.loop = None

    def emit(self, name, eng):
        q = self.q[name]

        def run(ops, loop, i):
            for op in ops:
                if isinstance(op[0], Loop):
                    with eng.Fori(0, op[0].n) as k:
                        run(op[1], op[0], k)
                    continue
                fn, waits, inc, mark = op
                most = {}
                for w in waits:
                    if w is not None:
                        low, step = w.value(loop)
                        s = most.setdefault((id(w.sem()), step), [w.sem(), low])
                        s[1] = max(s[1], low)
                for (_, step), (s, low) in most.items():
                    eng.wait_ge(s, i * step + low if step else low)
                ins = fn(eng, i)
                if mark is not None:
                    ins.then_inc(mark, 1)
                for s, k in inc:
                    ins.then_inc(s, k)
        run(q.ops, None, 0)


class Slot:

    def __init__(self, tok=None):
        self.free = tok
        self.outer = self.later = None

    def waits(self):
        if self.free is not None or self.later is None:
            return [self.free]
        return [self.outer, self.later]

    def enter(self):
        self.outer, self.later, self.free = self.free, Later(), None

    def leave(self):
        if self.free is None:
            self.free = self.outer
        else:
            self.later.tok = self.free
        self.outer = self.later = None


def two_block_kernel(nc, xT, pT, pos, slabs, cols, squares, rope1, dft, wf, cd, outT):
    with ExitStack() as ctx:
        base = 16512
        top = 207 * 1024

        def at(name, shape, dt, kb):
            size = int(np.prod(shape[1:])) * (2 if dt == BF16 else 4)
            assert int(kb * 1024) + size <= top, (name, kb, size)
            return nc.alloc_sbuf_tensor_at(name, shape, dt, offset=base + int(kb * 1024))

        def sem(name):
            return ctx.enter_context(nc.semaphore(name))

        ctx.enter_context(nc.sbuf_tensor("arena", [P, top // 4], F32))

        RAW = at("wraw", [P, 2, 1024], F32, 0)
        WH = [at(f"wh{j}", [P, 1024], F32R, 8 + 4 * j) for j in range(2)]
        WL = [at(f"wl{j}", [P, 1024], F32R, 16 + 4 * j) for j in range(2)]
        COLS = at("cols", [P, NCOL], F32, 24)
        SQC = at("sqc", [P, 4, P], F32, 24.5)
        TINY = at("tiny", [P, 64], F32, 26.5)
        ONE = at("one", [P, 1], F32, 26.75)
        XH = at("xh", [P, KT, L], F32R, 27)
        XL = at("xl", [P, KT, L], F32R, 59.5)
        X = at("x", [P, KT, L], F32, 92)
        FT = at("ft", [P, 4, 1042], F32, 92)
        K1 = at("k1", [P, L], F32, 112.75)
        V1 = at("v1", [P, L], F32, 117)
        Q1 = at("q1", [P, 4, T], F32, 121.25)
        TMP = [at(f"tmp{j}", [P, L], F32, 137.5 + 4.125 * j) for j in range(5)]
        COS1 = at("cos1", [P, L], F32, 158.25)
        SIN1 = at("sin1", [P, L], F32, 162.5)
        GT = at("gt", [P, KT, T], F32, 166.75)
        RS = at("rs", [P, L], F32, 199)
        CT = at("ct", [P, MT5, NL], F32, 27)
        ST = at("st", [P, MT5, NL], F32, 37.5)
        FE = at("fe", [P, 4, NM + 1], F32, 137.5)
        FO = at("fo", [P, 4, NM + 1], F32, 146)
        WF = at("wf", [64, 512], F32, 154.5)
        CD = at("cd", [64, 2, P], F32, 156.5)
        WBD = at("wbd", [P, 2, 4, P], F32, 158)
        GA = at("ga", [P, MT5, 512], F32, 92)
        GB = at("gb", [P, MT5, 512], F32, 102)
        QSB = at("qsb", [P, NL], F32, 203.5)
        PSB = at("psb", [P, NL], F32, 162.5)
        PTH = [at(f"pth{j}", [P, 8, HALF], F32R, 27 + 32 * j) for j in range(2)]
        PTL = [at(f"ptl{j}", [P, 8, HALF], F32R, 43 + 32 * j) for j in range(2)]
        PM = [at(f"pm{j}", [P, 4, META], F32, 91 + 0.25 * j) for j in range(2)]
        KHH = [at(f"khh{j}", [P, L], F32R, 92 + 8.25 * j) for j in range(2)]
        KLL = [at(f"kll{j}", [P, L], F32R, 96.125 + 8.25 * j) for j in range(2)]
        PMH = at("pmh", [META, HALF], F32R, 108.5)
        PML = at("pml", [META, HALF], F32R, 110.5)
        VS1 = [at(f"vs1{j}", [P, 9, P], F32R, 137.5 + 4.625 * j) for j in range(2)]
        QST = [at(f"qst{j}", [P, T], F32R, 146.75 + 4 * j) for j in range(2)]
        PB = [at(f"pb{j}", [P, T], F32, (154.75, 158.75, 112.75, 116.75)[j]) for j in range(4)]
        SMC = at("smc", [P, 2, 4 * META], F32, 203)
        OT = [at(f"ot{j}", [P, HALF], F32, 162.75 + 2 * j) for j in range(2)]
        MH = at("mh", [P, KT, T], F32R, 27)
        ML = at("ml", [P, KT, T], F32R, 59)
        H = at("h", [P, KT, T], F32, 92)
        COS2 = at("cos2", [P, T], F32, 124)
        SIN2 = at("sin2", [P, T], F32, 128)
        COS3 = at("cos3", [P, T], F32, 132)
        SIN3 = at("sin3", [P, T], F32, 136)
        PI = at("pi", [P, T], I32, 140)
        ANG = at("ang", [P, T], F32, 144)
        KR_ = at("kround", [P, T], F32, 148)
        RED = at("red", [P, T], F32, 152)
        N1 = [at(f"n1{j}", [P, T], F32, 199 + 4 * j) for j in range(2)]
        ACC1 = at("acc1", [P, T], F32, 156)
        RS1 = at("rs1", [P, T], F32, 160)
        MX = at("mx", [P, KT, T], F32, 140)
        GR = at("gr", [P, 4, T], F32, 156)
        RRAW = at("rraw", [P, T], F32, 172)
        RT1 = at("rt1", [P, T], F32, 176)
        RK = at("rk", [P, T], F32, 180)
        RQ = at("rq", [P, T], F32, 184)
        RV = at("rv", [P, T], F32, 188)
        RKN = at("rkn", [P, NCH, CH], F32, 192)
        RVN = at("rvn", [P, NCH, CH], F32, 196)
        RX = at("rx", [P, 8, P], F32, 200)
        CQR = at("cqr", [P, 5, T], F32, 172)
        KRR = at("krr", [P, T], F32, 192)
        LT = [at(f"lt{j}", [P, T], F32, 196 + 4 * j) for j in range(2)]
        CNH = at("cnh", [P, 5, T], F32R, 27)
        CNL = at("cnl", [P, 5, T], F32R, 47)
        QKS = [[at(f"qks{j}{n}", [P, T], F32R, (67 if j == 0 else 92) + 4 * n) for n in range(4)] for j in range(2)]
        VS2 = [at(f"vs2{j}", [P, 8, P], F32R, 83 + 4 * j) for j in range(2)]
        LTH = at("lth", [P, 8, HALF], F32R, 108)
        LTL = at("ltl", [P, 8, HALF], F32R, 172)
        LP = [at(f"lp{j}", [P, T], F32, (124, 128, 196)[j]) for j in range(3)]
        LPS = [at(f"lps{j}", [P, (j + 1) * P], F32, (203.5, 204, 205)[j]) for j in range(3)]
        MQ = at("mq", [P, T], F32, 188)
        MKV = at("mkv", [P, T], F32, 192)
        MT1 = at("mt1", [P, T], F32, 136)
        MOT = at("mot", [P, HALF], F32, 200)
        CMB = at("cmb", [P, 2, P], BF16, 202)
        CMF = at("cmf", [P, 1, P], F32, 203)
        O2 = at("o2", [P, KT, T], F32, 172)
        N2 = [at(f"n2{j}", [P, T], F32, 124 + 4 * j) for j in range(2)]
        ACC2 = at("acc2", [P, T], F32, 132)
        RS2 = at("rs2", [P, T], F32, 136)
        HBH = [at(f"hbh{j}", [P, 2, T], F32R, 124 + 16 * j) for j in range(2)]
        HBL = [at(f"hbl{j}", [P, 2, T], F32R, 132 + 16 * j) for j in range(2)]
        FA = at("fa", [P, KT, T], F32, 156)
        TH = [at(f"th{j}", [P, T], F32, 188 + 4 * j) for j in range(2)]
        HF = [at(f"hf{j}", [P, T], F32, 196 + 4 * j) for j in range(2)]
        PR = at("pr", [P, 2, T], F32, 124)
        PH = at("ph", [P, 2, T], F32R, 132)
        PL = at("pl", [P, 2, T], F32R, 140)
        EB = at("eb", [P, KT, T], F32, 27)
        OB = at("ob", [P, KT, T], F32, 59)
        RS3 = at("rs3", [P, T], F32, 59)
        RS4 = at("rs4", [P, T], F32, 63)
        GH = at("gh", [P, KT, T], F32R, 124)
        GL = at("gl", [P, KT, T], F32R, 156)

        PS = [ctx.enter_context(nc.psum_tensor(f"ps{n}", [P, 2, HALF], F32)) for n in "abcd"]
        A, B, C, Dp = range(4)

        s_q = {n: sem(f"s_{n}") for n in ("sp", "act", "pool", "pe", "dve")}
        s_raw = [sem(f"s_raw{j}") for j in range(2)]
        s_split = sem("s_split")
        s_used = sem("s_used")
        s_out = sem("s_out")
        s_q["used"] = s_used
        pr = Program({n: Queue(n, s_q[n]) for n in s_q})
        do = pr.do

        def act(fn, *w, **k):
            return do("act", fn, *w, **k)

        def dve(fn, *w, **k):
            return do("dve", fn, *w, **k)

        def pe(fn, *w, **k):
            return do("pe", fn, *w, **k)

        def own(*operands):
            return [pr.last("dve")] if any(callable(x) for x in operands) else []

        def copy_(o, i, *w, scale=1.0):
            return act(lambda e, k: e.activation(r(o, k), r(i, k), ACT.Copy, scale=scale), *w)

        def fun(f, o, i, *w, scale=1.0, bias=0.0, acc=None):
            if acc is None:
                return act(lambda e, k: e.activation(r(o, k), r(i, k), f, scale=scale, bias=bias), *w)
            return act(lambda e, k: e.activation(r(o, k), r(i, k), f, scale=scale, bias=bias, accum_out=acc), *w)

        def tt(o, a, b, op, *w, q="dve"):
            return do(q, lambda e, k: e.tensor_tensor(r(o, k), r(a, k), r(b, k), op), *w,
                      *(own(o, a, b) if q == "dve" else []))

        def ts(o, a, s1, op0, *w, s2=None, op1=None, q="dve"):
            if op1 is None:
                return do(q, lambda e, k: e.tensor_scalar(r(o, k), r(a, k), s1, None, op0), *w, *own(o, a))
            return do(q, lambda e, k: e.tensor_scalar(r(o, k), r(a, k), s1, s2, op0, op1), *w)

        def stt(o, a, s, b, op0, op1, *w):
            return dve(lambda e, k: e.scalar_tensor_tensor(out=r(o, k), in0=r(a, k), scalar=s, in1=r(b, k),
                                                           op0=op0, op1=op1), *w, *own(o, a, b))

        def vcopy(o, i, *w):
            return ts(o, i, 1.0, MUL, *w)

        def dcopy(o, i, *w):
            return dve(lambda e, k: e.tensor_copy(r(o, k), r(i, k)), *w)

        def recip(o, i, *w):
            return dve(lambda e, k: e.reciprocal(r(o, k), r(i, k)), *w)

        def mm(o, l, rh, st, sp, *w, **kw):
            return pe(lambda e, k: e.matmul(r(o, k), lhsT=r(l, k), rhs=r(rh, k), start=st, stop=sp,
                                            skip_group_check=True), *w, **kw)

        def tr(o, i, ident, *w, **kw):
            return pe(lambda e, k: e.transpose(r(o, k), r(i, k), ident), *w, **kw)

        def r(x, k):
            return x(k) if callable(x) else x

        loads = [0]

        def load(q, dst, src, *w):
            loads[0] += 1
            s = sem(f"s_load{loads[0]}")
            do(q, lambda e, k: e.dma_start(dst, src), *w, inc=[(s, 16)], mark=False)
            return At(s, 16)

        def col(name, j=0, lo=0, hi=P):
            return COLS[lo:hi, COL[name] + j:COL[name] + j + 1]

        MUL, ADD, SUB, MAX = ALU.mult, ALU.add, ALU.subtract, ALU.max

        def slab_in(s, step, *w):
            j = s % 2
            free = [] if s < 2 else [At(s_split, s - 1, step)]
            do("sp", lambda e, k: e.dma_start(RAW[:, j, :], slabs[s + (k * step if step else 0)]),
               *free, *w, inc=[(s_raw[j], 16)], mark=False)

        def slab_split(s, step):
            j = s % 2
            free = [] if s < 2 else [At(s_used, s - 1, step)]
            if s == 0:
                do("pool", lambda e, k: e.memset(ONE[:, :], 1.0))
            h = do("pool", lambda e, k: e.tensor_tensor(WH[j][:, :], RAW[:, j, :], ONE[:, 0:1].to_broadcast([P, 1024]), MUL),
                   At(s_raw[j], 16 * (s // 2 + 1), 16 * step // 2), *free, At(s_q["pool"], 1))
            do("pool", lambda e, k: e.tensor_tensor(WL[j][:, :], RAW[:, j, :], WH[j][:, :], SUB), h,
               inc=[(s_split, 1)], mark=False)

        def feed(fn, a, b):
            if b > a:
                pr.begin((b - a) // 2)
                fn(a, 2)
                fn(a + 1, 2)
                pr.end()

        done_split = [0]

        def split_to(b):
            if done_split[0] == 0:
                slab_split(0, 0)
                slab_split(1, 0)
                done_split[0] = 2
            feed(slab_split, done_split[0], b)
            done_split[0] = b

        def project(s, step, blocks, xh, xl, outs, *w, xw=None, m=P, last=True, start=True, stop=True):
            j = s % 2
            n = 0
            total = 3 * len(blocks)
            tok = None
            for bi, (blk, kt) in enumerate(blocks):
                wh, wl = WH[j][:, blk * P:blk * P + m], WL[j][:, blk * P:blk * P + m]
                for pas, (lw, xx) in enumerate(((wh, xh), (wh, xl), (wl, xh))):
                    for oi, (o, c0, cn) in enumerate(outs):
                        ws = []
                        if n == 0 and oi == 0:
                            ws += [At(s_split, s + 1, step), *w]
                        if pas < 2 and oi == 0 and xw is not None:
                            ws.append(xw[pas][kt])
                        end = n == total - 1 and oi == len(outs) - 1
                        tok = mm(o, lw, xx(kt, c0, cn), start and n == 0, stop and n == total - 1, *ws,
                                 mark=end, counter="used" if last else None)
                    n += 1
            return tok

        def halves(p):
            return [(PS[p][:, 0, :], 0, HALF), (PS[p][:, 1, :], HALF, HALF)]

        def both(p):
            return PS[p][:, :, :].rearrange("p a b -> p (a b)")

        ps = [Slot() for _ in range(4)]

        def loop(n, slots, body):
            pr.begin(n)
            for x in slots:
                x.enter()
            body()
            for x in slots:
                x.leave()
            pr.end()

        def sums(tile, pair, w, meta=None, square=None):
            sq = SQC[:, 1, :] if square is None else square
            o = halves(pair)
            t = mm(o[0][0], sq, tile[:, 0:HALF], True, True, w, *ps[pair].waits(), mark=False)
            t = mm(o[1][0], sq, tile[:, HALF:T], True, True)
            if meta is not None:
                t = mm(PS[meta][:, 0, 0:META], sq, tile[:, T:L], True, True, *ps[meta].waits())
            return t

        def rstd(rs, pair, n, *w, meta=None):
            a = fun(ACT.Sqrt, rs[:, 0:T], both(pair), *w, scale=1.0 / n, bias=col("eps"))
            if meta is not None:
                a = fun(ACT.Sqrt, rs[:, T:L], PS[meta][:, 0, 0:META], *w, scale=1.0 / n, bias=col("eps"))
                ps[meta].free = a
            ps[pair].free = a
            return recip(rs[:, 0:L if meta is not None else T], rs[:, 0:L if meta is not None else T], a)

        def split_tile(hi, lo, src, tmp, w):
            h = copy_(hi, src, w)
            return h, tt(lo, src, hi, SUB, h)

        w_cols = load("sp", COLS[:, :], cols)
        w_x = [load("sp", X[:, kt, :], xT[kt]) for kt in range(KT)]
        w_sq = load("act", SQC[:, :, :], squares[0:4].rearrange("n p c -> p n c"))
        w_cs = load("act", COS1[:, :], rope1[0])
        w_sn = load("act", SIN1[:, :], rope1[1])
        slab_in(0, 0)
        slab_in(1, 0)
        feed(slab_in, 2, NSLAB)
        split_to(S_OUT1)

        def squares_to_psum(tiles, waits, tmp, pair, meta, width):
            n = len(tiles)
            free = [None, None]
            for j in range(n):
                a = fun(ACT.Square, tmp[j % 2][:, 0:width], tiles[j], waits[j], free[j % 2])
                o = halves(pair)
                first, last = j == 0, j == n - 1
                mm(o[0][0], SQC[:, 1, :], tmp[j % 2][:, 0:HALF], first, last, a,
                   *(ps[pair].waits() + [w_sq] if first else []), mark=False)
                t = mm(o[1][0], SQC[:, 1, :], tmp[j % 2][:, HALF:T], first, last)
                if meta is not None:
                    t = mm(PS[meta][:, 0, 0:META], SQC[:, 1, :], tmp[j % 2][:, T:L], first, last,
                           *(ps[meta].waits() if first else []))
                free[j % 2] = t
            return t

        t = squares_to_psum([X[:, kt, :] for kt in range(KT)], w_x, TMP, C, Dp, L)
        t_rs = rstd(RS, C, D, t, w_cols, meta=Dp)
        xw = ([None] * KT, [None] * KT)
        free = [None, None]
        for kt in range(KT):
            n_ = stt(TMP[2 + kt % 2][:, :], X[:, kt, :], col("norm_g", kt), RS[:, :], MUL, MUL, t_rs, w_cols,
                     free[kt % 2])
            xw[0][kt] = copy_(XH[:, kt, :], TMP[2 + kt % 2][:, :], n_)
            free[kt % 2] = xw[1][kt] = tt(XL[:, kt, :], TMP[2 + kt % 2][:, :], XH[:, kt, :], SUB, xw[0][kt])

        def xh(kt, c, n):
            return XH[:, kt, c:c + n]

        def xl(kt, c, n):
            return XL[:, kt, c:c + n]

        full = [(kt, kt) for kt in range(KT)]

        pair_meta = [(A, C), (B, Dp)]
        ft_zero = dve(lambda e, k: e.memset(FT[:, :, L:L + 2], 0.0), xw[1][KT - 1])

        def f_in():
            for j in range(2):
                p, m = pair_meta[j]
                t = project(S_IN1 + j, 2, full, xh, xl, halves(p) + [(PS[m][:, 0, 0:META], T, META)],
                            *ps[p].waits(), *ps[m].waits(), xw=xw)
                a = vcopy(lambda k, j=j: FT[:, k * 2 + j, META:L], both(p), t)
                a = vcopy(lambda k, j=j: FT[:, k * 2 + j, 0:META], PS[m][:, 0, 0:META], t)
                ps[p].free = ps[m].free = a

        loop(2, ps, f_in)
        ft_done = ps[B].free

        raw, sqt, t1, rsk, t2 = TMP
        S_raw, S_sq, S_t1, S_rs, S_t2 = (Slot() for _ in range(5))
        kq_slots = [S_raw, S_sq, S_t1, S_rs, S_t2]
        for x in kq_slots:
            x.free = xw[1][KT - 1]

        def turn(t, p, pm, meta, g, width):
            a = copy_(raw[:, 0:T], both(p), t, *S_raw.waits())
            ps[p].free = a
            if meta:
                a = copy_(raw[:, T:L], pm, t)
            b = fun(ACT.Square, sqt[:, 0:width], raw[:, 0:width], a, *S_sq.waits())
            stt(t1[:, 0:width], raw[:, 0:width], col(g), COS1[:, 0:width], MUL, MUL, a, w_cs, w_sn, *S_t1.waits())
            for q4 in range(4):
                lo, src = 32 * q4, 32 * (q4 ^ 1)
                v = stt(t2[lo:lo + 32, 0:width], raw[src:src + 32, 0:width], col(g, 0, src, src + 32),
                        SIN1[src:src + 32, 0:width], MUL, MUL, *(S_t2.waits() if q4 == 0 else []))
            S_raw.free = v
            v = tt(t1[:, 0:width], t1[:, 0:width], t2[:, 0:width], ADD, v)
            S_t2.free = v
            return a, b, v

        def norm_heads(b, v, pair, meta, out, width):
            s = sums(sqt, pair, b, meta=meta, square=SQC[:, 2, :])
            S_sq.free = s
            x = rstd(rsk, pair, HD, s, *S_rs.waits(), meta=meta)
            x = tt(out, t1[:, 0:width], rsk[:, 0:width], MUL, x, v)
            S_rs.free = S_t1.free = x
            return x

        t = project(S_IN1 + 4, 0, full, xh, xl, halves(A) + [(PS[C][:, 0, 0:META], T, META)],
                    *ps[A].waits(), *ps[C].waits(), xw=xw)
        a, b_, v_ = turn(t, A, PS[C][:, 0, 0:META], True, "k_g", L)
        ps[C].free = a
        t = project(S_IN1 + 5, 0, full, xh, xl, halves(B) + [(PS[Dp][:, 1, 0:META], T, META)],
                    *ps[B].waits(), *ps[Dp].waits())
        t_v = copy_(V1[:, 0:T], both(B), t)
        t_v = copy_(V1[:, T:L], PS[Dp][:, 1, 0:META], t)
        ps[B].free = ps[Dp].free = t_v
        t_k = norm_heads(b_, v_, C, Dp, K1[:, :], L)

        def q_tiles():
            t = project(S_IN1 + 6, 2, full, xh, xl, halves(A), *ps[A].waits())
            _, b0, v0 = turn(t, A, None, False, "q_g", T)
            t = project(S_IN1 + 7, 2, full, xh, xl, halves(B), *ps[B].waits())
            norm_heads(b0, v0, C, None, lambda k: Q1[:, k * 2, :], T)
            _, b1, v1 = turn(t, B, None, False, "q_g", T)
            norm_heads(b1, v1, Dp, None, lambda k: Q1[:, k * 2 + 1, :], T)

        loop(2, ps + kq_slots, q_tiles)
        t_q = S_t1.free

        S_th = [Slot(t_q), Slot(t_q)]

        def gates():
            for j in range(2):
                p = (A, B)[j]
                t = project(S_IN1 + 10 + j, 2, full, xh, xl, halves(p), *ps[p].waits())
                a = fun(ACT.Tanh, TMP[j][:, 0:T], both(p), t, *S_th[j].waits(), scale=0.5)
                g = stt(lambda k, j=j: GT[:, k * 2 + j, :], TMP[j][:, 0:T], 1.0, both(p), ADD, MUL, a)
                S_th[j].free = ps[p].free = g

        loop(4, ps + S_th, gates)
        t_gates = ps[B].free
        split_to(S_OUT1 + 2)

        w_ct = load("act", CT[:, :, :], dft[0].rearrange("(m p) n -> p m n", p=P), t_gates)
        w_st = load("act", ST[:, :, :], dft[1].rearrange("(m p) n -> p m n", p=P))
        w_wf = load("act", WF[:, :], wf)
        w_cd = load("act", CD[:, :, :], cd.rearrange("a p c -> p a c"))
        f1 = tt(FE[:, :, 0:NM], FT[:, :, 0:NM], FT[:, :, L:L - NM:-1], ADD, t_gates, ft_done, ft_zero)
        f2 = tt(FO[:, :, 0:NM], FT[:, :, 0:NM], FT[:, :, L:L - NM:-1], SUB)
        z = dve(lambda e, k: e.memset(WBD[:, :, :, :], 0.0), f1)
        for a in range(2):
            t = mm(PS[A][:, a, :], CD[:, a, :], WF[:, :], True, True, *ps[A].waits(), w_wf, w_cd)
        for a in range(2):
            for h in range(2):
                rows = slice(64 * h, 64 * h + 64)
                c = dcopy(WBD[rows, a, :, 64 * h:64 * h + 64],
                          PS[A][rows, a, :].rearrange("p (j two c) -> p j two c", two=2, c=64)[:, :, h, :], t, z)
        ps[A].free = c
        w_g = c
        for mt in range(MT5):
            w = min(P, NM - mt * P)
            p = (A, B, C, Dp)[mt % 4]
            for a, F_ in enumerate((FE, FO)):
                for ct in range(4):
                    t = mm(PS[p][0:w, a, ct * P:ct * P + P], F_[:, ct, mt * P:mt * P + w], WBD[:, a, ct, :],
                           True, True, w_g, f2, *ps[p].waits(), mark=(a == 1 and ct == 3))
            ga = copy_(GA[0:w, mt, :], PS[p][0:w, 0, :], t)
            gb = copy_(GB[0:w, mt, :], PS[p][0:w, 1, :], t)
            ps[p].free = gb
        S_q, S_p = Slot(), Slot()
        n = 0
        for dt in range(4):
            for h in range(2):
                p = (A, B, C, Dp)[(MT5 + n) % 4]
                n += 1
                c0, cn = h * (NL // 2), NL // 2
                for a, (G_, TB) in enumerate(((GA, CT), (GB, ST))):
                    for mt in range(MT5):
                        w = min(P, NM - mt * P)
                        t = mm(PS[p][:, a, 0:cn], G_[0:w, mt, dt * P:dt * P + P], TB[0:w, mt, c0:c0 + cn],
                               mt == 0, mt == MT5 - 1, gb, w_ct, w_st, *ps[p].waits(),
                               mark=(a == 1 and mt == MT5 - 1))
                q_ = copy_(QSB[:, 0:cn], PS[p][:, 1, 0:cn], t, *S_q.waits())
                k0 = META - 1 if h == 0 else 0
                k1 = cn if h == 0 else cn - 1
                x = stt(PSB[:, 0:cn], PS[p][:, 0, 0:cn], col("b_fmix", dt), QSB[:, 0:cn], ADD, SUB, q_, S_p.free)
                r0 = c0 + 1 + k0 - META
                seg = GT[:, dt, r0:r0 + cn - k0]
                x = stt(seg, PSB[:, k0:cn], 0.5, seg, MUL, MUL, x)
                y = stt(PSB[:, cn:2 * cn], PS[p][:, 0, 0:cn], col("b_fmix", dt), QSB[:, 0:cn], ADD, ADD)
                S_q.free = ps[p].free = y
                hi_, lo_ = T - (c0 + 1), T - (c0 + k1)
                seg = GT[:, dt, lo_:hi_ + 1]
                S_p.free = stt(seg, PSB[:, cn + k1 - 1:cn - 1:-1] if cn > 0 else None, 0.5, seg, MUL, MUL, y)
        t_four = S_p.free

        for kv in range(2):
            mine, rest = slice(64 * kv, 64 * kv + 64), slice(64 - 64 * kv, 128 - 64 * kv)
            a = copy_(KHH[kv][mine, :], K1[mine, :], t_four, t_k)
            t_kh = copy_(KHH[kv][rest, :], K1[mine, :])
            tt(KLL[kv][mine, :], K1[mine, :], KHH[kv][mine, :], SUB, a)
            t_kl = tt(KLL[kv][rest, :], K1[mine, :], KHH[kv][mine, :], SUB)
        for kt in range(8):
            t = tr(PS[C][:, kt // 4, (kt % 4) * P:(kt % 4) * P + P], V1[:, kt * P:kt * P + P], SQC[:, 0, :],
                   *ps[C].waits(), t_v, mark=kt == 7)
        t = tr(PS[Dp][0:META, 0, 0:P], V1[:, T:L], SQC[:, 0, :], *ps[Dp].waits())
        src = [PS[C][:, :, :].rearrange("p a (k c) -> p (a k) c", c=P)[:, :, 64 * kv:64 * kv + 64] for kv in range(2)]
        srm = [PS[Dp][0:META, 0, 64 * kv:64 * kv + 64] for kv in range(2)]
        for kv in range(2):
            copy_(VS1[kv][:, 0:8, 0:64], src[kv], t, t_four)
            a = copy_(VS1[kv][0:META, 8, 0:64], srm[kv])
        for kv in range(2):
            t_vs = tt(VS1[kv][:, 0:8, 64:128], src[kv], VS1[kv][:, 0:8, 0:64], SUB, a)
            t_vs = tt(VS1[kv][0:META, 8, 64:128], srm[kv], VS1[kv][0:META, 8, 0:64], SUB)
        ps[C].free = ps[Dp].free = t_vs

        MXM, NB, RSA, RSM, RI = (TINY[:, 4 * n:4 * n + 4] for n in range(1, 6))
        MXT = TINY[:, 24:32]
        S_qs, S_pm, S_pt, S_ot = ([Slot(), Slot()] for _ in range(4))
        S_pb = [Slot(t_vs) for _ in range(4)]
        S_pmh, S_sm, S_av = Slot(), Slot(t_vs), Slot(t_vs)
        S_smc = [Slot(t_vs), Slot(t_vs)]
        S_tc = [Slot(t_vs), Slot(t_vs)]
        S_sc = [ps[A], ps[B]]
        at_slots = S_qs + S_pb + S_pm + S_pt + [S_pmh, S_sm, S_av] + S_smc + S_tc + S_ot + S_sc
        scale1 = HD ** -0.5
        st = {}

        def stage(s, tile):
            mine, rest = slice(64 * s, 64 * s + 64), slice(64 - 64 * s, 128 - 64 * s)
            a = vcopy(QST[s][mine, :], lambda k: Q1[mine, k + tile, :], *S_qs[s].waits())
            st["q", s] = tt(QST[s][rest, :], lambda k: Q1[mine, k + tile, :], QST[s][mine, :], SUB, a)

        def meta_scores(g):
            s = g // 2
            for v in range(4):
                c0 = (4 * (g % 2) + v) * P
                o = PS[Dp][:, 0, v * META:v * META + META]
                mm(o, QST[s][:, c0:c0 + P], KHH[s][:, T:L], True, False, st["q", s], *S_sm.waits(), mark=False)
                t = mm(o, QST[s][:, c0:c0 + P], KLL[s][:, T:L], False, True, mark=v == 3)
            S_sm.free = st["smc", g] = copy_(SMC[:, g % 2, :], PS[Dp][:, 0, 0:4 * META], t, *S_smc[g % 2].waits())
            st["mt", g] = dve(lambda e, k: e.tensor_reduce(
                MXT[:, 4 * (g % 2):4 * (g % 2) + 4], SMC[:, g % 2, :].rearrange("p (a b) -> p a b", b=META),
                AX.X, MAX), st["smc", g])

        def scores(u):
            s, qt = divmod(u, 8)
            q = QST[s][:, qt * P:qt * P + P]
            for h in range(2):
                c = slice(h * HALF, h * HALF + HALF)
                mm(PS[u % 2][:, h, :], q, KHH[s][:, c], True, False, st["q", s] if qt == 0 else None,
                   *S_sc[u % 2].waits(), t_kl, t_kh, mark=False)
                t = mm(PS[u % 2][:, h, :], q, KLL[s][:, c], False, True, mark=h == 1)
            st["s", u] = t
            if qt == 7:
                S_qs[s].free = t

        def maxima(u):
            v, g = u % 4, u // 4
            m = dve(lambda e, k: e.tensor_reduce(MXM[:, v:v + 1], both(u % 2), AX.X, MAX), *waits_of("s", u),
                    st["mt", g] if v == 0 else None)
            st["nb", u] = ts(NB[:, v:v + 1], MXM[:, v:v + 1], MXT[:, 4 * (g % 2) + v:4 * (g % 2) + v + 1], MAX, m,
                             s2=-scale1, op1=MUL)

        def exps(u):
            v, g = u % 4, (u // 4) % 2
            S_sc[u % 2].free = fun(ACT.Exp, PB[v][:, :], both(u % 2), st["nb", u], *S_pb[v].waits(), scale=scale1,
                                   bias=NB[:, v:v + 1], acc=RSA[:, v:v + 1])
            st["e", u] = S_smc[g].free = fun(
                ACT.Exp, PM[g][:, v, :], SMC[:, g, v * META:v * META + META],
                *(S_pm[g].waits() + [st["smc", u // 4]] if v == 0 else []), scale=scale1, bias=NB[:, v:v + 1],
                acc=RSM[:, v:v + 1])

        def norms(u):
            v, g = u % 4, (u // 4) % 2
            x = tt(RI[:, v:v + 1], RSA[:, v:v + 1], RSM[:, v:v + 1], ADD, *waits_of("e", u))
            x = recip(RI[:, v:v + 1], RI[:, v:v + 1], x)
            tt(PB[v][:, :], PB[v][:, :], RI[:, v:v + 1].to_broadcast([P, T]), MUL, x, q="pool")
            st["p", u] = tt(PM[g][:, v, :], PM[g][:, v, :], RI[:, v:v + 1].to_broadcast([P, META]), MUL, q="pool")

        def turns(u):
            v = u % 4
            for h in range(2):
                for kt in range(4):
                    c = (4 * h + kt) * P
                    t = tr(PS[C][:, h, kt * P:kt * P + P], PB[v][:, c:c + P], SQC[:, 0, :],
                           *(waits_of("p", u) + S_tc[h].waits() if kt == 0 else []), mark=kt == 3)
                st["t", u, h] = t
            S_pb[v].free = t

        def parts(u):
            v, g = u % 4, (u // 4) % 2
            w = S_pt[g].waits() if v == 0 else []
            for h in range(2):
                src = PS[C][:, h, :].rearrange("p (k q) -> p k q", q=P)
                dst = slice(4 * h, 4 * h + 4)
                a = copy_(PTH[g][:, dst, v * P:v * P + P], src, st["t", u, h], *w)
                S_tc[h].free = tt(PTL[g][:, dst, v * P:v * P + P], src, PTH[g][:, dst, v * P:v * P + P],
                                  SUB, a, *w)

        def meta_parts(u):
            g = (u // 4) % 2
            for x in range(4):
                t = tr(PS[C][0:META, 0, x * P:x * P + P], PM[g][:, x, :], SQC[:, 0, :],
                       *(S_tc[0].waits() if x == 0 else []), mark=x == 3)
            S_pm[g].free = t
            a = copy_(PMH[:, :], PS[C][0:META, 0, :], t, *S_pmh.waits())
            st["l", u // 4] = S_tc[0].free = tt(PML[:, :], PS[C][0:META, 0, :], PMH[:, :], SUB, a, *S_pmh.waits())

        def values(g, quarter, tile):
            s = g // 2
            steps = [(kt, hl) for kt in range(9) for hl in range(2)]
            for n in range(5 * quarter, min(5 * quarter + 5, 18)):
                kt, hl = steps[n]
                rows = slice(0, P) if kt < 8 else slice(0, META)
                rh = (PTH, PTL)[hl][g % 2][:, kt, :] if kt < 8 else (PMH, PML)[hl][:, :]
                t = mm(PS[Dp][:, 1, :], VS1[s][rows, kt, :], rh, n == 0, n == 17,
                       *(waits_of("l", g) + S_av.waits() + [t_vs] if n == 0 else []), mark=n == 17)
            if quarter == 3:
                S_pt[g % 2].free = S_pmh.free = st["o", g] = t

        def outputs(g, tile):
            s = g // 2
            t = st["o", g]
            mine, rest = slice(64 * s, 64 * s + 64), slice(64 - 64 * s, 128 - 64 * s)
            a = copy_(OT[g % 2][mine, :], PS[Dp][rest, 1, :], t, *S_ot[g % 2].waits())
            x = tt(OT[g % 2][mine, :], OT[g % 2][mine, :], PS[Dp][mine, 1, :], ADD, a)
            S_av.free = x
            c0 = (g % 2) * HALF
            seg = lambda k: GT[mine, k + tile + 4, c0:c0 + HALF]
            S_ot[g % 2].free = stt(seg, OT[g % 2][mine, :], 0.5, seg, MUL, MUL, x)

        def waits_of(*key):
            x = st[key if len(key) > 1 else key[0]]
            return x.waits() if isinstance(x, Slot) else [x]

        def carried(*keys):
            made = []
            for key in keys:
                made.append((key, Slot(st[key])))
                st[key] = made[-1][1]
            return made

        LAG = 3
        AHEAD = 7

        def step(u, tile, last=False):
            end = 16 if last else 16 + AHEAD
            front, back = u < end, 0 <= u - LAG < (16 if last else end)
            f, b = u % 16, (u - LAG) % 16
            g, quarter = divmod(u - AHEAD, 4)
            if u == AHEAD:
                stage(1, tile)
            if u == 11 and not last:
                stage(0, tile + 1)
            if back:
                turns(b)
            if u + 1 < (16 if last else end + 1):
                scores((u + 1) % 16)
            if g >= 0:
                values(g, quarter, tile)
            if front:
                maxima(f)
            if 0 <= u - 1 < (16 if last else end):
                norms((u - 1) % 16)
            if back:
                parts(b)
            if front:
                exps(f)
            if back and b % 4 == 3:
                meta_parts(b)
            if g >= 0 and quarter == 3:
                outputs(g, tile)
            if f % 4 == 3 and u < (15 if last else end):
                meta_scores((f // 4 + 1) % 4)

        stage(0, 0)
        meta_scores(0)
        scores(0)
        for u in range(AHEAD):
            step(u, 0)
        hand = carried(("p", 4), ("p", 5), ("l", 0), ("e", 6), ("s", AHEAD))

        def attention():
            for u in range(AHEAD, 16 + AHEAD):
                step(u, 0)
            for key, slot in hand:
                slot.free = st[key]

        loop(3, at_slots + [x for _, x in hand], attention)
        for u in range(AHEAD, 16 + AHEAD):
            step(u, 3, last=True)
        t_att = S_ot[1].free
        ps[C].free, ps[Dp].free = S_tc[0].free, S_av.free

        w_h = [load("act", H[:, m, :], xT[m][:, 0:T], t_att if m == 0 else None) for m in range(KT)]

        def mh(kt, c, n):
            return MH[:, kt, c:c + n]

        def ml(kt, c, n):
            return ML[:, kt, c:c + n]

        def split_all(src, w, hi=MH, lo=ML):
            xw = ([None] * KT, [None] * KT)
            for m in range(KT):
                xw[0][m] = copy_(hi[:, m, :], src[:, m, :], w)
                xw[1][m] = tt(lo[:, m, :], src[:, m, :], hi[:, m, :], SUB, xw[0][m])
            return xw

        xw = split_all(GT, t_att)
        z1 = dve(lambda e, k: e.memset(ACC1[:, :], 0.0), t_att)

        w_pos = load("act", PI[:, :], pos.broadcast_to((P, T)), t_att)
        TWO_PI = 2 * np.pi
        C1 = 6.28125
        C2 = float(np.round((TWO_PI - C1) * 2 ** 21) / 2 ** 21)
        C3 = float(np.float32(TWO_PI - C1 - C2))
        MAGIC = float(3 << 22)
        PI_LO = float(np.nextafter(np.float32(np.pi), np.float32(0)))
        last_a = None
        for inv, sgn, CO, SI in (("inv_ret", "sgn_ret", COS2, SIN2), ("inv_mla", "sgn_mla", COS3, SIN3)):
            x = ts(ANG[:, :], PI[:, :], col(inv), MUL, w_pos, last_a)
            x = ts(KR_[:, :], ANG[:, :], 1.0 / TWO_PI, MUL, x, s2=MAGIC, op1=ADD)
            x = ts(KR_[:, :], KR_[:, :], MAGIC, SUB, x)
            for c in (C1, C2, C3):
                x = stt(RED[:, :], KR_[:, :], -c, ANG[:, :] if c == C1 else RED[:, :],
                        MUL, ADD, x)
            x = ts(RED[:, :], RED[:, :], PI_LO, ALU.min, x, s2=-PI_LO, op1=MAX)
            a = fun(ACT.Sin, SI[:, :], RED[:, :], x)
            a = fun(ACT.Abs, ANG[:, :], RED[:, :])
            last_a = fun(ACT.Sin, CO[:, :], ANG[:, :], a, scale=-1.0, bias=col("halfpi"))
            t_tab = ts(SI[:, :], SI[:, :], col(sgn), MUL, last_a)

        S_n = [Slot(), Slot()]
        split_to(S_RET)
        n1 = N1

        def out1():
            for j in range(2):
                p = (A, B)[j]
                t = project(S_OUT1 + j, 2, full, mh, ml, halves(p), *ps[p].waits(), xw=xw)
                hm = lambda k, j=j: H[:, k * 2 + j, :]
                x = tt(hm, hm, both(p), ADD, t, *w_h)
                ps[p].free = x
                a = tt(N1[j][:, :], hm, hm, MUL, x)
                S_n[j].free = st["acc"] = tt(ACC1[:, :], ACC1[:, :], N1[j][:, :], ADD, a)

        loop(4, ps + S_n, out1)

        def norm_sum(acc, pair, rs, n, w):
            t = sums(acc, pair, w)
            return rstd(rs, pair, n, t)

        x = norm_sum(ACC1, C, RS1, D, st["acc"])
        hw = []
        sq = []
        for m in range(KT):
            hw.append(stt(H[:, m, :], H[:, m, :], col("final_g", m), RS1[:, :], MUL, MUL, x))
            a = fun(ACT.Square, N1[m % 2][:, :], H[:, m, :], hw[m], S_n[m % 2].free)
            if m == 0:
                y = dcopy(ACC1[:, :], N1[0][:, :], a)
            else:
                y = tt(ACC1[:, :], ACC1[:, :], N1[m % 2][:, :], ADD, a)
            S_n[m % 2].free = y

        def norm_split(src, g, rs, w, tmp, slots):
            xw = ([None] * KT, [None] * KT)
            for m in range(KT):
                v = stt(tmp[m % 2][:, :], src[:, m, :], col(g, m), rs[:, :], MUL, MUL, w, slots[m % 2].free)
                xw[0][m] = copy_(MH[:, m, :], tmp[m % 2][:, :], v)
                slots[m % 2].free = xw[1][m] = tt(ML[:, m, :], tmp[m % 2][:, :], MH[:, m, :], SUB, xw[0][m])
            return xw

        x = norm_sum(ACC1, Dp, RS1, D, y)
        xw = norm_split(H, "pre_mix", RS1, x, N1, S_n)
        xw_norm2 = xw[1][KT - 1]

        w_rx = load("act", RX[:, :, :], squares[5:13].rearrange("n p c -> p n c"), xw_norm2)
        hs = nc.dram_tensor("residual", (KT, P, T), F32, kind="Internal").ap()
        w_spill = [load("act", hs[m], H[:, m, :], hw[m]) for m in range(KT)]
        (S_rr, S_t, S_rk, S_rq, S_rv, S_kn, S_vn, S_zt) = ret_slots = [Slot(xw_norm2) for _ in range(8)]
        s_ret = S_RET
        ret_scale = CH ** -0.5
        split_to(S_LORA)

        def turn2(p, dst, slot, t, sc):
            a = copy_(RRAW[:, :], both(p), t, *S_rr.waits(), scale=sc)
            ps[p].free = a
            x = tt(RT1[:, :], RRAW[:, :], COS2[:, :], MUL, a, t_tab, *S_t.waits())
            tt(dst[0:64, :], RRAW[64:128, :], SIN2[64:128, :], MUL, *slot.waits())
            y = tt(dst[64:128, :], RRAW[0:64, :], SIN2[0:64, :], MUL)
            S_rr.free = y
            y = tt(dst[:, :], dst[:, :], RT1[:, :], ADD, y)
            S_t.free = y
            return y

        def chunk(x, n):
            return x[:, n * CH:n * CH + CH]

        def retention():
            t = project(s_ret, 4, full, mh, ml, halves(A), *ps[A].waits(), xw=xw)
            k_ = turn2(A, RK, S_rk, t, ret_scale)
            z_ = dcopy(TINY[:, 32:33], lambda k: COLS[:, bass.ds(k + COL["zeta"], 1)], *S_zt.waits())
            z_ = dcopy(TINY[:, 33:34], lambda k: COLS[:, bass.ds(k + COL["gch"], 1)])
            t = project(s_ret + 1, 4, full, mh, ml, halves(B), *ps[B].waits())
            v_ = copy_(RV[:, :], both(B), t, *S_rv.waits())
            ps[B].free = v_
            for n in range(NCH):
                t = tr(PS[C][:, n // 4, (n % 4) * CH:(n % 4) * CH + CH], chunk(RK, n), SQC[:, 0, :], k_,
                       *ps[C].waits(), mark=n == 7)
            kn = ts(RKN[:, :, :].rearrange("p a b -> p (a b)"), both(C), TINY[:, 32:33], MUL, t, z_, *S_kn.waits())
            ps[C].free = kn
            for n in range(NCH):
                t = tr(PS[Dp][:, n // 4, (n % 4) * CH:(n % 4) * CH + CH], chunk(RV, n), SQC[:, 0, :], v_,
                       *ps[Dp].waits(), mark=n == 7)
            S_rv.free = t
            vn = copy_(RVN[:, :, :].rearrange("p a b -> p (a b)"), both(Dp), t, *S_vn.waits())
            ps[Dp].free = vn
            t = project(s_ret + 2, 4, full, mh, ml, halves(A), *ps[A].waits())
            for n in range(NCH - 1):
                u = mm(PS[C][:, n // 4, (n % 4) * CH:(n % 4) * CH + CH], RKN[:, n, :], RVN[:, n, :], True, True, kn, vn,
                       *ps[C].waits(), mark=n == 6)
            S_kn.free = u
            x = dve(lambda e, k: e.memset(chunk(RV, 0), 0.0), u)
            for n in range(NCH - 1):
                x = stt(chunk(RV, n + 1), chunk(RV, n), TINY[:, 33:34],
                        PS[C][:, n // 4, (n % 4) * CH:(n % 4) * CH + CH], MUL, ADD, x)
            ps[C].free = S_zt.free = x
            states = x
            q_ = turn2(A, RQ, S_rq, t, 1.0)
            t = project(s_ret + 3, 4, full, mh, ml, halves(B), *ps[B].waits())
            th = RKN[:, :, :].rearrange("p a b -> p (a b)")
            a = fun(ACT.Tanh, th, both(B), t, u, scale=0.5)
            x = stt(lambda k: GR[:, k, :], th, 1.0, both(B), ADD, MUL, a)
            S_kn.free = x
            ps[B].free = x
            xq = tt(RRAW[:, :].rearrange("p (n c) -> p n c", c=CH), RQ[:, :].rearrange("p (n c) -> p n c", c=CH),
                    lambda k: RX[:, k, :].unsqueeze(1).to_broadcast([P, NCH, CH]), MUL, w_rx, q_)
            for n in range(NCH):
                t = mm(PS[Dp][:, n // 4, (n % 4) * CH:(n % 4) * CH + CH], chunk(RK, n), chunk(RQ, n), True, True, q_,
                       *ps[Dp].waits(), mark=n == 7)
            S_rk.free = S_rq.free = t
            sc = tt(RT1[:, :].rearrange("p (n c) -> p n c", c=CH),
                    PS[Dp][:, :, :].rearrange("p a (n c) -> p (a n) c", c=CH),
                    lambda k: RX[:, k + 4, :].unsqueeze(1).to_broadcast([P, NCH, CH]), MUL, t, q_)
            ps[Dp].free = sc
            for n in range(NCH):
                o = PS[A][:, n // 4, (n % 4) * CH:(n % 4) * CH + CH]
                mm(o, chunk(RV, n), chunk(RRAW, n), True, False, xq, states, *ps[A].waits(), mark=False)
                t = mm(o, RVN[:, n, :], chunk(RT1, n), False, True, sc, mark=n == 7)
            S_rr.free = S_t.free = S_rv.free = S_vn.free = t
            a = vcopy(lambda k: MX[:, k, :], both(A), t)
            ps[A].free = a

        loop(4, ps + ret_slots, retention)
        t_ret = ps[A].free

        split_to(S_MLA)
        S_lt = [Slot(t_ret), Slot(t_ret)]
        lora = []
        xw_mean = SQC[:, 3, :]
        y = sq_ = None
        for n in range(6):
            p = (A, B)[n % 2]
            t = project(S_LORA + n, 0, full, mh, ml, halves(p), *ps[p].waits())
            a = copy_(CQR[:, n, :] if n < 5 else KRR[:, :], both(p), t, t_ret)
            ps[p].free = a
            lora.append(a)
            if 1 <= n < 5:
                m = n - 1
                v = sums(LT[0], Dp, sq_, square=xw_mean)
                S_lt[0].free = v
                y = rstd(LT[1], Dp, 1, v, S_lt[1].free)
                y = stt(MX[:, m, :], MX[:, m, :], col("ret_gn", m), LT[1][:, :], MUL, MUL, y)
                S_lt[1].free = y
                y = stt(MX[:, m, :], MX[:, m, :], 0.5, GR[:, m, :], MUL, MUL, y)
            if n < 4:
                v = sums(MX[:, n, :], C, t_ret, square=xw_mean)
                x = tt(MX[:, n, :], MX[:, n, :], both(C), SUB, v)
                ps[C].free = x
                sq_ = fun(ACT.Square, LT[0][:, :], MX[:, n, :], x, S_lt[0].free)
        t_gn = y
        t_lora = t

        cw = ([None] * 5, [None] * 5)
        free = [S_lt[0].free, t_gn]
        for name, lo, cnt, pair, rs in (("mla_q", 0, 3, C, LP[0]), ("mla_kv", 3, 2, Dp, LP[1])):
            for j in range(cnt):
                b = j % 2
                a = fun(ACT.Square, LT[b][:, :], CQR[:, lo + j, :], free[b], t_gn)
                mm(PS[pair][:, 0, :], SQC[:, 1, :], LT[b][:, 0:HALF], j == 0, j == cnt - 1, a, *ps[pair].waits(),
                   mark=False)
                free[b] = mm(PS[pair][:, 1, :], SQC[:, 1, :], LT[b][:, HALF:T], j == 0, j == cnt - 1)
            x = rstd(rs, pair, cnt * P, free[(cnt - 1) % 2])
            for j in range(cnt):
                b = j % 2
                v = stt(LT[b][:, :], CQR[:, lo + j, :], col(name, j), rs[:, :], MUL, MUL, x, free[b])
                cw[0][lo + j] = copy_(CNH[:, lo + j, :], LT[b][:, :], v, t_lora)
                free[b] = cw[1][lo + j] = tt(CNL[:, lo + j, :], LT[b][:, :], CNH[:, lo + j, :], SUB, cw[0][lo + j])
        cn_done = free[0], free[1]
        tt(KRR[64:96, :], KRR[64:96, :], COS3[64:96, :], MUL, lora[5], t_tab)
        x = tt(LT[0][64:96, :], KRR[96:128, :], SIN3[96:128, :], MUL, *cn_done)
        x = tt(KRR[64:96, :], KRR[64:96, :], LT[0][64:96, :], ADD, x)
        for j in range(2):
            a = copy_(QKS[j][2][64:96, :], KRR[64:96, :], x, t_lora, *w_spill)
            t_kr = tt(QKS[j][3][64:96, :], KRR[64:96, :], QKS[j][2][64:96, :], SUB, a)
        cm = load("act", CMF[:, :, :], squares[4:5].rearrange("n p c -> p n c"), t_kr)
        c1 = dcopy(CMB[:, 0, :], CMF[:, 0, :], cm)
        t_cmb = dcopy(CMB[:, 1, :], SQC[:, 0, :], c1)

        def cnh(kt, c, n):
            return CNH[:, kt, c:c + n]

        def cnl(kt, c, n):
            return CNL[:, kt, c:c + n]

        S_set, S_v2 = [Slot(t_kr), Slot(t_kr)], [Slot(t_kr), Slot(t_kr)]
        ready = [Slot(), Slot()]
        S_mq, S_mkv, S_mt = Slot(t_kr), Slot(t_kr), Slot(t_kr)
        LPB = LPS + [LP[u % 3] for u in range(3, 8)]
        S_lps, S_lp = [Slot(t_kr) for _ in range(3)], [Slot(t_kr) for _ in range(3)]
        S_lpb = S_lps + [S_lp[u % 3] for u in range(3, 8)]
        S_ptl, S_mot = Slot(t_kr), Slot()
        S_av = Slot(ps[Dp].free)
        S_tc = [Slot(ps[C].free), Slot(ps[C].free)]
        ml_slots = ready + S_set + S_v2 + [S_mq, S_mkv, S_mt] + S_lps + S_lp + [S_ptl, S_mot, S_av] + S_tc + [ps[A], ps[B]]
        scale2 = MQK ** -0.5
        st = {}

        def mla_project(h, step, j):
            s = S_MLA + h
            project(s, step, [(0, 0), (1, 1), (2, 2)], cnh, cnl, halves(A), *ps[A].waits(), xw=cw, last=False)
            t = project(s, step, [(3, 3), (4, 4)], cnh, cnl, halves(B), *ps[B].waits(), xw=cw)
            st["mq"] = ps[A].free = copy_(MQ[:, :], both(A), t, *S_mq.waits())
            st["kv"] = ps[B].free = copy_(MKV[:, :], both(B), t, *S_mkv.waits())

        def query_sines():
            st["qs"] = tt(MT1[64:96, :], MQ[96:128, :], SIN3[96:128, :], MUL, st["mq"], *S_mt.waits())

        def query_cosines():
            st["qc"] = tt(MQ[64:96, :], MQ[64:96, :], COS3[64:96, :], MUL, st["mq"])

        def query_turned():
            st["mq"] = S_mt.free = tt(MQ[64:96, :], MQ[64:96, :], MT1[64:96, :], ADD, st["qs"], st["qc"])

        def key_parts(j):
            a = copy_(QKS[j][2][0:64, :], MKV[0:64, :], st["kv"], *S_set[j].waits())
            st["kl"] = tt(QKS[j][3][0:64, :], MKV[0:64, :], QKS[j][2][0:64, :], SUB, a)
            S_mkv.free = st["kl"]

        def query_parts(j):
            a = copy_(QKS[j][0][0:MQK, :], MQ[0:MQK, :], st["mq"], *S_set[j].waits())
            ready[j].free = S_mq.free = tt(QKS[j][1][0:MQK, :], MQ[0:MQK, :], QKS[j][0][0:MQK, :], SUB, a, st["kl"])

        def mla_values(j):
            for kt in range(8):
                t = tr(PS[C][:, kt // 4, (kt % 4) * P:(kt % 4) * P + P], MKV[:, kt * P:kt * P + P], SQC[:, 0, :],
                       st["kv"], *S_tc[0].waits(), *S_tc[1].waits(), mark=kt == 7)
            v = PS[C][:, :, :].rearrange("p a (k c) -> p (a k) c", c=P)[:, :, 64:128]
            a = copy_(VS2[j][:, :, 0:64], v, t, *S_v2[j].waits())
            S_tc[0].free = S_tc[1].free = tt(VS2[j][:, :, 64:128], v, VS2[j][:, :, 0:64], SUB, a)

        def scores(j, u):
            QH, QL, KH, KL = QKS[j]
            p = ps[u % 2]
            q0 = u * P
            n = q0 + P
            for h in range((n + HALF - 1) // HALF):
                c = slice(h * HALF, min(n, h * HALF + HALF))
                o = PS[u % 2][:, h, 0:c.stop - c.start]
                diag = c.start <= q0 < c.stop
                mm(o, QH[0:MQK, q0:q0 + P], KH[0:MQK, c], True, False, *ready[j].waits(), *p.waits(), mark=False)
                mm(o, QH[0:MQK, q0:q0 + P], KL[0:MQK, c], False, False, mark=False)
                t = mm(o, QL[0:MQK, q0:q0 + P], KH[0:MQK, c], False, not diag, mark=not diag)
                if diag:
                    t = mm(PS[u % 2][:, h, q0 - c.start:q0 - c.start + P], CMB[:, 1, :], CMB[:, 0, :], False, True,
                           t_cmb)
            st["s", j, u] = t

        def maxima(j, u):
            v, n = u % 4, u * P + P
            m = dve(lambda e, k: e.tensor_reduce(MXM[:, v:v + 1], both(u % 2)[:, 0:n], AX.X, MAX),
                    *waits_of("s", j, u))
            st["nb", u] = ts(NB[:, v:v + 1], MXM[:, v:v + 1], -scale2, MUL, m)

        def exps(j, u):
            v, n = u % 4, u * P + P
            st["e", j, u] = ps[u % 2].free = fun(ACT.Exp, LPB[u][:, 0:n], both(u % 2)[:, 0:n], st["nb", u],
                                              *S_lpb[u].waits(), scale=scale2, bias=NB[:, v:v + 1],
                                              acc=RSA[:, v:v + 1])

        def norms(j, u):
            v, n = u % 4, u * P + P
            x = recip(RI[:, v:v + 1], RSA[:, v:v + 1], *waits_of("e", j, u))
            st["p", j, u] = tt(LPB[u][:, 0:n], LPB[u][:, 0:n], RI[:, v:v + 1].to_broadcast([P, n]), MUL, x,
                               q="pool")

        def turns(j, u):
            for kt in range(u + 1):
                h = kt // 4
                last = kt == u or kt % 4 == 3
                t = tr(PS[C][:, h, (kt % 4) * P:(kt % 4) * P + P], LPB[u][:, kt * P:kt * P + P], SQC[:, 0, :],
                       *(waits_of("p", j, u) + S_tc[h].waits() if kt % 4 == 0 else []), mark=last)
                st["t", u, h] = t
            S_lpb[u].free = t

        def parts(j, u):
            v = u % 4
            w = S_ptl.waits() if v == 0 else []
            for h in range((u + 4) // 4):
                k0, k1 = 4 * h, min(4 * h + 4, u + 1)
                src = PS[C][:, h, 0:(k1 - k0) * P].rearrange("p (k q) -> p k q", q=P)
                a = copy_(LTH[:, k0:k1, v * P:v * P + P], src, st["t", u, h], *w)
                S_tc[h].free = tt(LTL[:, k0:k1, v * P:v * P + P], src, LTH[:, k0:k1, v * P:v * P + P], SUB, a, *w)
                st["l", u] = S_tc[h].free

        def values(j, u):
            g = u // 4
            nk = 4 * g + 4
            for kt in range(nk):
                c0 = max(0, kt - 4 * g) * P
                for hl, Pt in enumerate((LTH, LTL)):
                    last = kt == nk - 1 and hl == 1
                    t = mm(PS[Dp][:, 1, c0:HALF], VS2[j][:, kt, :], Pt[:, kt, c0:HALF], kt == 0 and hl == 0, last,
                           st["l", u], *ready[j].waits(), *S_av.waits(), mark=last)
            S_ptl.free = st["o", u] = t
            if g == 1:
                S_v2[j].free = S_set[j].free = t

        def outputs(j, u, tile):
            g = u // 4
            mine, rest = slice(64 * j, 64 * j + 64), slice(64 - 64 * j, 128 - 64 * j)
            a = copy_(MOT[mine, :], PS[Dp][rest, 1, :], st["o", u], *S_mot.waits())
            dst = lambda k: MX[mine, k + tile, g * HALF:g * HALF + HALF]
            S_av.free = S_mot.free = tt(dst, MOT[mine, :], PS[Dp][mine, 1, :], ADD, a, t_gn)

        def step(j, u, tile, nxt=None, last=False):
            front = u < 8 or not last
            jf, f = (j, u) if u < 8 else (1 - j, u - 8)
            b = u - LAG
            if b >= 0:
                turns(j, b)
            project_now = u == 3 and nxt is not None
            if u + 1 < (8 if last else 12) and not project_now:
                scores(jf if u + 1 != 8 else 1 - j, (u + 1) % 8)
            if front:
                maxima(jf, f)
            if 0 <= u - 1 < (8 if last else 11):
                norms(*((j, u - 1) if u - 1 < 8 else (1 - j, u - 9)))
            if b >= 0:
                parts(j, b)
            if front:
                exps(jf, f)
            if b >= 0 and b % 4 == 3:
                values(j, b)
                outputs(j, b, tile)
            if project_now:
                mla_project(*nxt, 1 - j)
                scores(j, u + 1)
                query_sines()
            if u == 4 and nxt is not None:
                mla_values(1 - j)
                query_cosines()
            if u == 5 and nxt is not None:
                key_parts(1 - j)
                query_turned()
            if u == 6 and nxt is not None:
                query_parts(1 - j)

        split_to(S_MLA + 2)
        mla_project(0, 0, 0)
        query_sines()
        mla_values(0)
        query_cosines()
        key_parts(0)
        query_turned()
        query_parts(0)
        scores(0, 0)
        step(0, 0, 4)
        step(0, 1, 4)
        step(0, 2, 4)
        hand = carried(("p", 0, 0), ("p", 0, 1), ("e", 0, 2), ("s", 0, 3))

        def mla_pair():
            slab_split(S_MLA + 2, 2)
            for u in range(LAG, 8 + LAG):
                step(0, u, 4, (1, 2))
            slab_split(S_MLA + 3, 2)
            for u in range(LAG, 8 + LAG):
                step(1, u, 4, (2, 2))
            for key, slot in hand:
                slot.free = st[key]

        loop(3, ml_slots + [x for _, x in hand], mla_pair)
        for u in range(LAG, 8 + LAG):
            step(0, u, 7, (7, 0))
        for u in range(LAG, 8 + LAG):
            step(1, u, 7, last=True)
        done_split[0] = S_OUT2
        t_mla = S_av.free
        ps[C].free, ps[Dp].free = S_tc[1].free, S_av.free

        w_h = [load("act", H[:, m, :], hs[m], t_mla, *w_spill) for m in range(KT)]
        xw = split_all(MX, t_mla)
        z2 = dve(lambda e, k: e.memset(ACC2[:, :], 0.0), t_mla)
        S_n = [Slot(), Slot()]
        split_to(S_FFN)

        def out2():
            for j in range(2):
                p = (A, B)[j]
                t = project(S_OUT2 + j, 2, full, mh, ml, halves(p), *ps[p].waits(), xw=xw)
                b = fun(ACT.Square, N2[j][:, :], both(p), t, z2, *S_n[j].waits())
                a = vcopy(lambda k, j=j: O2[:, k * 2 + j, :], both(p), b)
                ps[p].free = a
                S_n[j].free = st["acc"] = tt(ACC2[:, :], ACC2[:, :], N2[j][:, :], ADD, b)

        loop(4, ps + S_n, out2)
        x = norm_sum(ACC2, C, RS2, D, st["acc"])
        for m in range(KT):
            b = m % 2
            v = stt(O2[:, m, :], O2[:, m, :], col("post_mix", m), RS2[:, :], MUL, MUL, x)
            v = tt(H[:, m, :], H[:, m, :], O2[:, m, :], ADD, v, w_h[m])
            a = fun(ACT.Square, N2[b][:, :], H[:, m, :], v, S_n[b].free)
            y = dcopy(ACC2[:, :], N2[b][:, :], a) if m == 0 else tt(ACC2[:, :], ACC2[:, :], N2[b][:, :], ADD, a)
            S_n[b].free = y
        x = norm_sum(ACC2, Dp, RS2, D, y)
        xw = norm_split(H, "pre_ffn", RS2, x, N2, S_n)

        z3 = dve(lambda e, k: e.memset(FA[:, :, :].rearrange("p a b -> p (a b)"), 0.0), xw[1][KT - 1])
        S_th, S_hf, S_hb = [Slot(z3), Slot(z3)], [Slot(z3), Slot(z3)], [Slot(z3), Slot(z3)]
        hb_ready = [Slot(), Slot()]
        ffn_slots = ps + S_th + S_hf + S_hb + hb_ready
        st = {}

        def gate_up(s, step, b):
            for m in range(2):
                pg, pu = (A, C)[m], (B, Dp)[m]
                t = project(s + 2 * m, step, full, mh, ml, halves(pg), *ps[pg].waits(), xw=xw)
                a = fun(ACT.Tanh, TH[m][:, :], both(pg), t, *S_th[m].waits(), scale=0.5)
                x = stt(TH[m][:, :], TH[m][:, :], 1.0, both(pg), ADD, MUL, a)
                ps[pg].free = x
                t = project(s + 2 * m + 1, step, full, mh, ml, halves(pu), *ps[pu].waits())
                x = stt(HF[m][:, :], TH[m][:, :], 0.5, both(pu), MUL, MUL, t, x, *S_hf[m].waits())
                ps[pu].free = S_th[m].free = x
                a = copy_(HBH[b][:, m, :], HF[m][:, :], x, *(S_hb[b].waits() if m == 0 else []))
                S_hf[m].free = tt(HBL[b][:, m, :], HF[m][:, :], HBH[b][:, m, :], SUB, a,
                                  *(S_hb[b].waits() if m == 0 else []))
            hb_ready[b].free = S_hf[1].free

        def down(s, step, b):
            for m in range(8):
                p = m % 4
                hx = lambda kt, c, n: HBH[b][:, kt, c:c + n]
                lx = lambda kt, c, n: HBL[b][:, kt, c:c + n]
                ws = hb_ready[b].waits() if m == 0 else []
                t = project(s + m // 4, step, [(2 * (m % 4), 0), (2 * (m % 4) + 1, 1)], hx, lx, halves(p),
                            *ps[p].waits(), *ws, last=m % 4 == 3)
                x = tt(FA[:, m, :], FA[:, m, :], both(p), ADD, t)
                ps[p].free = x
            S_hb[b].free = t
            st["fa"] = x

        split_to(S_PLEP)
        gate_up(S_FFN, 0, 0)

        def ffn_pair():
            gate_up(S_FFN + 4, 12, 1)
            down(S_FFN + 8, 12, 0)
            gate_up(S_FFN + 10, 12, 0)
            down(S_FFN + 14, 12, 1)

        loop(5, ffn_slots, ffn_pair)
        down(S_PLEP - 2, 0, 0)
        t_ffn = st["fa"]

        w_p = load("act", PR[:, :, :], pT.rearrange("a p t -> p a t"), t_ffn)
        split_to(NSLAB)
        pw = ([None] * 2, [None] * 2)
        for j in range(2):
            pw[0][j] = copy_(PH[:, j, :], PR[:, j, :], w_p)
            pw[1][j] = tt(PL[:, j, :], PR[:, j, :], PH[:, j, :], SUB, pw[0][j])
        S_n = [Slot(t_ffn), Slot(t_ffn)]

        def add_square(src, b, acc, first, w):
            a = fun(ACT.Square, TH[b][:, :], src, w, S_n[b].free)
            y = dcopy(acc, TH[b][:, :], a) if first else tt(acc, acc, TH[b][:, :], ADD, a)
            S_n[b].free = y
            return y

        for m in range(8):
            p = m % 2
            t = project(S_PLEP + m // 4, 0, [(2 * (m % 4), 0), (2 * (m % 4) + 1, 1)],
                        lambda kt, c, n: PH[:, kt, c:c + n], lambda kt, c, n: PL[:, kt, c:c + n], halves(p),
                        *ps[p].waits(), xw=pw, last=m % 4 == 3)
            a = copy_(EB[:, m, :], both(p), t, t_ffn)
            ps[p].free = a
            y1 = add_square(FA[:, m, :], 0, HF[0][:, :], m == 0, t_ffn)
            y2 = add_square(EB[:, m, :], 1, HF[1][:, :], m == 0, a)
        t_e = t
        x = norm_sum(HF[0], C, RS3, D, y1)
        hw = ([None] * KT, [None] * KT)
        for m in range(KT):
            v = stt(FA[:, m, :], FA[:, m, :], col("post_ffn", m), RS3[:, :], MUL, MUL, x)
            v = tt(H[:, m, :], H[:, m, :], FA[:, m, :], ADD, v)
            hw[0][m] = copy_(GH[:, m, :], H[:, m, :], v, t_e)
            hw[1][m] = tt(GL[:, m, :], H[:, m, :], GH[:, m, :], SUB, hw[0][m], v)
        x = norm_sum(HF[1], Dp, RS4, D, y2)
        hb = ts(TINY[:, 40:48], COLS[:, COL["b_ple"]:COL["b_ple"] + 8], 0.5, MUL)
        e_done = [stt(EB[:, m, :], EB[:, m, :], col("ple_norm", m), RS4[:, :], MUL, MUL, x) for m in range(KT)]
        for m in range(KT):
            p = (A, B, C, Dp)[m % 4]
            t = project(S_PLEG + m, 0, full, lambda kt, c, n: GH[:, kt, c:c + n], lambda kt, c, n: GL[:, kt, c:c + n],
                        halves(p), *ps[p].waits(), xw=hw)
            a = fun(ACT.Tanh, OB[:, m, :], both(p), t, e_done[KT - 1], hb, scale=0.5, bias=TINY[:, 40 + m:41 + m])
            ps[p].free = a
            x = stt(OB[:, m, :], OB[:, m, :], 1.0, EB[:, m, :], ADD, MUL, a, e_done[m], hb)
            x = stt(OB[:, m, :], OB[:, m, :], 0.5, H[:, m, :], MUL, ADD, x)
            do("act", lambda e, k, m=m: e.dma_start(outT[m], OB[:, m, :]), x, inc=[(s_out, 16)], mark=False)
        block = ctx.enter_context(nc.Block())

        @block.sync
        def _(e):
            pr.emit("sp", e)
            e.wait_ge(s_out, 16 * KT)

        @block.scalar
        def _(e):
            pr.emit("act", e)

        @block.gpsimd
        def _(e):
            pr.emit("pool", e)

        @block.tensor
        def _(e):
            pr.emit("pe", e)

        @block.vector
        def _(e):
            pr.emit("dve", e)


def shape_constants():
    sq = np.zeros((13, P, P), np.float64)
    sq[0] = np.eye(P)
    sq[1] = 1.0
    sq[2, :64, :64] = sq[2, 64:, 64:] = 1.0
    sq[3] = 1.0 / P
    j = np.arange(P)
    sq[4] = np.where(j[None, :] > j[:, None], -1e30, 0.0)
    zeta, gch = np.zeros((P, RH)), np.zeros((P, RH))
    for h in range(RH):
        lg = np.log(1.0 - 2.0 ** (-5.0 - h))
        sq[5 + h] = np.exp((j + 1) * lg)[None, :]
        diff = j[None, :] - j[:, None]
        sq[9 + h] = np.where(diff >= 0, np.exp(np.maximum(diff, 0) * lg), 0.0)
        zeta[:, h] = np.exp((CH - 1 - j) * lg)
        gch[:, h] = np.exp(CH * lg)
    n_f = HD // 4
    fr = 1.0 / (10000.0 ** (np.arange(n_f) * 2.0 / (HD // 2)))
    tok = np.arange(T)
    row, cl = tok // 64 - (T // 64) // 2, tok % 64 - 32
    ang = np.concatenate([row[:, None] * fr, cl[:, None] * fr], axis=1)
    ang = np.concatenate([ang, np.zeros((META, HD // 2))], axis=0).T
    rope1 = np.stack([np.tile(np.cos(ang), (4, 1)),
                      np.concatenate([np.sin(ang), -np.sin(ang)] * 2, axis=0)])
    m, l = np.arange(MT5 * P)[:, None], np.arange(1, NL + 1)[None, :]
    dft = np.stack([np.cos(2 * np.pi * ((m * l) % L) / L), np.sin(2 * np.pi * ((m * l) % L) / L)]) / np.sqrt(L * 64.0)
    dft[:, NM:] = 0.0
    dft[:, NL] *= 0.5
    c = np.arange(64)
    cd = np.stack([np.cos(2 * np.pi * c[:, None] * c[None, :] / 64), np.sin(2 * np.pi * c[:, None] * c[None, :] / 64)])
    cd = np.concatenate([cd, cd], axis=2)
    inv_ret = np.tile(1.0 / 10000.0 ** (np.arange(64) / 64.0), 2)
    inv_mla = np.tile(1.0 / 10000.0 ** (np.arange(16) / 16.0), 8)
    half = np.repeat([1.0, -1.0], 64)
    sgn_mla = np.ones(P)
    sgn_mla[96:112] = -1.0
    vec = {"zeta": zeta, "gch": gch, "inv_ret": inv_ret[:, None], "inv_mla": inv_mla[:, None],
           "sgn_ret": half[:, None], "sgn_mla": sgn_mla[:, None], "eps": np.full((P, 1), EPS),
           "halfpi": np.full((P, 1), np.pi / 2)}
    f = np.float32
    return sq.astype(f), rope1.astype(f), dft.astype(f), cd.astype(f), {k: v.astype(f) for k, v in vec.items()}


def slab_layout(w_in, w_out, w_in2, w_uq, w_ukv, w_o, w_gate, w_up, w_down, w_pp, w_pg):
    def tile(w, m):
        k = w.shape[0] // P
        return w[:, m * P:m * P + P].reshape(k, P, P).transpose(1, 0, 2).reshape(P, k * P)

    def pairs(w, k0, m0):
        x = w[k0 * P:k0 * P + 2 * P, m0 * P:m0 * P + 4 * P].reshape(2, P, 4, P)
        return x.transpose(1, 2, 0, 3).reshape(P, 8 * P)

    halves_ = np.concatenate([np.arange(0, HD, 2), np.arange(1, HD, 2)])
    q0 = 2 * FW
    k0 = q0 + 512
    v0 = k0 + 128
    heads = [k + 4 * s for k in range(4) for s in range(2)]
    head_rows = np.concatenate([np.arange(h * HD, h * HD + HD) for h in heads])
    perm_q = np.concatenate([q0 + h * HD + halves_ for h in heads])
    perm_k = np.concatenate([k0 + h * HD + halves_ for h in range(2)])
    order = np.concatenate([np.arange(FW), perm_k, np.arange(v0, v0 + 128), perm_q, np.arange(FW, 2 * FW),
                            v0 + 128 + head_rows])
    w_out = w_out[np.concatenate([np.arange(FW), FW + head_rows])]
    w1 = w_in[:, order]
    out = [tile(w1, m) for m in range(18)] + [tile(w_out, m) for m in range(8)]
    for h in range(RH):
        out += [tile(w_in2, 4 * x + h) for x in (1, 2, 0, 3)]
    out += [tile(w_in2, 16 + n) for n in range(5)]
    kr = w_in2[:, 2048 + 640:]
    sw = np.concatenate([np.arange(16, 32), np.arange(16)])
    out.append(tile(np.concatenate([np.zeros((D, 64), kr.dtype), kr, kr[:, sw]], axis=1), 0))
    for h in range(MH_):
        q = w_uq[:, h * MQK:h * MQK + MQK]
        q = np.concatenate([q, q[:, 64 + sw]], axis=1)
        kv = w_ukv[:, h * 128:h * 128 + 128]
        x = np.concatenate([tile(q, 0), tile(kv, 0)], axis=1)
        out.append(np.concatenate([x, np.zeros((P, 1024 - x.shape[1]), x.dtype)], axis=1))
    out += [tile(w_o, m) for m in range(8)]

    def gu(c):
        return [tile(w, 2 * c + m) for m in range(2) for w in (w_gate, w_up)]

    def dn(c):
        return [pairs(w_down, 2 * c, 0), pairs(w_down, 2 * c, 4)]

    n = DFF // 256
    out += gu(0)
    for c in range(1, n):
        out += gu(c) + dn(c - 1)
    out += dn(n - 1)
    out += [pairs(w_pp, 0, 0), pairs(w_pp, 0, 4)] + [tile(w_pg, m) for m in range(8)]
    return np.ascontiguousarray(np.stack(out))


def kernel(**inputs):
    import concourse.bacc as bacc
    from concourse.bass_utils import run_bass_kernel_spmd as run

    a = {k: np.asarray(v) for k, v in inputs.items()}
    sq, rope1, dft, cd, vec = shape_constants()
    xm = np.concatenate([a["x"][0], a["meta_tokens"]], axis=0)
    xT = np.ascontiguousarray(xm.T.reshape(KT, P, L))
    pT = np.ascontiguousarray(a["p_2"][0, 0].T.reshape(2, P, T))
    slabs = slab_layout(a["w_in"][0], a["w_out"][0], a["w_in_2"][0], a["w_uq_2"][0], a["w_ukv_2"][0], a["w_o_2"][0],
                        a["w_gate_2"][0], a["w_up_2"][0], a["w_down_2"][0], a["w_ple_proj_2"][0],
                        a["w_ple_gate_2"][0])
    assert slabs.shape == (NSLAB, P, 1024)
    halves_ = np.concatenate([np.arange(0, HD, 2), np.arange(1, HD, 2)])
    put = {"norm_g": a["norm_g"], "final_g": a["final_g"], "pre_mix": a["pre_mix_norm_2"],
           "post_mix": a["post_mix_norm_2"], "pre_ffn": a["pre_ffn_norm_2"], "post_ffn": a["post_ffn_norm_2"],
           "ple_norm": a["ple_norm_2"], "b_ple": a["b_ple_gate_2"], "mla_q": a["mla_q_norm_2"],
           "mla_kv": a["mla_kv_norm_2"], "ret_gn": a["ret_gn_w_2"], "b_fmix": a["b_fmix"],
           "q_g": np.tile(a["q_norm_g"][0][halves_], 2), "k_g": np.tile(a["k_norm_g"][0][halves_], 2)}
    cols = np.zeros((P, NCOL), np.float32)
    for n, k in _names:
        cols[:, COL[n]:COL[n] + k] = vec[n] if n in vec else put[n].reshape(k, P).T
    wf = np.ascontiguousarray(a["w_fmix"][0].transpose(1, 0, 2).reshape(64, 512))
    arrays = {"xT": xT, "pT": pT, "pos": np.ascontiguousarray(a["positions_2"]), "slabs": slabs, "cols": cols,
              "squares": sq, "rope1": rope1, "dft": dft, "wf": wf, "cd": cd}
    nc = bacc.Bacc("TRN2", target_bir_lowering=False, num_devices=1)
    args = [nc.dram_tensor(n, v.shape, mybir.dt.from_np(v.dtype), kind="ExternalInput").ap() for n, v in arrays.items()]
    args.append(nc.dram_tensor("outT", (KT, P, T), F32, kind="ExternalOutput").ap())
    two_block_kernel(nc, *args)
    r = run(nc, [arrays], core_ids=[0])
    o = r.results[0]["outT"].reshape(D, T)
    return np.ascontiguousarray(o.T)[None]
```

```python
from contextlib import ExitStack

import numpy as np
import concourse.bass as bass
from concourse import mybir

F32 = mybir.dt.float32
F32R = mybir.dt.float32r
BF16 = mybir.dt.bfloat16
I32 = mybir.dt.int32
ALU = mybir.AluOpType
ACT = mybir.ActivationFunctionType
AX = mybir.AxisListType

P = 128
T = 1024
META = 16
L = T + META
D = 1024
KT = D // P
EPS = 1e-6
HD = 64
FW = 512
NL = L // 2
NM = NL + 1
MT5 = (NM + P - 1) // P
DFF = 2816
CH = 128
NCH = T // CH
RH = 4
MH_ = 8
MQK = 96
HALF = 512

S_IN1 = 0
S_OUT1 = 18
S_RET = S_OUT1 + 8
S_LORA = S_RET + 4 * RH
S_MLA = S_LORA + 6
S_OUT2 = S_MLA + MH_
S_FFN = S_OUT2 + 8
S_PLEP = S_FFN + 6 * (DFF // 256)
S_PLEG = S_PLEP + 2
NSLAB = S_PLEG + 8

_names = [("norm_g", 8), ("final_g", 8), ("pre_mix", 8), ("post_mix", 8), ("pre_ffn", 8), ("post_ffn", 8),
          ("ple_norm", 8), ("b_ple", 8), ("mla_q", 3), ("mla_kv", 2), ("ret_gn", 4), ("b_fmix", 4), ("q_g", 1),
          ("k_g", 1), ("zeta", 4), ("inv_ret", 1), ("inv_mla", 1), ("sgn_ret", 1), ("sgn_mla", 1), ("eps", 1),
          ("halfpi", 1), ("gch", 4)]
COL = {}
NCOL = 0
for _n, _k in _names:
    COL[_n] = NCOL
    NCOL += _k


class Tok:

    def __init__(self, q, off, loop, back=0):
        self.q, self.off, self.loop, self.back = q, off, loop, back

    @property
    def prev(self):
        return Tok(self.q, self.off, self.loop, 1)

    def sem(self):
        return self.q.sem

    def value(self, loop):
        if self.loop is None:
            return self.off, 0
        n = self.loop.incs[self.q]
        if self.loop is loop:
            low = self.off - self.back * n
            assert low > 0, ("wait below one", self.q.name, self.off, n)
            return low, n
        return self.off + (self.loop.n - 1) * n, 0


class Later(Tok):

    def __init__(self):
        self.tok = None

    def sem(self):
        return self.tok.sem()

    def value(self, loop):
        return self.tok.prev.value(loop)


class At:

    def __init__(self, sem, const, step=0):
        self._sem, self.const, self.step = sem, const, step

    def sem(self):
        return self._sem

    def value(self, loop):
        return self.const, (self.step if loop is not None else 0)


class Queue:
    def __init__(self, name, sem):
        self.name, self.sem, self.count, self.ops = name, sem, 0, []


class Loop:
    def __init__(self, n):
        self.n, self.incs, self.bodies = n, {}, {}


class Program:

    def __init__(self, queues):
        self.q = queues
        self.loop = None

    def do(self, name, fn, *waits, inc=(), mark=True, counter=None):
        q = self.q[name]
        c = self.q[counter or name]
        q.ops.append((fn, waits, tuple(inc), c.sem if mark else None))
        if mark:
            c.count += 1
        return Tok(c, c.count, self.loop)

    def last(self, name):
        q = self.q[name]
        return Tok(q, q.count, self.loop)

    def begin(self, n):
        self.loop = Loop(n)
        self.saved = {k: (q.ops, q.count) for k, q in self.q.items()}
        for q in self.q.values():
            q.ops = []

    def end(self):
        for k, q in self.q.items():
            ops, count = self.saved[k]
            self.loop.incs[q] = q.count - count
            if q.ops:
                ops.append((self.loop, q.ops))
            q.count = count + self.loop.n * (q.count - count)
            q.ops = ops
        self.loop = None

    def emit(self, name, eng):
        q = self.q[name]

        def run(ops, loop, i):
            for op in ops:
                if isinstance(op[0], Loop):
                    with eng.Fori(0, op[0].n) as k:
                        run(op[1], op[0], k)
                    continue
                fn, waits, inc, mark = op
                most = {}
                for w in waits:
                    if w is not None:
                        low, step = w.value(loop)
                        s = most.setdefault((id(w.sem()), step), [w.sem(), low])
                        s[1] = max(s[1], low)
                for (_, step), (s, low) in most.items():
                    eng.wait_ge(s, i * step + low if step else low)
                ins = fn(eng, i)
                if mark is not None:
                    ins.then_inc(mark, 1)
                for s, k in inc:
                    ins.then_inc(s, k)
        run(q.ops, None, 0)


class Slot:

    def __init__(self, tok=None):
        self.free = tok
        self.outer = self.later = None

    def waits(self):
        if self.free is not None or self.later is None:
            return [self.free]
        return [self.outer, self.later]

    def enter(self):
        self.outer, self.later, self.free = self.free, Later(), None

    def leave(self):
        if self.free is None:
            self.free = self.outer
        else:
            self.later.tok = self.free
        self.outer = self.later = None


def two_block_kernel(nc, xT, pT, pos, slabs, cols, squares, rope1, dft, wf, cd, outT):
    with ExitStack() as ctx:
        base = 16512
        top = 207 * 1024

        def at(name, shape, dt, kb):
            size = int(np.prod(shape[1:])) * (2 if dt == BF16 else 4)
            assert int(kb * 1024) + size <= top, (name, kb, size)
            return nc.alloc_sbuf_tensor_at(name, shape, dt, offset=base + int(kb * 1024))

        def sem(name):
            return ctx.enter_context(nc.semaphore(name))

        ctx.enter_context(nc.sbuf_tensor("arena", [P, top // 4], F32))

        RAW = at("wraw", [P, 2, 1024], F32, 0)
        WH = [at(f"wh{j}", [P, 1024], F32R, 8 + 4 * j) for j in range(2)]
        WL = [at(f"wl{j}", [P, 1024], F32R, 16 + 4 * j) for j in range(2)]
        COLS = at("cols", [P, NCOL], F32, 24)
        SQC = at("sqc", [P, 4, P], F32, 24.5)
        TINY = at("tiny", [P, 64], F32, 26.5)
        ONE = at("one", [P, 1], F32, 26.75)
        TOK = at("tok", [P, 56], F32, 26.78125)
        GSQ = at("gsq", [P, KT], F32, 24.4375)
        XH = at("xh", [P, KT, L], F32R, 27)
        XL = at("xl", [P, KT, L], F32R, 59.5)
        X = at("x", [P, KT, L], F32, 92)
        FT = at("ft", [P, 4, 1042], F32, 92)
        K1 = at("k1", [P, L], F32, 112.75)
        V1 = at("v1", [P, L], F32, 117)
        Q1 = at("q1", [P, 4, T], F32, 121.25)
        TMP = [at(f"tmp{j}", [P, L], F32, 137.5 + 4.125 * j) for j in range(5)]
        COS1 = at("cos1", [P, L], F32, 158.25)
        SIN1 = at("sin1", [P, L], F32, 162.5)
        GT = at("gt", [P, KT, T], F32, 166.75)
        RS = at("rs", [P, L], F32, 199)
        RBM = at("rbm", [P, P], F32, 204)
        GTH = [at(f"gth{j}", [P, T], F32, (199, 162.5)[j]) for j in range(2)]
        CT = at("ct", [P, MT5, NL], F32, 92)
        ST = at("st", [P, MT5, NL], F32, 102.25)
        FE = at("fe", [P, 4, NM + 1], F32, 137.5)
        FO = at("fo", [P, 4, NM + 1], F32, 146)
        WF = at("wf", [64, 512], F32, 154.5)
        CD = at("cd", [64, 2, P], F32, 156.5)
        WBD = at("wbd", [P, 2, 4, P], F32, 158)
        GA = at("ga", [P, MT5, 512], F32, 27)
        GB = at("gb", [P, MT5, 512], F32, 37)
        QSB = at("qsb", [P, NL], F32, 203.5)
        PSB = at("psb", [P, NL], F32, 162.5)
        PTH = [at(f"pth{j}", [P, 8, HALF], F32R, 27 + 32 * j) for j in range(2)]
        PTL = [at(f"ptl{j}", [P, 8, HALF], F32R, 43 + 32 * j) for j in range(2)]
        PM = [at(f"pm{j}", [P, 4, META], F32, 91 + 0.25 * j) for j in range(2)]
        KHH = [at(f"khh{j}", [P, L], F32R, 137.5 + 8.25 * j) for j in range(2)]
        KLL = [at(f"kll{j}", [P, L], F32R, 141.625 + 8.25 * j) for j in range(2)]
        PMH = at("pmh", [META, HALF], F32R, 108.5)
        PML = at("pml", [META, HALF], F32R, 110.5)
        VS1 = [at(f"vs1{j}", [P, 9, P], F32R, 92 + 4.625 * j) for j in range(2)]
        QST = [at(f"qst{j}", [P, T], F32R, (199, 101.25)[j]) for j in range(2)]
        PB = [at(f"pb{j}", [P, T], F32, (154.75, 158.75, 112.75, 116.75)[j]) for j in range(4)]
        SMC = at("smc", [P, 2, 4 * META], F32, 203)
        OT = [at(f"ot{j}", [P, HALF], F32, 162.75 + 2 * j) for j in range(2)]
        MH = at("mh", [P, KT, T], F32R, 27)
        ML = at("ml", [P, KT, T], F32R, 59)
        H = at("h", [P, KT, T], F32, 92)
        COS2 = at("cos2", [P, T], F32, 124)
        SIN2 = at("sin2", [P, T], F32, 128)
        COS3 = at("cos3", [P, T], F32, 132)
        SIN3 = at("sin3", [P, T], F32, 136)
        PI = at("pi", [P, T], I32, 140)
        ANG = at("ang", [P, T], F32, 144)
        KR_ = at("kround", [P, T], F32, 148)
        RED = at("red", [P, T], F32, 152)
        N1 = [at(f"n1{j}", [P, T], F32, 199 + 4 * j) for j in range(2)]
        ACC1 = at("acc1", [P, T], F32, 156)
        ACC2 = at("acc2", [P, T], F32, 164)
        RS1 = at("rs1", [P, T], F32, 160)
        MX = at("mx", [P, KT, T], F32, 140)
        GR = at("gr", [P, 4, T], F32, 156)
        RRAW = at("rraw", [P, T], F32, 172)
        RT1 = at("rt1", [P, T], F32, 176)
        RK = at("rk", [P, T], F32, 180)
        RQ = at("rq", [P, T], F32, 184)
        RV = at("rv", [P, T], F32, 188)
        RKN = at("rkn", [P, NCH, CH], F32, 192)
        RVN = at("rvn", [P, NCH, CH], F32, 196)
        RTH = at("rth", [P, T], F32, 120)
        RX = at("rx", [P, 8, P], F32, 200)
        PI2 = at("pi2", [P, T], I32, 116)
        TAB = [at(f"tab{j}", [P, T], F32, 120 + 4 * j) for j in range(3)]
        LSQ = [at(f"lsq{j}", [P, T], F32, 92 + 4 * j) for j in range(5)]
        LL = [at(f"ll{j}", [P, T], F32, 112 + 4 * j) for j in range(2)]
        CQR = at("cqr", [P, 5, T], F32, 172)
        KRR = at("krr", [P, T], F32, 192)
        LT = [at(f"lt{j}", [P, T], F32, 196 + 4 * j) for j in range(2)]
        CNH = at("cnh", [P, 5, T], F32R, 27)
        CNL = at("cnl", [P, 5, T], F32R, 47)
        QKS = [[at(f"qks{j}{n}", [P, T], F32R, (67 if j == 0 else 92) + 4 * n) for n in range(4)] for j in range(2)]
        VS2 = [at(f"vs2{j}", [P, 8, P], F32R, 83 + 4 * j) for j in range(2)]
        LTH = at("lth", [P, 8, HALF], F32R, 108)
        LTL = at("ltl", [P, 8, HALF], F32R, 172)
        LP = [at(f"lp{j}", [P, T], F32, (124, 128, 196)[j]) for j in range(3)]
        LPS = [at(f"lps{j}", [P, (j + 1) * P], F32, (203.5, 204, 205)[j]) for j in range(3)]
        MQ = at("mq", [P, T], F32, 188)
        MKV = at("mkv", [P, T], F32, 192)
        MOT = at("mot", [P, HALF], F32, 200)
        CMB = at("cmb", [P, 2, P], BF16, 202)
        CMF = at("cmf", [P, 1, P], F32, 203)
        O2 = at("o2", [P, KT, T], F32, 172)
        N2 = [at(f"n2{j}", [P, T], F32, 124 + 4 * j) for j in range(2)]
        ACC3 = at("acc3", [P, T], F32, 132)
        RS2 = at("rs2", [P, T], F32, 136)
        HBH = [at(f"hbh{j}", [P, 2, T], F32R, 124 + 16 * j) for j in range(2)]
        HBL = [at(f"hbl{j}", [P, 2, T], F32R, 132 + 16 * j) for j in range(2)]
        FA = at("fa", [P, KT, T], F32, 156)
        TH = [at(f"th{j}", [P, T], F32, 188 + 4 * j) for j in range(2)]
        HF = [at(f"hf{j}", [P, T], F32, 196 + 4 * j) for j in range(2)]
        PR = at("pr", [P, 2, T], F32, 27)
        PH = at("ph", [P, 2, T], F32R, 35)
        PL = at("pl", [P, 2, T], F32R, 43)
        EB = at("eb", [P, KT, T], F32, 59)
        OB = at("ob", [P, KT, T], F32, 27)
        GH = at("gh", [P, KT, T], F32R, 124)
        GL = at("gl", [P, KT, T], F32R, 156)

        PS = [ctx.enter_context(nc.psum_tensor(f"ps{n}", [P, 2, HALF], F32)) for n in "abcd"]
        A, B, C, Dp = range(4)

        s_q = {n: sem(f"s_{n}") for n in ("sp", "act", "pool", "pe", "dve")}
        s_raw = [sem(f"s_raw{j}") for j in range(2)]
        s_split = sem("s_split")
        s_used = sem("s_used")
        s_out = sem("s_out")
        s_q["used"] = s_used
        pr = Program({n: Queue(n, s_q[n]) for n in s_q})
        do = pr.do

        def act(fn, *w, **k):
            return do("act", fn, *w, **k)

        def dve(fn, *w, **k):
            return do("dve", fn, *w, **k)

        def pe(fn, *w, **k):
            return do("pe", fn, *w, **k)

        def own(*operands):
            return [pr.last("dve")] if any(callable(x) for x in operands) else []

        def copy_(o, i, *w, scale=1.0):
            return act(lambda e, k: e.activation(r(o, k), r(i, k), ACT.Copy, scale=scale), *w)

        def fun(f, o, i, *w, scale=1.0, bias=0.0, acc=None):
            if acc is None:
                return act(lambda e, k: e.activation(r(o, k), r(i, k), f, scale=scale, bias=bias), *w)
            return act(lambda e, k: e.activation(r(o, k), r(i, k), f, scale=scale, bias=bias, accum_out=acc), *w)

        def tt(o, a, b, op, *w, q="dve"):
            return do(q, lambda e, k: e.tensor_tensor(r(o, k), r(a, k), r(b, k), op), *w,
                      *(own(o, a, b) if q == "dve" else []))

        def ts(o, a, s1, op0, *w, s2=None, op1=None, q="dve"):
            if op1 is None:
                return do(q, lambda e, k: e.tensor_scalar(r(o, k), r(a, k), s1, None, op0), *w, *own(o, a))
            return do(q, lambda e, k: e.tensor_scalar(r(o, k), r(a, k), s1, s2, op0, op1), *w)

        def stt(o, a, s, b, op0, op1, *w):
            return dve(lambda e, k: e.scalar_tensor_tensor(out=r(o, k), in0=r(a, k), scalar=s, in1=r(b, k),
                                                           op0=op0, op1=op1), *w, *own(o, a, b))

        def vcopy(o, i, *w):
            return ts(o, i, 1.0, MUL, *w)

        def dcopy(o, i, *w):
            return dve(lambda e, k: e.tensor_copy(r(o, k), r(i, k)), *w)

        def recip(o, i, *w):
            return dve(lambda e, k: e.reciprocal(r(o, k), r(i, k)), *w)

        def mm(o, l, rh, st, sp, *w, **kw):
            return pe(lambda e, k: e.matmul(r(o, k), lhsT=r(l, k), rhs=r(rh, k), start=st, stop=sp,
                                            skip_group_check=True), *w, **kw)

        def tr(o, i, ident, *w, **kw):
            return pe(lambda e, k: e.transpose(r(o, k), r(i, k), ident), *w, **kw)

        def r(x, k):
            return x(k) if callable(x) else x

        loads = [0]

        def load(q, dst, src, *w):
            loads[0] += 1
            s = sem(f"s_load{loads[0]}")
            do(q, lambda e, k: e.dma_start(dst, src), *w, inc=[(s, 16)], mark=False)
            return At(s, 16)

        def col(name, j=0, lo=0, hi=P):
            return COLS[lo:hi, COL[name] + j:COL[name] + j + 1]

        MUL, ADD, SUB, MAX = ALU.mult, ALU.add, ALU.subtract, ALU.max

        def slab_in(s, step, *w):
            j = s % 2
            free = [] if s < 2 else [At(s_split, s - 1, step)]
            do("sp", lambda e, k: e.dma_start(RAW[:, j, :], slabs[s + (k * step if step else 0)]),
               *free, *w, inc=[(s_raw[j], 16)], mark=False)

        def slab_split(s, step):
            j = s % 2
            free = [] if s < 2 else [At(s_used, s - 1, step)]
            if s == 0:
                do("pool", lambda e, k: e.memset(ONE[:, :], 1.0))
            h = do("pool", lambda e, k: e.tensor_tensor(WH[j][:, :], RAW[:, j, :],
                                                        ONE[:, 0:1].to_broadcast([P, 1024]), MUL),
                   At(s_raw[j], 16 * (s // 2 + 1), 16 * step // 2), *free, At(s_q["pool"], 1))
            do("pool", lambda e, k: e.tensor_tensor(WL[j][:, :], RAW[:, j, :], WH[j][:, :], SUB), h,
               inc=[(s_split, 1)], mark=False)

        def feed(fn, a, b):
            if b > a:
                pr.begin((b - a) // 2)
                fn(a, 2)
                fn(a + 1, 2)
                pr.end()

        done_split = [0]

        def split_to(b):
            if done_split[0] == 0:
                slab_split(0, 0)
                slab_split(1, 0)
                done_split[0] = 2
            feed(slab_split, done_split[0], b)
            done_split[0] = b

        def project(s, step, blocks, xh, xl, outs, *w, xw=None, m=P, last=True, start=True, stop=True):
            j = s % 2
            n = 0
            total = 3 * len(blocks)
            tok = None
            for bi, (blk, kt) in enumerate(blocks):
                wh, wl = WH[j][:, blk * P:blk * P + m], WL[j][:, blk * P:blk * P + m]
                for pas, (lw, xx) in enumerate(((wh, xh), (wh, xl), (wl, xh))):
                    for oi, (o, c0, cn) in enumerate(outs):
                        ws = []
                        if n == 0 and oi == 0:
                            ws += [At(s_split, s + 1, step), *w]
                        if pas < 2 and oi == 0 and xw is not None:
                            ws.append(xw[pas][kt])
                        end = n == total - 1 and oi == len(outs) - 1
                        tok = mm(o, lw, xx(kt, c0, cn), start and n == 0, stop and n == total - 1, *ws,
                                 mark=end, counter="used" if last else None)
                    n += 1
            return tok

        def halves(p):
            return [(PS[p][:, 0, :], 0, HALF), (PS[p][:, 1, :], HALF, HALF)]

        def both(p):
            return PS[p][:, :, :].rearrange("p a b -> p (a b)")

        def flat(x):
            return x[:, :, :].rearrange("p a b -> p (a b)")

        ps = [Slot() for _ in range(4)]

        def loop(n, slots, body):
            pr.begin(n)
            for x in slots:
                x.enter()
            body()
            for x in slots:
                x.leave()
            pr.end()

        def means(tile, pair, w):
            o = halves(pair)
            mm(o[0][0], SQC[:, 3, :], tile[:, 0:HALF], True, True, w, *ps[pair].waits(), mark=False)
            return mm(o[1][0], SQC[:, 3, :], tile[:, HALF:T], True, True)

        def token_sums(pair, tile, rhs, w, *waits, first=True, last=True, meta=False, bank=0):
            n = 9 if meta else 8
            for c in range(n):
                rows = P if c < 8 else META
                t = mm(PS[pair][0:rows, bank, c * w:c * w + w], tile[:, c * P:c * P + rows], rhs,
                       first and c == 0, last,
                       *(waits if c == 0 else []), mark=c == n - 1)
            return t

        def token_rstd(pair, n, w, *waits, meta=False, off=0):
            o = 18 * off
            a = fun(ACT.Sqrt, TOK[:, o:o + 8 * w], PS[pair][:, 0, 0:8 * w], *waits, scale=1.0 / n, bias=col("eps"))
            x = recip(TOK[:, o:o + 8 * w], TOK[:, o:o + 8 * w], a)
            if meta:
                m = slice(o + 8 * w, o + 9 * w)
                a = fun(ACT.Sqrt, TOK[0:META, m], PS[pair][0:META, 0, 8 * w:9 * w], *waits, scale=1.0 / n,
                        bias=col("eps", 0, 0, META))
                x = recip(TOK[0:META, m], TOK[0:META, m], a)
            return x

        def spread(pair, src, w, rb, x, meta=None, rbm=None):
            a = copy_(rb.rearrange("p (c n) -> p c n", n=P // w),
                      src[:, 0:8 * w].unsqueeze(2).to_broadcast([P, 8 * w, P // w]), x)
            for c in range(8):
                t = tr(PS[pair][:, c // 4, (c % 4) * P:(c % 4) * P + P], rb[:, c * P:c * P + P], SQC[:, 0, :],
                       *([a] + ps[pair].waits() if c == 0 else []), mark=c == 7)
            if meta is not None:
                a = copy_(rbm[0:META, :].rearrange("p (c n) -> p c n", n=P // w),
                          src[0:META, 8 * w:9 * w].unsqueeze(2).to_broadcast([META, w, P // w]), x)
                t = tr(PS[meta][:, 0, 0:META], rbm[0:META, :], SQC[0:META, 0, 0:META], a, *ps[meta].waits())
            return t

        def split_tiles(n, product, hi, lo, tmp, slots, *w):
            xw = ([None] * n, [None] * n)
            for m in range(n + 1):
                if m < n:
                    v = product(m, tmp[m % 2], slots[m % 2].free)
                    xw[0][m] = copy_(hi(m), tmp[m % 2], v, *w)
                if m >= 1:
                    b = (m - 1) % 2
                    q = "pool" if m % 3 == 0 and n == KT else "dve"
                    slots[b].free = xw[1][m - 1] = tt(lo(m - 1), tmp[b], hi(m - 1), SUB, xw[0][m - 1], *w, q=q)
            return xw

        st = {}

        def waits_of(*key):
            x = st[key]
            return x.waits() if isinstance(x, Slot) else [x]

        def carried(*keys):
            made = []
            for key in keys:
                made.append((key, Slot(st[key])))
                st[key] = made[-1][1]
            return made

        w_cols = load("sp", COLS[:, :], cols)
        w_x = [load("sp", X[:, kt, :], xT[kt]) for kt in range(KT)]
        w_sq = load("act", SQC[:, :, :], squares[0:4].rearrange("n p c -> p n c"))
        w_cs = load("act", COS1[:, :], rope1[0])
        w_sn = load("act", SIN1[:, :], rope1[1])
        slab_in(0, 0)
        slab_in(1, 0)
        feed(slab_in, 2, NSLAB)
        split_to(2)

        tt(GSQ[:, :], COLS[:, COL["final_g"]:COL["final_g"] + 8], COLS[:, COL["final_g"]:COL["final_g"] + 8], MUL,
           w_cols)
        GG = TINY[:, 48:56]
        t_gg = tt(GG, COLS[:, COL["final_g"]:COL["final_g"] + 8], COLS[:, COL["pre_mix"]:COL["pre_mix"] + 8], MUL)
        free = [None, None]
        for kt in range(KT):
            j = kt % 2
            if kt == 0:
                y = fun(ACT.Square, TMP[4][:, :], X[:, kt, :], w_x[kt])
            else:
                a = fun(ACT.Square, TMP[j][:, :], X[:, kt, :], w_x[kt], free[j])
                y = free[j] = tt(TMP[4][:, :], TMP[4][:, :], TMP[j][:, :], ADD, a, y)
        y = token_sums(C, TMP[4], SQC[:, 1, 0:1], 1, y, w_sq, meta=True)
        x = token_rstd(C, D, 1, y, w_cols, meta=True)
        ps[C].free = x
        t = spread(C, TOK[:, 0:9], 1, TMP[0][:, 0:T], x, meta=Dp, rbm=RBM)
        a = copy_(RS[:, T:L], PS[Dp][:, 0, 0:META], t)
        t_rs = copy_(RS[:, 0:T], both(C), t)
        ps[C].free = ps[Dp].free = t_rs
        xw = split_tiles(KT, lambda m, o, f: stt(o, X[:, m, :], col("norm_g", m), RS[:, :], MUL, MUL, t_rs, f),
                         lambda m: XH[:, m, :], lambda m: XL[:, m, :], [TMP[2][:, :], TMP[3][:, :]],
                         [Slot(), Slot()])

        split_to(S_OUT1)

        def xh(kt, c, n):
            return XH[:, kt, c:c + n]

        def xl(kt, c, n):
            return XL[:, kt, c:c + n]

        full = [(kt, kt) for kt in range(KT)]

        CUTS = ((0, 352), (352, 352), (704, 336))

        def thirds(p, m):
            return [(PS[q][:, b, 0:n], c, n) for (q, b), (c, n) in zip(((p, 0), (p, 1), (m, 0)), CUTS)]

        def pieces(p, m):
            (a, _, _), (b, _, _), (c, _, _) = thirds(p, m)
            return [(0, 352, a), (352, 352, b), (704, T - 704, c[:, 0:T - 704]), (T, META, c[:, T - 704:L - 704])]

        pair_meta = [(A, C), (B, Dp)]
        ft_zero = dve(lambda e, k: e.memset(FT[:, :, L:L + 2], 0.0), xw[1][KT - 1])

        def f_in(step, tile):
            for j in range(2):
                p, m = pair_meta[j]
                t = project(S_IN1 + tile + j, step, full, xh, xl, thirds(p, m),
                            *ps[p].waits(), *ps[m].waits(), xw=xw)
                for c, n, o in pieces(p, m):
                    c = c + META if c < T else 0
                    a = vcopy(FT[:, tile + j, c:c + n], o, t)
                ps[p].free = ps[m].free = a

        f_in(0, 0)
        f_in(0, 2)
        ft_done = ps[B].free

        raw, sqt, t1, rsk, t2 = TMP
        S_raw, S_sq, S_t1, S_rs, S_t2 = (Slot() for _ in range(5))
        kq_slots = [S_raw, S_sq, S_t1, S_rs, S_t2]
        for x in kq_slots:
            x.free = xw[1][KT - 1]

        def turn(t, p, pm, g, width):
            for c, n, o in (pieces(p, pm) if pm is not None else [(0, T, both(p))]):
                a = copy_(raw[:, c:c + n], o, t, *S_raw.waits())
            ps[p].free = a
            b = fun(ACT.Square, sqt[:, 0:width], raw[:, 0:width], a, *S_sq.waits())
            stt(t1[:, 0:width], raw[:, 0:width], col(g), COS1[:, 0:width], MUL, MUL, a, w_cs, w_sn, *S_t1.waits())
            for q4 in range(4):
                lo, src = 32 * q4, 32 * (q4 ^ 1)
                v = stt(t2[lo:lo + 32, 0:width], raw[src:src + 32, 0:width], col(g, 0, src, src + 32),
                        SIN1[src:src + 32, 0:width], MUL, MUL, *(S_t2.waits() if q4 == 0 else []))
            S_raw.free = v
            v = tt(t1[:, 0:width], t1[:, 0:width], t2[:, 0:width], ADD, v)
            S_t2.free = v
            return a, b, v

        def norm_heads(b, v, pair, meta, out, width):
            m = meta is not None
            s = token_sums(pair, sqt, SQC[:, 2, 0:P:HD], 2, b, *ps[pair].waits(), meta=m)
            S_sq.free = s
            x = token_rstd(pair, HD, 2, s, *S_rs.waits(), meta=m)
            ps[pair].free = x
            t = spread(pair, TOK[:, 0:18], 2, rsk[:, 0:T], x, meta=meta, rbm=RBM)
            S_rs.free = t
            if m:
                x = tt(out[:, T:L], t1[:, T:L], PS[meta][:, 0, 0:META], MUL, t, v)
                ps[meta].free = x
                out = out[:, 0:T]
            x = tt(out, t1[:, 0:T], both(pair), MUL, t, v)
            ps[pair].free = S_t1.free = x
            return x

        t = project(S_IN1 + 4, 0, full, xh, xl, thirds(A, C),
                    *ps[A].waits(), *ps[C].waits(), xw=xw)
        a, b_, v_ = turn(t, A, C, "k_g", L)
        ps[C].free = a
        t = project(S_IN1 + 5, 0, full, xh, xl, thirds(B, Dp),
                    *ps[B].waits(), *ps[Dp].waits())
        for c, n, o in pieces(B, Dp):
            t_v = copy_(V1[:, c:c + n], o, t)
        ps[B].free = ps[Dp].free = t_v
        t_k = norm_heads(b_, v_, C, Dp, K1[:, :], L)

        prev = None
        for j in range(4):
            p, pn = (A, B)[j % 2], (C, Dp)[j % 2]
            t = project(S_IN1 + 6 + j, 0, full, xh, xl, halves(p), *ps[p].waits())
            if prev is not None:
                norm_heads(*prev)
            _, b0, v0 = turn(t, p, None, "q_g", T)
            prev = (b0, v0, pn, None, Q1[:, j, :], T)
        t_turned = v0

        S_th = [Slot(xw[1][KT - 1]), Slot(t_turned)]

        def gates(step, tile):
            for j in range(2):
                p = (A, B)[j]
                t = project(S_IN1 + 10 + tile + j, step, full, xh, xl, halves(p), *ps[p].waits())
                a = fun(ACT.Tanh, GTH[j][:, :], both(p), t, *S_th[j].waits(), scale=0.5)
                g = stt(lambda k, j=j: GT[:, k * 2 + tile + j, :], GTH[j][:, :], 1.0, both(p), ADD, MUL, a)
                S_th[j].free = ps[p].free = g

        gates(0, 0)
        t_q = norm_heads(*prev)
        w_wf = load("act", WF[:, :], wf, t_q)
        w_cd = load("act", CD[:, :, :], cd.rearrange("a p c -> p a c"))
        tt(FE[:, :, 0:NM], FT[:, :, 0:NM], FT[:, :, L:L - NM:-1], ADD, t_q, ft_done, ft_zero)
        f2 = tt(FO[:, :, 0:NM], FT[:, :, 0:NM], FT[:, :, L:L - NM:-1], SUB)
        w_ct = load("act", CT[:, :, :], dft[0].rearrange("(m p) n -> p m n", p=P), f2)
        w_st = load("act", ST[:, :, :], dft[1].rearrange("(m p) n -> p m n", p=P))
        z = dve(lambda e, k: e.memset(WBD[:, :, :, :], 0.0), f2)
        for a in range(2):
            t = mm(PS[C][:, a, :], CD[:, a, :], WF[:, :], True, True, *ps[C].waits(), w_wf, w_cd)
        for a in range(2):
            for h in range(2):
                rows = slice(64 * h, 64 * h + 64)
                c = dcopy(WBD[rows, a, :, 64 * h:64 * h + 64],
                          PS[C][rows, a, :].rearrange("p (j two c) -> p j two c", two=2, c=64)[:, :, h, :], t, z)
        ps[C].free = w_g = c
        loop(3, ps + S_th, lambda: gates(2, 2))
        t_gates = ps[B].free
        split_to(S_OUT1 + 2)

        for mt in range(MT5):
            w = min(P, NM - mt * P)
            p = (A, B, C, Dp)[mt % 4]
            for a, F_ in enumerate((FE, FO)):
                for ct in range(4):
                    t = mm(PS[p][0:w, a, ct * P:ct * P + P], F_[:, ct, mt * P:mt * P + w], WBD[:, a, ct, :],
                           True, True, w_g, f2, *ps[p].waits(), mark=(a == 1 and ct == 3))
            ga = copy_(GA[0:w, mt, :], PS[p][0:w, 0, :], t, t_gates)
            gb = copy_(GB[0:w, mt, :], PS[p][0:w, 1, :], t)
            ps[p].free = gb
        t_folded = t
        for kv in range(2):
            mine, rest = slice(64 * kv, 64 * kv + 64), slice(64 - 64 * kv, 128 - 64 * kv)
            a = copy_(KHH[kv][mine, :], K1[mine, :], t_folded, t_k)
            t_kh = copy_(KHH[kv][rest, :], K1[mine, :])
            tt(KLL[kv][mine, :], K1[mine, :], KHH[kv][mine, :], SUB, a)
            t_kl = tt(KLL[kv][rest, :], K1[mine, :], KHH[kv][mine, :], SUB)
        S_q, S_p = Slot(), Slot()
        n = 0
        for dt in range(4):
            for h in range(2):
                p = (A, B, C, Dp)[(MT5 + n) % 4]
                n += 1
                c0, cn = h * (NL // 2), NL // 2
                for a, (G_, TB) in enumerate(((GA, CT), (GB, ST))):
                    for mt in range(MT5):
                        w = min(P, NM - mt * P)
                        t = mm(PS[p][:, a, 0:cn], G_[0:w, mt, dt * P:dt * P + P], TB[0:w, mt, c0:c0 + cn],
                               mt == 0, mt == MT5 - 1, gb, w_ct, w_st, *ps[p].waits(),
                               mark=(a == 1 and mt == MT5 - 1))
                q_ = copy_(QSB[:, 0:cn], PS[p][:, 1, 0:cn], t, *S_q.waits())
                k0 = META - 1 if h == 0 else 0
                k1 = cn if h == 0 else cn - 1
                x = stt(PSB[:, 0:cn], PS[p][:, 0, 0:cn], col("b_fmix", dt), QSB[:, 0:cn], ADD, SUB, q_, S_p.free)
                r0 = c0 + 1 + k0 - META
                seg = GT[:, dt, r0:r0 + cn - k0]
                x = stt(seg, PSB[:, k0:cn], 0.5, seg, MUL, MUL, x)
                y = stt(PSB[:, cn:2 * cn], PS[p][:, 0, 0:cn], col("b_fmix", dt), QSB[:, 0:cn], ADD, ADD)
                S_q.free = ps[p].free = y
                hi_, lo_ = T - (c0 + 1), T - (c0 + k1)
                seg = GT[:, dt, lo_:hi_ + 1]
                S_p.free = stt(seg, PSB[:, cn + k1 - 1:cn - 1:-1], 0.5, seg, MUL, MUL, y)
        t_four = S_p.free

        for kt in range(8):
            t = tr(PS[C][:, kt // 4, (kt % 4) * P:(kt % 4) * P + P], V1[:, kt * P:kt * P + P], SQC[:, 0, :],
                   *ps[C].waits(), t_v, mark=kt == 7)
        t = tr(PS[Dp][0:META, 0, 0:P], V1[:, T:L], SQC[:, 0, :], *ps[Dp].waits())
        src = [PS[C][:, :, :].rearrange("p a (k c) -> p (a k) c", c=P)[:, :, 64 * kv:64 * kv + 64] for kv in range(2)]
        srm = [PS[Dp][0:META, 0, 64 * kv:64 * kv + 64] for kv in range(2)]
        for kv in range(2):
            copy_(VS1[kv][:, 0:8, 0:64], src[kv], t, t_four)
            a = copy_(VS1[kv][0:META, 8, 0:64], srm[kv])
        for kv in range(2):
            t_vs = tt(VS1[kv][:, 0:8, 64:128], src[kv], VS1[kv][:, 0:8, 0:64], SUB, a)
            t_vs = tt(VS1[kv][0:META, 8, 64:128], srm[kv], VS1[kv][0:META, 8, 0:64], SUB)
        ps[C].free = ps[Dp].free = t_vs

        MXM, NB, RSA, RSM, RI = (TINY[:, 4 * n:4 * n + 4] for n in range(1, 6))
        MXT = TINY[:, 24:32]
        S_qs, S_pm, S_pt, S_ot = ([Slot(), Slot()] for _ in range(4))
        S_pb = [Slot(t_vs) for _ in range(4)]
        S_pmh, S_sm, S_av = Slot(), Slot(t_vs), Slot(t_vs)
        S_smc = [Slot(t_vs), Slot(t_vs)]
        S_tc = [Slot(t_vs), Slot(t_vs)]
        S_sc = [ps[A], ps[B]]
        at_slots = S_qs + S_pb + S_pm + S_pt + [S_pmh, S_sm, S_av] + S_smc + S_tc + S_ot + S_sc
        scale1 = HD ** -0.5
        st.clear()

        def stage(s, tile):
            mine, rest = slice(64 * s, 64 * s + 64), slice(64 - 64 * s, 128 - 64 * s)
            a = vcopy(QST[s][mine, :], lambda k: Q1[mine, k + tile, :], *S_qs[s].waits())
            st["q", s] = tt(QST[s][rest, :], lambda k: Q1[mine, k + tile, :], QST[s][mine, :], SUB, a)

        def meta_scores(g):
            s = g // 2
            for v in range(4):
                c0 = (4 * (g % 2) + v) * P
                o = PS[Dp][:, 0, v * META:v * META + META]
                mm(o, QST[s][:, c0:c0 + P], KHH[s][:, T:L], True, False, *waits_of("q", s), *S_sm.waits(), mark=False)
                t = mm(o, QST[s][:, c0:c0 + P], KLL[s][:, T:L], False, True, mark=v == 3)
            S_sm.free = st["smc", g] = copy_(SMC[:, g % 2, :], PS[Dp][:, 0, 0:4 * META], t, *S_smc[g % 2].waits())
            st["mt", g] = dve(lambda e, k: e.tensor_reduce(
                MXT[:, 4 * (g % 2):4 * (g % 2) + 4], SMC[:, g % 2, :].rearrange("p (a b) -> p a b", b=META),
                AX.X, MAX), st["smc", g])

        def scores(u):
            s, qt = divmod(u, 8)
            q = QST[s][:, qt * P:qt * P + P]
            for h in range(2):
                c = slice(h * HALF, h * HALF + HALF)
                mm(PS[u % 2][:, h, :], q, KHH[s][:, c], True, False, *(waits_of("q", s) if qt == 0 else []),
                   *S_sc[u % 2].waits(), t_kl, t_kh, mark=False)
                t = mm(PS[u % 2][:, h, :], q, KLL[s][:, c], False, True, mark=h == 1)
            st["s", u] = t
            if qt == 7:
                S_qs[s].free = t

        def maxima(u):
            v, g = u % 4, u // 4
            m = dve(lambda e, k: e.tensor_reduce(MXM[:, v:v + 1], both(u % 2), AX.X, MAX), *waits_of("s", u),
                    *(waits_of("mt", g) if v == 0 else []))
            st["nb", u] = ts(NB[:, v:v + 1], MXM[:, v:v + 1], MXT[:, 4 * (g % 2) + v:4 * (g % 2) + v + 1], MAX, m,
                             s2=-scale1, op1=MUL)

        def exps(u):
            v, g = u % 4, (u // 4) % 2
            S_sc[u % 2].free = fun(ACT.Exp, PB[v][:, :], both(u % 2), st["nb", u], *S_pb[v].waits(), scale=scale1,
                                   bias=NB[:, v:v + 1], acc=RSA[:, v:v + 1])
            st["e", u] = S_smc[g].free = fun(
                ACT.Exp, PM[g][:, v, :], SMC[:, g, v * META:v * META + META],
                *(S_pm[g].waits() + waits_of("smc", u // 4) if v == 0 else []), scale=scale1, bias=NB[:, v:v + 1],
                acc=RSM[:, v:v + 1])

        def norms(u):
            v, g = u % 4, (u // 4) % 2
            x = tt(RI[:, v:v + 1], RSA[:, v:v + 1], RSM[:, v:v + 1], ADD, *waits_of("e", u))
            x = recip(RI[:, v:v + 1], RI[:, v:v + 1], x)
            tt(PB[v][:, :], PB[v][:, :], RI[:, v:v + 1].to_broadcast([P, T]), MUL, x, q="pool")
            st["p", u] = tt(PM[g][:, v, :], PM[g][:, v, :], RI[:, v:v + 1].to_broadcast([P, META]), MUL, q="pool")

        def turns(u):
            v = u % 4
            for h in range(2):
                for kt in range(4):
                    c = (4 * h + kt) * P
                    t = tr(PS[C][:, h, kt * P:kt * P + P], PB[v][:, c:c + P], SQC[:, 0, :],
                           *(waits_of("p", u) + S_tc[h].waits() if kt == 0 else []), mark=kt == 3)
                st["t", u, h] = t
            S_pb[v].free = t

        def parts(u):
            v, g = u % 4, (u // 4) % 2
            w = S_pt[g].waits() if v == 0 else []
            for h in range(2):
                src = PS[C][:, h, :].rearrange("p (k q) -> p k q", q=P)
                dst = slice(4 * h, 4 * h + 4)
                a = copy_(PTH[g][:, dst, v * P:v * P + P], src, st["t", u, h], *w)
                S_tc[h].free = tt(PTL[g][:, dst, v * P:v * P + P], src, PTH[g][:, dst, v * P:v * P + P],
                                  SUB, a, *w)
            if v == 3:
                st["lo", u // 4] = S_tc[1].free

        def meta_turn(g):
            for x in range(4):
                t = tr(PS[Dp][0:META, 0, x * P:x * P + P], PM[g % 2][:, x, :], SQC[:, 0, :],
                       *(waits_of("p", 4 * g + 3) + S_sm.waits() if x == 0 else []), mark=x == 3)
            S_pm[g % 2].free = st["tm"] = t

        def meta_parts(g):
            a = copy_(PMH[:, :], PS[Dp][0:META, 0, :], st["tm"], *S_pmh.waits())
            st["lm", g] = S_sm.free = tt(PML[:, :], PS[Dp][0:META, 0, :], PMH[:, :], SUB, a, *S_pmh.waits())

        def values(g, third, tile):
            s = g // 2
            for n in range(6 * third, 6 * third + 6):
                kt, hl = divmod(n, 2)
                rows = slice(0, P) if kt < 8 else slice(0, META)
                rh = (PTH, PTL)[hl][g % 2][:, kt, :] if kt < 8 else (PMH, PML)[hl][:, :]
                w = waits_of("lo", g) + S_av.waits() + [t_vs] if n == 0 else [st["lm", g]] if n == 16 else []
                t = mm(PS[Dp][:, 1, :], VS1[s][rows, kt, :], rh, n == 0, n == 17, *w, mark=n == 17)
            if third == 2:
                S_pt[g % 2].free = S_pmh.free = st["o", g] = t

        def outputs(g, tile):
            s = g // 2
            t = st["o", g]
            mine, rest = slice(64 * s, 64 * s + 64), slice(64 - 64 * s, 128 - 64 * s)
            a = copy_(OT[g % 2][mine, :], PS[Dp][rest, 1, :], t, *S_ot[g % 2].waits())
            x = tt(OT[g % 2][mine, :], OT[g % 2][mine, :], PS[Dp][mine, 1, :], ADD, a)
            S_av.free = x
            c0 = (g % 2) * HALF
            seg = lambda k: GT[mine, k + tile + 4, c0:c0 + HALF]
            S_ot[g % 2].free = stt(seg, OT[g % 2][mine, :], 0.5, seg, MUL, MUL, x)

        LAG = 3
        AHEAD = 7

        def step(u, tile, last=False):
            end = 16 if last else 16 + AHEAD
            front, back = u < end, 0 <= u - LAG < (16 if last else end)
            f, b = u % 16, (u - LAG) % 16
            g, phase = divmod(u - AHEAD, 4)
            if f == 5 and not last:
                stage(1, tile + u // 16)
            if u == 13 and not last:
                stage(0, tile + 1)
            if g >= 0 and phase == 1:
                meta_turn(g)
            if back:
                turns(b)
            if u + 1 < (16 if last else end + 1):
                scores((u + 1) % 16)
            if g >= 0 and phase < 3:
                values(g, phase, tile)
            if front:
                maxima(f)
            if 0 <= u - 1 < (16 if last else end):
                norms((u - 1) % 16)
            if back:
                parts(b)
            if front:
                exps(f)
            if g >= 0 and phase == 1:
                meta_parts(g)
            if g >= 0 and phase == 3:
                outputs(g, tile)
            if f % 4 == 1 and u < (13 if last else end):
                meta_scores((f // 4 + 1) % 4)

        stage(0, 0)
        meta_scores(0)
        scores(0)
        for u in range(AHEAD):
            step(u, 0)
        hand = carried(("p", 3), ("p", 4), ("p", 5), ("lo", 0), ("e", 6), ("s", AHEAD), ("q", 1), ("smc", 2), ("mt", 2))

        def attention():
            for u in range(AHEAD, 16 + AHEAD):
                step(u, 0)
            for key, slot in hand:
                slot.free = st[key]

        loop(3, at_slots + [x for _, x in hand], attention)
        for u in range(AHEAD, 16 + AHEAD):
            step(u, 3, last=True)
        t_att = S_ot[1].free
        ps[C].free, ps[Dp].free = S_tc[0].free, S_av.free

        w_h = [load("act", H[:, m, :], xT[m][:, 0:T], t_att if m == 0 else None) for m in range(KT)]

        def mh(kt, c, n):
            return MH[:, kt, c:c + n]

        def ml(kt, c, n):
            return ML[:, kt, c:c + n]

        def split_all(src, w):
            xw = ([None] * KT, [None] * KT)
            for m in range(KT):
                xw[0][m] = copy_(MH[:, m, :], src[:, m, :], w)
                xw[1][m] = tt(ML[:, m, :], src[:, m, :], MH[:, m, :], SUB, xw[0][m])
            return xw

        xw = split_all(GT, t_att)

        w_pos = load("act", PI[:, :], pos.broadcast_to((P, T)), t_att)
        TWO_PI = 2 * np.pi
        C1 = 6.28125
        C2 = float(np.round((TWO_PI - C1) * 2 ** 21) / 2 ** 21)
        C3 = float(np.float32(TWO_PI - C1 - C2))
        MAGIC = float(3 << 22)
        PI_LO = float(np.nextafter(np.float32(np.pi), np.float32(0)))

        def rope_table(inv, sgn, CO, SI, pi, ang, kround, red, *w):
            x = ts(ang, pi, col(inv), MUL, *w)
            x = ts(kround, ang, 1.0 / TWO_PI, MUL, x, s2=MAGIC, op1=ADD)
            x = ts(kround, kround, MAGIC, SUB, x)
            for c in (C1, C2, C3):
                x = stt(red, kround, -c, ang if c == C1 else red, MUL, ADD, x)
            yield x
            x = ts(red, red, PI_LO, ALU.min, x, s2=-PI_LO, op1=MAX)
            a = fun(ACT.Sin, SI[:, :], red, x)
            a = fun(ACT.Abs, ang, red, a)
            a = fun(ACT.Sin, CO[:, :], ang, a, scale=-1.0, bias=col("halfpi"))
            yield ts(SI[:, :], SI[:, :], col(sgn), MUL, a)

        S_n = [Slot(t_att), Slot(t_att)]
        split_to(S_RET + 2)
        st.clear()

        def out1(step, tile):
            for j in range(2):
                p = (A, B)[j]
                t = project(S_OUT1 + tile + j, step, full, mh, ml, halves(p), *ps[p].waits(), xw=xw)
                m = tile + j
                hm = lambda k, m=m: H[:, k * 2 + m, :]
                x = tt(hm, hm, both(p), ADD, t, *w_h)
                ps[p].free = x
                if m == 0:
                    x = tt(ACC1[:, :], hm, hm, MUL, x)
                    st["acc"] = ts(ACC2[:, :], ACC1[:, :], GSQ[:, 0:1], MUL, x)
                    continue
                g = dcopy(TINY[:, 56:57], lambda k, m=m: GSQ[:, bass.ds(k * 2 + m, 1)], x)
                x = tt(N1[0][:, :], hm, hm, MUL, x)
                tt(ACC1[:, :], ACC1[:, :], N1[0][:, :], ADD, x)
                st["acc"] = stt(ACC2[:, :], N1[0][:, :], TINY[:, 56:57], ACC2[:, :], MUL, ADD, g)

        out1(0, 0)
        loop(3, ps, lambda: out1(2, 2))
        token_sums(C, ACC1, SQC[:, 1, 0:1], 1, st["acc"], *ps[C].waits())
        t = token_sums(C, ACC2, SQC[:, 1, 0:1], 1, bank=1)
        R1, R12 = TOK[:, 0:8], TOK[:, 8:16]
        x = fun(ACT.Sqrt, R1, PS[C][:, 0, 0:8], t, scale=1.0 / D, bias=col("eps"))
        x = recip(R1, R1, x)
        y = tt(R12, R1, R1, MUL, x)
        y = tt(R12, R12, PS[C][:, 1, 0:8], MUL, y)
        ps[C].free = y
        y = fun(ACT.Sqrt, R12, R12, y, scale=1.0 / D, bias=col("eps"))
        y = recip(R12, R12, y)
        y = tt(R12, R12, R1, MUL, y)
        t12 = spread(Dp, R12, 1, RS1[:, :], y)
        t1_ = spread(C, R1, 1, ACC1[:, :], x)
        xw = split_tiles(KT, lambda m, o, f: stt(o, H[:, m, :], GG[:, m:m + 1], both(Dp), MUL, MUL, t12, t_gg, f),
                         lambda m: MH[:, m, :], lambda m: ML[:, m, :], [N1[0][:, :], N1[1][:, :]], S_n, t)
        xw_norm2 = xw[1][KT - 1]
        ps[Dp].free = xw_norm2
        t_tab1 = x = None
        for x in rope_table("inv_ret", "sgn_ret", COS2, SIN2, PI[:, :], ANG[:, :], KR_[:, :], RED[:, :], w_pos, t_att):
            t_tab1 = x
        hw = [stt(H[:, m, :], H[:, m, :], col("final_g", m), both(C), MUL, MUL, t1_) for m in range(KT)]
        ps[C].free = hw[-1]

        w_rx = load("act", RX[:, :, :], squares[5:13].rearrange("n p c -> p n c"), xw_norm2)
        hs = nc.dram_tensor("residual", (KT, P, T), F32, kind="Internal").ap()
        w_spill = [load("act", hs[m], H[:, m, :], hw[m]) for m in range(KT)]
        (S_rr, S_t, S_rk, S_rq, S_rv, S_kn, S_vn, S_zt) = ret_slots = [Slot(xw_norm2) for _ in range(8)]
        ret_scale = CH ** -0.5
        S_th = [Slot(w_spill[-1])]
        split_to(S_LORA)

        def turn2(p, dst, slot, t, sc):
            a = copy_(RRAW[:, :], both(p), t, *S_rr.waits(), scale=sc)
            ps[p].free = a
            x = tt(RT1[:, :], RRAW[:, :], COS2[:, :], MUL, a, t_tab1, *S_t.waits())
            tt(dst[0:64, :], RRAW[64:128, :], SIN2[64:128, :], MUL, *slot.waits())
            y = tt(dst[64:128, :], RRAW[0:64, :], SIN2[0:64, :], MUL)
            S_rr.free = y
            y = tt(dst[:, :], dst[:, :], RT1[:, :], ADD, y)
            S_t.free = y
            return y

        def chunk(x, n):
            return x[:, n * CH:n * CH + CH]

        def retention(step, head):
            s_ret = S_RET + 4 * head

            def tokens(pair, src, w, slot):
                for n in range(NCH):
                    t = tr(PS[pair][:, n // 4, (n % 4) * CH:(n % 4) * CH + CH], chunk(src, n), SQC[:, 0, :], w,
                           *slot.waits(), mark=n == 7)
                return t

            def place(pair, n):
                return PS[pair][:, n // 4, (n % 4) * CH:(n % 4) * CH + CH]

            t = project(s_ret, step, full, mh, ml, halves(A), *ps[A].waits(), xw=xw)
            k_ = turn2(A, RK, S_rk, t, ret_scale)
            dcopy(TINY[:, 32:33], lambda k: COLS[:, bass.ds(k + head + COL["zeta"], 1)], *S_zt.waits())
            z_ = dcopy(TINY[:, 33:34], lambda k: COLS[:, bass.ds(k + head + COL["gch"], 1)])
            t = project(s_ret + 1, step, full, mh, ml, halves(B), *ps[B].waits())
            ps[B].free = v_ = copy_(RV[:, :], both(B), t, *S_rv.waits())
            t_qp = project(s_ret + 2, step, full, mh, ml, halves(A), *ps[A].waits())
            q_ = turn2(A, RQ, S_rq, t_qp, 1.0)
            t = tokens(C, RK, k_, ps[C])
            kn = ts(flat(RKN), both(C), TINY[:, 32:33], MUL, t, z_, *S_kn.waits())
            t = tokens(Dp, RV, v_, ps[Dp])
            ps[Dp].free = vn = copy_(flat(RVN), both(Dp), t, *S_vn.waits())
            t_rv = t
            t = project(s_ret + 3, step, full, mh, ml, halves(B), *ps[B].waits())
            a = fun(ACT.Tanh, RTH[:, :], both(B), t, *S_th[0].waits(), scale=0.5)
            ps[B].free = S_th[0].free = stt(lambda k: GR[:, k + head, :], RTH[:, :], 1.0, both(B), ADD, MUL, a)
            for n in range(NCH - 1):
                u = mm(place(C, n), RKN[:, n, :], RVN[:, n, :], True, True, kn, vn, mark=n == NCH - 2)
            S_kn.free = u
            for n in range(NCH):
                t = mm(place(Dp, n), chunk(RK, n), chunk(RQ, n), True, True, q_, *ps[Dp].waits(), mark=n == 7)
            S_rk.free = S_rq.free = t
            xq = tt(RRAW[:, :].rearrange("p (n c) -> p n c", c=CH), RQ[:, :].rearrange("p (n c) -> p n c", c=CH),
                    lambda k: RX[:, k + head, :].unsqueeze(1).to_broadcast([P, NCH, CH]), MUL, w_rx, q_)
            ps[Dp].free = sc = tt(RT1[:, :].rearrange("p (n c) -> p n c", c=CH),
                                  PS[Dp][:, :, :].rearrange("p a (n c) -> p (a n) c", c=CH),
                                  lambda k: RX[:, k + head + 4, :].unsqueeze(1).to_broadcast([P, NCH, CH]), MUL, t, q_)
            x = dve(lambda e, k: e.memset(chunk(RV, 0), 0.0), u, t_rv)
            for n in range(NCH - 1):
                x = stt(chunk(RV, n + 1), chunk(RV, n), TINY[:, 33:34], place(C, n), MUL, ADD, x)
            ps[C].free = S_zt.free = states = x
            for n in range(NCH):
                mm(place(A, n), RVN[:, n, :], chunk(RT1, n), n % 4 == 0, False, sc, *ps[A].waits(), mark=False)
            for n in range(NCH):
                t = mm(place(A, n), chunk(RV, n), chunk(RRAW, n), False, True, xq, states, mark=n == 7)
            S_rr.free = S_t.free = S_rv.free = S_vn.free = t
            ps[A].free = vcopy(lambda k: MX[:, k + head, :], both(A), t)

        retention(0, 0)
        loop(3, ps + ret_slots + [S_th[0]], lambda: retention(4, 1))
        t_ret = ps[A].free

        split_to(S_MLA)
        GS, S_gs = (LT[0], LL[0]), (Slot(t_ret), Slot(t_ret))
        lora, lat_sq = [], []

        def head_mean(n):
            v = means(MX[:, n, :], C, t_ret)
            x = tt(MX[:, n, :], MX[:, n, :], both(C), SUB, v)
            ps[C].free = x
            st["gsq", n] = fun(ACT.Square, GS[n % 2][:, :], MX[:, n, :], x, S_gs[n % 2].free, *w_spill)

        def head_sums(n):
            S_gs[n % 2].free = t = token_sums(Dp, GS[n % 2], SQC[:, 3, 0:1], 1, st["gsq", n], *ps[Dp].waits())
            st["grs"] = ps[Dp].free = token_rstd(Dp, 1, 1, t)

        def head_scaled(n):
            v = spread(Dp, TOK[:, 0:8], 1, LT[1][:, :], st["grs"])
            y = stt(MX[:, n, :], MX[:, n, :], col("ret_gn", n), both(Dp), MUL, MUL, v)
            ps[Dp].free = y
            return stt(MX[:, n, :], MX[:, n, :], 0.5, GR[:, n, :], MUL, MUL, y)

        def latent_sums(lo, cnt, pair, off):
            t = lat_sq[lo]
            for j in range(1, cnt):
                t = tt(LSQ[lo][:, :], LSQ[lo][:, :], LSQ[lo + j][:, :], ADD, lat_sq[lo + j], t)
            t = token_sums(pair, LSQ[lo], SQC[:, 1, 0:1], 1, t, *ps[pair].waits())
            ps[pair].free = x = token_rstd(pair, cnt * P, 1, t, off=off)
            return x

        def latent_split(name, lo, cnt, pair, off, rb, x):
            t = spread(pair, TOK[:, 18 * off:18 * off + 8], 1, rb[:, :], x)
            w = split_tiles(cnt, lambda m, o, f: stt(o, CQR[:, lo + m, :], col(name, m), both(pair), MUL, MUL, t, f),
                            lambda m: CNH[:, lo + m, :], lambda m: CNL[:, lo + m, :], [LL[0][:, :], LL[1][:, :]], S_ll,
                            t_lora)
            ps[pair].free = w[1][cnt - 1]
            return w

        w_pi = load("act", PI2[:, :], pos.broadcast_to((P, T)), *w_spill, t_ret)
        table = rope_table("inv_mla", "sgn_mla", COS3, SIN3, PI2[:, :], *(TAB[n][:, :] for n in range(3)), w_pi, t_ret)
        for n in range(6):
            p = (A, B)[n % 2]
            t = project(S_LORA + n, 0, full, mh, ml, halves(p), *ps[p].waits())
            a = copy_(CQR[:, n, :] if n < 5 else KRR[:, :], both(p), t, t_ret)
            if n < 5:
                a = fun(ACT.Square, LSQ[n][:, :], both(p), a, *w_spill)
                lat_sq.append(a)
            ps[p].free = a
            lora.append(a)
            t_lora = t
            if 2 <= n:
                t_gn = head_scaled(n - 2)
            if n < 4:
                head_mean(n)
            if 1 <= n < 5:
                head_sums(n - 1)
            if n in (2, 3):
                t_tab = next(table)
            if n == 4:
                x_q = latent_sums(0, 3, C, 1)
        S_ll = [Slot(S_gs[1].free), Slot()]
        x_kv = latent_sums(3, 2, Dp, 2)
        cq = latent_split("mla_q", 0, 3, C, 1, LP[0], x_q)
        ckv = latent_split("mla_kv", 3, 2, Dp, 2, LP[1], x_kv)
        cw = (cq[0] + ckv[0], cq[1] + ckv[1])
        tt(KRR[64:96, :], KRR[64:96, :], COS3[64:96, :], MUL, lora[5], t_tab)
        x = tt(LT[0][64:96, :], KRR[96:128, :], SIN3[96:128, :], MUL, S_gs[0].free)
        x = tt(KRR[64:96, :], KRR[64:96, :], LT[0][64:96, :], ADD, x)
        for j in range(2):
            a = copy_(QKS[j][2][64:96, :], KRR[64:96, :], x, t_lora, x_q)
            t_kr = tt(QKS[j][3][64:96, :], KRR[64:96, :], QKS[j][2][64:96, :], SUB, a)
        t_swap = dcopy(COS3[96:128, :], SIN3[96:128, :], t_tab)
        cm = load("act", CMF[:, :, :], squares[4:5].rearrange("n p c -> p n c"), t_kr)
        c1 = dcopy(CMB[:, 0, :], CMF[:, 0, :], cm)
        t_cmb = dcopy(CMB[:, 1, :], SQC[:, 0, :], c1)

        def cnh(kt, c, n):
            return CNH[:, kt, c:c + n]

        def cnl(kt, c, n):
            return CNL[:, kt, c:c + n]

        S_set, S_v2 = [Slot(t_kr), Slot(t_kr)], [Slot(t_kr), Slot(t_kr)]
        ready = [Slot(), Slot()]
        S_mq, S_mkv = Slot(t_kr), Slot(t_kr)
        LPB = LPS + [LP[u % 3] for u in range(3, 8)]
        S_lps, S_lp = [Slot(t_kr) for _ in range(3)], [Slot(t_kr) for _ in range(3)]
        S_lpb = S_lps + [S_lp[u % 3] for u in range(3, 8)]
        S_ptl, S_mot = Slot(t_kr), Slot()
        S_av, S_pj = Slot(ps[Dp].free), Slot(ps[Dp].free)
        S_tc = [Slot(ps[C].free), Slot(ps[C].free)]
        ml_slots = ready + S_set + S_v2 + S_lps + S_lp + S_tc + [S_pj, S_mq, S_mkv, S_ptl, S_mot, S_av, ps[A], ps[B]]
        scale2 = MQK ** -0.5
        st.clear()

        def mla_project(h, step, n):
            q, half = n < 2, n % 2
            t = project(S_MLA + h, step, [(0, 0), (1, 1), (2, 2)] if q else [(3, 3), (4, 4)], cnh, cnl,
                        [(PS[Dp][:, 0, :], half * HALF, HALF)], *S_pj.waits(), xw=cw, last=n == 3)
            st["pj"] = n, t

        def mla_projected():
            n, t = st["pj"]
            q, half = n < 2, n % 2
            dst, slot = (MQ, S_mq) if q else (MKV, S_mkv)
            st["q" if q else "kv",] = S_pj.free = copy_(dst[:, half * HALF:half * HALF + HALF], PS[Dp][:, 0, :], t,
                                                        *(slot.waits() if half == 0 else []))

        def query_products():
            st["qp"] = tt(MQ[64:128, :], MQ[64:128, :], COS3[64:128, :], MUL, *waits_of("q"), t_swap)

        def query_turned():
            st["mq"] = tt(MQ[64:96, :], MQ[64:96, :], MQ[96:128, :], ADD, st["qp"])

        def key_parts(j):
            a = copy_(QKS[j][2][0:64, :], MKV[0:64, :], st["kv",], *S_set[j].waits())
            st["kl"] = tt(QKS[j][3][0:64, :], MKV[0:64, :], QKS[j][2][0:64, :], SUB, a)
            S_mkv.free = st["kl"]

        def query_parts(j):
            a = copy_(QKS[j][0][0:MQK, :], MQ[0:MQK, :], st["mq"], *S_set[j].waits())
            ready[j].free = S_mq.free = tt(QKS[j][1][0:MQK, :], MQ[0:MQK, :], QKS[j][0][0:MQK, :], SUB, a, st["kl"])

        def mla_values(j):
            for kt in range(8):
                t = tr(PS[C][:, kt // 4, (kt % 4) * P:(kt % 4) * P + P], MKV[:, kt * P:kt * P + P], SQC[:, 0, :],
                       st["kv",], *S_tc[0].waits(), *S_tc[1].waits(), mark=kt == 7)
            v = PS[C][:, :, :].rearrange("p a (k c) -> p (a k) c", c=P)[:, :, 64:128]
            a = copy_(VS2[j][:, :, 0:64], v, t, *S_v2[j].waits())
            S_tc[0].free = S_tc[1].free = tt(VS2[j][:, :, 64:128], v, VS2[j][:, :, 0:64], SUB, a)

        def scores(j, u):
            QH, QL, KH, KL = QKS[j]
            p = ps[u % 2]
            q0 = u * P
            n = q0 + P
            for h in range((n + HALF - 1) // HALF):
                c = slice(h * HALF, min(n, h * HALF + HALF))
                o = PS[u % 2][:, h, 0:c.stop - c.start]
                diag = c.start <= q0 < c.stop
                mm(o, QH[0:MQK, q0:q0 + P], KH[0:MQK, c], True, False, *ready[j].waits(), *p.waits(), mark=False)
                mm(o, QH[0:MQK, q0:q0 + P], KL[0:MQK, c], False, False, mark=False)
                t = mm(o, QL[0:MQK, q0:q0 + P], KH[0:MQK, c], False, not diag, mark=not diag)
                if diag:
                    t = mm(PS[u % 2][:, h, q0 - c.start:q0 - c.start + P], CMB[:, 1, :], CMB[:, 0, :], False, True,
                           t_cmb)
            st["s", j, u] = t

        def maxima(j, u):
            v, n = u % 4, u * P + P
            m = dve(lambda e, k: e.tensor_reduce(MXM[:, v:v + 1], both(u % 2)[:, 0:n], AX.X, MAX),
                    *waits_of("s", j, u))
            st["nb", u] = ts(NB[:, v:v + 1], MXM[:, v:v + 1], -scale2, MUL, m)

        def exps(j, u):
            v, n = u % 4, u * P + P
            st["e", j, u] = ps[u % 2].free = fun(ACT.Exp, LPB[u][:, 0:n], both(u % 2)[:, 0:n], st["nb", u],
                                              *S_lpb[u].waits(), scale=scale2, bias=NB[:, v:v + 1],
                                              acc=RSA[:, v:v + 1])

        def norms(j, u):
            v, n = u % 4, u * P + P
            x = recip(RI[:, v:v + 1], RSA[:, v:v + 1], *waits_of("e", j, u))
            st["p", j, u] = tt(LPB[u][:, 0:n], LPB[u][:, 0:n], RI[:, v:v + 1].to_broadcast([P, n]), MUL, x,
                               q="pool")

        def turns(j, u):
            for kt in range(u + 1):
                h = kt // 4
                last = kt == u or kt % 4 == 3
                t = tr(PS[C][:, h, (kt % 4) * P:(kt % 4) * P + P], LPB[u][:, kt * P:kt * P + P], SQC[:, 0, :],
                       *(waits_of("p", j, u) + S_tc[h].waits() if kt % 4 == 0 else []), mark=last)
                st["t", u, h] = t
            S_lpb[u].free = t

        def parts(j, u):
            v = u % 4
            w = S_ptl.waits() if v == 0 else []
            for h in range((u + 4) // 4):
                k0, k1 = 4 * h, min(4 * h + 4, u + 1)
                src = PS[C][:, h, 0:(k1 - k0) * P].rearrange("p (k q) -> p k q", q=P)
                a = copy_(LTH[:, k0:k1, v * P:v * P + P], src, st["t", u, h], *w)
                S_tc[h].free = tt(LTL[:, k0:k1, v * P:v * P + P], src, LTH[:, k0:k1, v * P:v * P + P], SUB, a, *w)
                st["l", u] = S_tc[h].free

        def values(j, u):
            g = u // 4
            nk = 4 * g + 4
            for kt in range(nk):
                c0 = max(0, kt - 4 * g) * P
                for hl, Pt in enumerate((LTH, LTL)):
                    last = kt == nk - 1 and hl == 1
                    t = mm(PS[Dp][:, 1, c0:HALF], VS2[j][:, kt, :], Pt[:, kt, c0:HALF], kt == 0 and hl == 0, last,
                           st["l", u], *ready[j].waits(), *S_av.waits(), mark=last)
            S_ptl.free = st["o", u] = t
            if g == 1:
                S_v2[j].free = S_set[j].free = t

        def outputs(j, u, tile):
            g = u // 4
            mine, rest = slice(64 * j, 64 * j + 64), slice(64 - 64 * j, 128 - 64 * j)
            a = copy_(MOT[mine, :], PS[Dp][rest, 1, :], st["o", u], *S_mot.waits())
            dst = lambda k: MX[mine, k + tile, g * HALF:g * HALF + HALF]
            S_av.free = S_mot.free = tt(dst, MOT[mine, :], PS[Dp][mine, 1, :], ADD, a, t_gn)

        def step(j, u, tile, nxt=None, after=None, last=False):
            front = u < 8 or not last
            jf, f = (j, u) if u < 8 else (1 - j, u - 8)
            b = u - LAG
            if b >= 0:
                turns(j, b)
            if u + 1 < (8 if last else 12):
                scores(jf if u + 1 != 8 else 1 - j, (u + 1) % 8)
            if u >= 8 and after is not None:
                mla_project(*after, u - 8)
            if u == 3 and nxt is not None:
                mla_project(*nxt, 3)
            if front:
                maxima(jf, f)
            if 0 <= u - 1 < (8 if last else 11):
                norms(*((j, u - 1) if u - 1 < 8 else (1 - j, u - 9)))
            if b >= 0:
                parts(j, b)
            if front:
                exps(jf, f)
            if u >= 8 and after is not None or u == 3 and nxt is not None:
                mla_projected()
            if b >= 0 and b % 4 == 3:
                values(j, b)
                outputs(j, b, tile)
            if nxt is None:
                return
            if u == 3:
                query_products()
            if u == 4:
                query_turned()
                key_parts(1 - j)
            if u == 5:
                query_parts(1 - j)
                mla_values(1 - j)

        split_to(S_MLA + 2)
        for n in range(4):
            mla_project(0, 0, n)
            mla_projected()
        query_products()
        query_turned()
        key_parts(0)
        query_parts(0)
        mla_values(0)
        scores(0, 0)
        for u in range(LAG):
            step(0, u, 4)
            mla_project(1, 0, u)
            mla_projected()
        hand = carried(("p", 0, 0), ("p", 0, 1), ("e", 0, 2), ("s", 0, 3), ("q",))

        def mla_pair():
            slab_split(S_MLA + 2, 2)
            for u in range(LAG, 8 + LAG):
                step(0, u, 4, nxt=(1, 2), after=(2, 2))
            slab_split(S_MLA + 3, 2)
            for u in range(LAG, 8 + LAG):
                step(1, u, 4, nxt=(2, 2), after=(3, 2))
            for key, slot in hand:
                slot.free = st[key]

        loop(3, ml_slots + [x for _, x in hand], mla_pair)
        for u in range(LAG, 8 + LAG):
            step(0, u, 7, nxt=(7, 0))
        for u in range(LAG, 8 + LAG):
            step(1, u, 7, last=True)
        done_split[0] = S_OUT2
        t_mla = S_av.free
        ps[C].free, ps[Dp].free = S_tc[1].free, S_av.free

        w_h = [load("act", H[:, m, :], hs[m], t_mla, *w_spill) for m in range(KT)]
        xw = split_all(MX, t_mla)
        S_n = [Slot(t_mla), Slot(t_mla)]
        split_to(S_FFN + 2)

        def out2(step, tile):
            for j in range(2):
                p = (A, B)[j]
                t = project(S_OUT2 + tile + j, step, full, mh, ml, halves(p), *ps[p].waits(), xw=xw)
                m = tile + j
                a = fun(ACT.Square, N2[j][:, :] if m else ACC3[:, :], both(p), t, *S_n[j].waits())
                ps[p].free = vcopy(lambda k, m=m: O2[:, k * 2 + m, :], both(p), a)
                if m:
                    S_n[j].free = st["acc"] = tt(ACC3[:, :], ACC3[:, :], N2[j][:, :], ADD, a)

        out2(0, 0)
        loop(3, ps + S_n, lambda: out2(2, 2))
        t = token_sums(C, ACC3, SQC[:, 1, 0:1], 1, st["acc"], *ps[C].waits())
        ps[C].free = x = token_rstd(C, D, 1, t)
        t = spread(C, TOK[:, 0:8], 1, RS2[:, :], x)
        sq4, a4, free4 = (N2[0], N2[1], ACC3, RS2), {}, [S_n[0].free, S_n[1].free, t, t]

        def pair_sums(m):
            b = m % 4
            y = tt(sq4[b][:, :], sq4[b][:, :], sq4[b + 1][:, :], ADD, a4[m + 1])
            free4[b] = free4[b + 1] = token_sums(Dp, sq4[b], SQC[:, 1, 0:1], 1, y, *ps[Dp].waits(), first=m == 0,
                                                 last=m == KT - 2)
            return free4[b]

        for m in range(KT):
            v = stt(O2[:, m, :], O2[:, m, :], col("post_mix", m), both(C), MUL, MUL, t)
            ps[C].free = v
            v = tt(H[:, m, :], H[:, m, :], O2[:, m, :], ADD, v, w_h[m], q="pool" if m % 3 == 0 else "dve")
            a4[m] = fun(ACT.Square, sq4[m % 4][:, :], H[:, m, :], v, free4[m % 4])
            if m % 2 == 0 and m:
                pair_sums(m - 2)
        t = pair_sums(KT - 2)
        ps[Dp].free = x = token_rstd(Dp, D, 1, t)
        S_n = [Slot(t), Slot(t)]
        t = spread(Dp, TOK[:, 0:8], 1, ACC3[:, :], x)
        xw = split_tiles(KT, lambda m, o, f: stt(o, H[:, m, :], col("pre_ffn", m), both(Dp), MUL, MUL, t, f),
                         lambda m: MH[:, m, :], lambda m: ML[:, m, :], [N2[0][:, :], N2[1][:, :]], S_n)
        ps[Dp].free = xw[1][KT - 1]

        z3 = dve(lambda e, k: e.memset(FA[:, :, :].rearrange("p a b -> p (a b)"), 0.0), xw[1][KT - 1])
        S_th, S_hf, S_hb = [Slot(z3), Slot(z3)], [Slot(z3), Slot(z3)], [Slot(z3), Slot(z3)]
        hb_ready = [Slot(), Slot()]
        ffn_slots = ps + S_th + S_hf + S_hb + hb_ready
        st.clear()

        def gate_up(s, step, b):
            for m in range(2):
                pg, pu = (A, C)[m], (B, Dp)[m]
                t = project(s + 2 * m, step, full, mh, ml, halves(pg), *ps[pg].waits(), xw=xw)
                a = fun(ACT.Tanh, TH[m][:, :], both(pg), t, *S_th[m].waits(), scale=0.5)
                x = stt(TH[m][:, :], TH[m][:, :], 1.0, both(pg), ADD, MUL, a)
                ps[pg].free = x
                t = project(s + 2 * m + 1, step, full, mh, ml, halves(pu), *ps[pu].waits())
                x = stt(HF[m][:, :], TH[m][:, :], 0.5, both(pu), MUL, MUL, t, x, *S_hf[m].waits())
                ps[pu].free = S_th[m].free = x
                a = copy_(HBH[b][:, m, :], HF[m][:, :], x, *(S_hb[b].waits() if m == 0 else []))
                S_hf[m].free = tt(HBL[b][:, m, :], HF[m][:, :], HBH[b][:, m, :], SUB, a,
                                  *(S_hb[b].waits() if m == 0 else []))
            hb_ready[b].free = S_hf[1].free

        def down(s, step, b, pairs=(A, B, C, Dp), after=lambda m, x: None):
            for m in range(8):
                p = pairs[m % len(pairs)]
                hx = lambda kt, c, n: HBH[b][:, kt, c:c + n]
                lx = lambda kt, c, n: HBL[b][:, kt, c:c + n]
                ws = hb_ready[b].waits() if m == 0 else []
                t = project(s + m // 4, step, [(2 * (m % 4), 0), (2 * (m % 4) + 1, 1)], hx, lx, halves(p),
                            *ps[p].waits(), *ws, last=m % 4 == 3)
                x = tt(FA[:, m, :], FA[:, m, :], both(p), ADD, t)
                ps[p].free = x
                after(m, x)
            S_hb[b].free = t
            st["fa"] = x

        split_to(S_PLEP)
        gate_up(S_FFN, 0, 0)

        def ffn_pair():
            gate_up(S_FFN + 4, 12, 1)
            down(S_FFN + 8, 12, 0)
            gate_up(S_FFN + 10, 12, 0)
            down(S_FFN + 14, 12, 1)

        loop(5, ffn_slots, ffn_pair)
        t_ffn_loop = pr.last("used")
        w_p = load("act", PR[:, :, :], pT.rearrange("a p t -> p a t"), t_ffn_loop)
        pw = ([None] * 2, [None] * 2)
        split_to(S_PLEG)
        S_n = [Slot(S_th[0].free), Slot(S_th[1].free)]

        def add_square(acc, m, src, w, q):
            b = m % 2
            if m == 0:
                return fun(ACT.Square, acc[:, :], src, w), None
            a = fun(ACT.Square, TH[b][:, :], src, w, S_n[b].free)
            S_n[b].free = y = tt(acc[:, :], acc[:, :], TH[b][:, :], ADD, a, st[q], q=q)
            return a, y

        def ffn_square(m, x):
            a, y = add_square(HF[0], m, FA[:, m, :], x, "dve")
            st["dve"] = y or a
            if m in (3, 4):
                j = m - 3
                pw[0][j] = copy_(PH[:, j, :], PR[:, j, :], w_p)
                pw[1][j] = tt(PL[:, j, :], PR[:, j, :], PH[:, j, :], SUB, pw[0][j])

        down(S_PLEP - 2, 0, 0, pairs=(A, B), after=ffn_square)
        t_ffn = st["fa"]

        hw = ([None] * KT, [None] * KT)

        def ffn_normed(m):
            if m < KT:
                v = stt(FA[:, m, :], FA[:, m, :], col("post_ffn", m), both(C), MUL, MUL, t_rf)
                v = tt(H[:, m, :], H[:, m, :], FA[:, m, :], ADD, v)
                hw[0][m] = copy_(GH[:, m, :], H[:, m, :], v, t_ffn)
            if m >= 1:
                hw[1][m - 1] = tt(GL[:, m - 1, :], H[:, m - 1, :], GH[:, m - 1, :], SUB, hw[0][m - 1])

        for m in range(8):
            p = m % 2
            t = project(S_PLEP + m // 4, 0, [(2 * (m % 4), 0), (2 * (m % 4) + 1, 1)],
                        lambda kt, c, n: PH[:, kt, c:c + n], lambda kt, c, n: PL[:, kt, c:c + n], halves(p),
                        *ps[p].waits(), xw=pw, last=m % 4 == 3)
            if m == 0:
                t_f = token_sums(C, HF[0], SQC[:, 1, 0:1], 1, st["dve"], *ps[C].waits())
                ps[C].free = x = token_rstd(C, D, 1, t_f)
            if m == 1:
                t_rf = spread(C, TOK[:, 0:8], 1, HF[0][:, :], x)
            a = copy_(EB[:, m, :], both(p), t)
            ps[p].free, y = add_square(HF[1], m, both(p), a, "pool")
            st["pool"] = y or ps[p].free
            if m >= 2:
                ffn_normed(m - 2)
        for m in range(KT - 2, KT + 1):
            ffn_normed(m)
        split_to(NSLAB)
        t_e = token_sums(Dp, HF[1], SQC[:, 1, 0:1], 1, st["pool"], *ps[Dp].waits())
        ps[C].free = hw[1][KT - 1]
        ps[Dp].free = x = token_rstd(Dp, D, 1, t_e, off=1)
        t = spread(Dp, TOK[:, 18:26], 1, HF[1][:, :], x)
        hb = ts(TINY[:, 40:48], COLS[:, COL["b_ple"]:COL["b_ple"] + 8], 0.5, MUL)
        e_done = [stt(EB[:, m, :], EB[:, m, :], col("ple_norm", m), both(Dp), MUL, MUL, t) for m in range(KT)]
        ps[Dp].free = e_done[KT - 1]
        for m in range(KT):
            p = (A, B, C)[m % 3]
            t = project(S_PLEG + m, 0, full, lambda kt, c, n: GH[:, kt, c:c + n], lambda kt, c, n: GL[:, kt, c:c + n],
                        halves(p), *ps[p].waits(), xw=hw)
            a = fun(ACT.Tanh, OB[:, m, :], both(p), t, e_done[KT - 1], hb, scale=0.5, bias=TINY[:, 40 + m:41 + m])
            ps[p].free = a
            x = stt(OB[:, m, :], OB[:, m, :], 1.0, EB[:, m, :], ADD, MUL, a, e_done[m], hb)
            x = stt(OB[:, m, :], OB[:, m, :], 0.5, H[:, m, :], MUL, ADD, x)
            do("act", lambda e, k, m=m: e.dma_start(outT[m], OB[:, m, :]), x, inc=[(s_out, 16)], mark=False)
        block = ctx.enter_context(nc.Block())

        @block.sync
        def _(e):
            pr.emit("sp", e)
            e.wait_ge(s_out, 16 * KT)

        @block.scalar
        def _(e):
            pr.emit("act", e)

        @block.gpsimd
        def _(e):
            pr.emit("pool", e)

        @block.tensor
        def _(e):
            pr.emit("pe", e)

        @block.vector
        def _(e):
            pr.emit("dve", e)


def shape_constants():
    sq = np.zeros((13, P, P), np.float64)
    sq[0] = np.eye(P)
    sq[1] = 1.0
    sq[2, :64, :64] = sq[2, 64:, 64:] = 1.0
    sq[3] = 1.0 / P
    j = np.arange(P)
    sq[4] = np.where(j[None, :] > j[:, None], -1e30, 0.0)
    zeta, gch = np.zeros((P, RH)), np.zeros((P, RH))
    for h in range(RH):
        lg = np.log(1.0 - 2.0 ** (-5.0 - h))
        sq[5 + h] = np.exp((j + 1) * lg)[None, :]
        diff = j[None, :] - j[:, None]
        sq[9 + h] = np.where(diff >= 0, np.exp(np.maximum(diff, 0) * lg), 0.0)
        zeta[:, h] = np.exp((CH - 1 - j) * lg)
        gch[:, h] = np.exp(CH * lg)
    n_f = HD // 4
    fr = 1.0 / (10000.0 ** (np.arange(n_f) * 2.0 / (HD // 2)))
    tok = np.arange(T)
    row, cl = tok // 64 - (T // 64) // 2, tok % 64 - 32
    ang = np.concatenate([row[:, None] * fr, cl[:, None] * fr], axis=1)
    ang = np.concatenate([ang, np.zeros((META, HD // 2))], axis=0).T
    rope1 = np.stack([np.tile(np.cos(ang), (4, 1)),
                      np.concatenate([np.sin(ang), -np.sin(ang)] * 2, axis=0)])
    m, l = np.arange(MT5 * P)[:, None], np.arange(1, NL + 1)[None, :]
    dft = np.stack([np.cos(2 * np.pi * ((m * l) % L) / L), np.sin(2 * np.pi * ((m * l) % L) / L)]) / np.sqrt(L * 64.0)
    dft[:, NM:] = 0.0
    dft[:, NL] *= 0.5
    c = np.arange(64)
    cd = np.stack([np.cos(2 * np.pi * c[:, None] * c[None, :] / 64), np.sin(2 * np.pi * c[:, None] * c[None, :] / 64)])
    cd = np.concatenate([cd, cd], axis=2)
    inv_ret = np.tile(1.0 / 10000.0 ** (np.arange(64) / 64.0), 2)
    inv_mla = np.tile(1.0 / 10000.0 ** (np.arange(16) / 16.0), 8)
    half = np.repeat([1.0, -1.0], 64)
    sgn_mla = np.ones(P)
    sgn_mla[96:112] = -1.0
    vec = {"zeta": zeta, "gch": gch, "inv_ret": inv_ret[:, None], "inv_mla": inv_mla[:, None],
           "sgn_ret": half[:, None], "sgn_mla": sgn_mla[:, None], "eps": np.full((P, 1), EPS),
           "halfpi": np.full((P, 1), np.pi / 2)}
    f = np.float32
    return sq.astype(f), rope1.astype(f), dft.astype(f), cd.astype(f), {k: v.astype(f) for k, v in vec.items()}


def slab_layout(w_in, w_out, w_in2, w_uq, w_ukv, w_o, w_gate, w_up, w_down, w_pp, w_pg):
    def tile(w, m):
        k = w.shape[0] // P
        return w[:, m * P:m * P + P].reshape(k, P, P).transpose(1, 0, 2).reshape(P, k * P)

    def pairs(w, k0, m0):
        x = w[k0 * P:k0 * P + 2 * P, m0 * P:m0 * P + 4 * P].reshape(2, P, 4, P)
        return x.transpose(1, 2, 0, 3).reshape(P, 8 * P)

    halves_ = np.concatenate([np.arange(0, HD, 2), np.arange(1, HD, 2)])
    q0 = 2 * FW
    k0 = q0 + 512
    v0 = k0 + 128
    heads = [k + 4 * s for k in range(4) for s in range(2)]
    head_rows = np.concatenate([np.arange(h * HD, h * HD + HD) for h in heads])
    perm_q = np.concatenate([q0 + h * HD + halves_ for h in heads])
    perm_k = np.concatenate([k0 + h * HD + halves_ for h in range(2)])
    order = np.concatenate([np.arange(FW), perm_k, np.arange(v0, v0 + 128), perm_q, np.arange(FW, 2 * FW),
                            v0 + 128 + head_rows])
    w_out = w_out[np.concatenate([np.arange(FW), FW + head_rows])]
    w1 = w_in[:, order]
    out = [tile(w1, m) for m in range(18)] + [tile(w_out, m) for m in range(8)]
    for h in range(RH):
        out += [tile(w_in2, 4 * x + h) for x in (1, 2, 0, 3)]
    out += [tile(w_in2, 16 + n) for n in range(5)]
    kr = w_in2[:, 2048 + 640:]
    sw = np.concatenate([np.arange(16, 32), np.arange(16)])
    out.append(tile(np.concatenate([np.zeros((D, 64), kr.dtype), kr, kr[:, sw]], axis=1), 0))
    for h in range(MH_):
        q = w_uq[:, h * MQK:h * MQK + MQK]
        q = np.concatenate([q, q[:, 64 + sw]], axis=1)
        kv = w_ukv[:, h * 128:h * 128 + 128]
        x = np.concatenate([tile(q, 0), tile(kv, 0)], axis=1)
        out.append(np.concatenate([x, np.zeros((P, 1024 - x.shape[1]), x.dtype)], axis=1))
    out += [tile(w_o, m) for m in range(8)]

    def gu(c):
        return [tile(w, 2 * c + m) for m in range(2) for w in (w_gate, w_up)]

    def dn(c):
        return [pairs(w_down, 2 * c, 0), pairs(w_down, 2 * c, 4)]

    n = DFF // 256
    out += gu(0)
    for c in range(1, n):
        out += gu(c) + dn(c - 1)
    out += dn(n - 1)
    out += [pairs(w_pp, 0, 0), pairs(w_pp, 0, 4)] + [tile(w_pg, m) for m in range(8)]
    return np.ascontiguousarray(np.stack(out))


def kernel(**inputs):
    import concourse.bacc as bacc
    from concourse.bass_utils import run_bass_kernel_spmd as run

    a = {k: np.asarray(v) for k, v in inputs.items()}
    sq, rope1, dft, cd, vec = shape_constants()
    xm = np.concatenate([a["x"][0], a["meta_tokens"]], axis=0)
    xT = np.ascontiguousarray(xm.T.reshape(KT, P, L))
    pT = np.ascontiguousarray(a["p_2"][0, 0].T.reshape(2, P, T))
    slabs = slab_layout(a["w_in"][0], a["w_out"][0], a["w_in_2"][0], a["w_uq_2"][0], a["w_ukv_2"][0], a["w_o_2"][0],
                        a["w_gate_2"][0], a["w_up_2"][0], a["w_down_2"][0], a["w_ple_proj_2"][0],
                        a["w_ple_gate_2"][0])
    assert slabs.shape == (NSLAB, P, 1024)
    halves_ = np.concatenate([np.arange(0, HD, 2), np.arange(1, HD, 2)])
    put = {"norm_g": a["norm_g"], "final_g": a["final_g"], "pre_mix": a["pre_mix_norm_2"],
           "post_mix": a["post_mix_norm_2"], "pre_ffn": a["pre_ffn_norm_2"], "post_ffn": a["post_ffn_norm_2"],
           "ple_norm": a["ple_norm_2"], "b_ple": a["b_ple_gate_2"], "mla_q": a["mla_q_norm_2"],
           "mla_kv": a["mla_kv_norm_2"], "ret_gn": a["ret_gn_w_2"], "b_fmix": a["b_fmix"],
           "q_g": np.tile(a["q_norm_g"][0][halves_], 2), "k_g": np.tile(a["k_norm_g"][0][halves_], 2)}
    cols = np.zeros((P, NCOL), np.float32)
    for n, k in _names:
        cols[:, COL[n]:COL[n] + k] = vec[n] if n in vec else put[n].reshape(k, P).T
    wf = np.ascontiguousarray(a["w_fmix"][0].transpose(1, 0, 2).reshape(64, 512))
    arrays = {"xT": xT, "pT": pT, "pos": np.ascontiguousarray(a["positions_2"]), "slabs": slabs, "cols": cols,
              "squares": sq, "rope1": rope1, "dft": dft, "wf": wf, "cd": cd}
    nc = bacc.Bacc("TRN2", target_bir_lowering=False, num_devices=1)
    args = [nc.dram_tensor(n, v.shape, mybir.dt.from_np(v.dtype), kind="ExternalInput").ap() for n, v in arrays.items()]
    args.append(nc.dram_tensor("outT", (KT, P, T), F32, kind="ExternalOutput").ap())
    two_block_kernel(nc, *args)
    r = run(nc, [arrays], core_ids=[0])
    o = r.results[0]["outT"].reshape(D, T)
    return np.ascontiguousarray(o.T)[None]
```
